# Optimizing a Trainium2 kernel written in Bass

```python
import jax, jax.numpy as jnp
from jax import lax
import numpy as np

D_MODEL = 1024
BATCH = 1
SEQ = 512
DEPTH = 1

N_META = 16
BLOCK = 128
N_PAD = BLOCK - N_META
HG_HEADS = 4
HG_DK = 128
HG_DV = 128
HG_WIDTH = HG_HEADS * HG_DK
AT_QHEADS = 8
AT_KVHEADS = 2
AT_GROUP = AT_QHEADS // AT_KVHEADS
AT_HDIM = 64
AT_WIDTH = AT_QHEADS * AT_HDIM
AT_KV_WIDTH = AT_KVHEADS * AT_HDIM
WINDOW = 128
IN_COLS = 4 * HG_WIDTH + AT_WIDTH + 2 * AT_KV_WIDTH + 2 * D_MODEL
PK_HEADS = 8
N_KEYS = 128
N_EXPERTS = N_KEYS * N_KEYS
D_QUERY = 256
D_HALF = D_QUERY // 2
TOPK = 16
TOK_BLOCK = 256
EPS = 1e-6

kernel_name = "hybrid_hgrn2_swa_sink_peer_block"

def _rmsnorm(x, g):
    xf = x.astype(jnp.float32)
    y = xf * lax.rsqrt(jnp.mean(xf * xf, axis=-1, keepdims=True) + EPS)
    return (y * g.astype(jnp.float32)).astype(x.dtype)

def _hgrn2(q, f_logit, v, lb):
    B, L = q.shape[:2]
    lb = lb.reshape(HG_HEADS, HG_DK).astype(jnp.float32)
    f = lb + (1.0 - lb) * jax.nn.sigmoid(f_logit.astype(jnp.float32))
    logf = jnp.log(f)
    k = 1.0 - f
    pad = ((0, 0), (N_PAD, 0), (0, 0), (0, 0))
    qf = jnp.pad(q.astype(jnp.float32), pad)
    logf = jnp.pad(logf, pad)
    k = jnp.pad(k, pad)
    vf = jnp.pad(v.astype(jnp.float32), pad)
    nc = (L + N_PAD) // BLOCK

    def to_chunks(t):
        return t.reshape(B, nc, BLOCK, HG_HEADS, t.shape[-1]).transpose(1, 0, 3, 2, 4)

    causal = jnp.tril(jnp.ones((BLOCK, BLOCK), dtype=bool))[:, :, None]

    def step(S, inp):
        qc, lc, kc, vc = inp
        A = jnp.cumsum(lc, axis=2)
        diff = A[:, :, :, None, :] - A[:, :, None, :, :]
        decay = jnp.where(causal, jnp.exp(jnp.where(causal, diff, 0.0)), 0.0)
        scores = jnp.einsum('bhtsd,bhsd->bhts', qc[:, :, :, None, :] * decay, kc)
        o = (jnp.einsum('bhts,bhse->bhte', scores, vc)
             + jnp.einsum('bhtd,bhde->bhte', qc * jnp.exp(A), S))
        A_end = A[:, :, -1:, :]
        S = (jnp.exp(A_end[:, :, 0, :])[..., None] * S
             + jnp.einsum('bhsd,bhse->bhde', kc * jnp.exp(A_end - A), vc))
        return S, o

    S0 = jnp.zeros((B, HG_HEADS, HG_DK, HG_DV), jnp.float32)
    _, o = lax.scan(step, S0, (to_chunks(qf), to_chunks(logf), to_chunks(k), to_chunks(vf)))
    o = o.transpose(1, 0, 3, 2, 4).reshape(B, nc * BLOCK, HG_HEADS, HG_DV)
    return o[:, N_PAD:]

def _swa_sinks(q, k, v, sinks):
    B, L = q.shape[:2]
    P = L + N_PAD
    nb = P // BLOCK
    pad = ((0, 0), (N_PAD, 0), (0, 0), (0, 0))
    qb = jnp.pad(q, pad).reshape(B, nb, BLOCK, AT_KVHEADS, AT_GROUP, AT_HDIM)
    kp = jnp.pad(k, pad).reshape(B, nb, BLOCK, AT_KVHEADS, AT_HDIM)
    vp = jnp.pad(v, pad).reshape(B, nb, BLOCK, AT_KVHEADS, AT_HDIM)

    def band(t):
        prev = jnp.pad(t, ((0, 0), (1, 0), (0, 0), (0, 0), (0, 0)))[:, :-1]
        return jnp.concatenate([prev, t], axis=2)

    kb, vb = band(kp), band(vp)
    km, vm = k[:, :N_META], v[:, :N_META]
    scale = AT_HDIM ** -0.5
    s_band = jnp.einsum('bnqhgd,bnshd->bnhgqs', qb, kb).astype(jnp.float32) * scale
    s_meta = jnp.einsum('bnqhgd,bmhd->bnhgqm', qb, km).astype(jnp.float32) * scale
    qpos = jnp.arange(nb * BLOCK).reshape(nb, BLOCK) - N_PAD
    kpos = qpos[:, :1] - BLOCK + jnp.arange(2 * BLOCK)[None, :]
    band_mask = ((kpos[:, None, :] >= N_META)
                 & (kpos[:, None, :] <= qpos[:, :, None])
                 & (qpos[:, :, None] - kpos[:, None, :] < WINDOW))
    meta_mask = jnp.arange(N_META)[None, None, :] <= qpos[:, :, None]
    neg = jnp.finfo(jnp.float32).min
    s_band = jnp.where(band_mask[None, :, None, None], s_band, neg)
    s_meta = jnp.where(meta_mask[None, :, None, None], s_meta, neg)
    s_sink = jnp.broadcast_to(
        sinks.reshape(AT_KVHEADS, AT_GROUP).astype(jnp.float32)[None, None, :, :, None, None],
        s_band.shape[:-1] + (1,))
    p = jax.nn.softmax(jnp.concatenate([s_band, s_meta, s_sink], axis=-1), axis=-1)
    p_band = p[..., :2 * BLOCK].astype(v.dtype)
    p_meta = p[..., 2 * BLOCK:2 * BLOCK + N_META].astype(v.dtype)
    o = (jnp.einsum('bnhgqs,bnshd->bnqhgd', p_band, vb)
         + jnp.einsum('bnhgqm,bmhd->bnqhgd', p_meta, vm))
    return o.reshape(B, P, AT_WIDTH)[:, N_PAD:]

def _peer(h, w_q, subkeys, u, v):
    B, L, D = h.shape
    T = B * L
    Tp = -(-T // TOK_BLOCK) * TOK_BLOCK
    t = jnp.pad(h.reshape(T, D), ((0, Tp - T), (0, 0))).reshape(Tp // TOK_BLOCK, TOK_BLOCK, D)

    def block(xb):
        q = (xb @ w_q).reshape(TOK_BLOCK, PK_HEADS, 2, D_HALF)
        s = jnp.einsum('thcd,hcnd->thcn', q, subkeys).astype(jnp.float32)
        sv, si = lax.top_k(s, TOPK)
        cand = sv[:, :, 0, :, None] + sv[:, :, 1, None, :]
        cand_idx = si[:, :, 0, :, None] * N_KEYS + si[:, :, 1, None, :]
        top_s, pos = lax.top_k(cand.reshape(TOK_BLOCK, PK_HEADS, TOPK * TOPK), TOPK)
        idx = jnp.take_along_axis(cand_idx.reshape(TOK_BLOCK, PK_HEADS, TOPK * TOPK), pos, axis=-1)
        g = jax.nn.softmax(top_s, axis=-1)
        a = jax.nn.gelu(jnp.einsum('td,thkd->thk', xb, u[idx]).astype(jnp.float32), approximate=False)
        w = (g * a).astype(xb.dtype)
        return jnp.einsum('thk,thkd->td', w, v[idx])

    out = lax.map(block, t)
    return out.reshape(Tp, D)[:T].reshape(B, L, D)

def setup_inputs(seed: int = 0) -> dict:
    key = jax.random.key(seed)
    ks = jax.random.split(key, 17)
    f32 = jnp.float32
    nrm = lambda k, shape, s: jax.random.normal(k, shape, f32) * s
    return {
        "x": nrm(ks[0], (BATCH, SEQ, D_MODEL), 1.0),
        "meta_tokens": nrm(ks[1], (N_META, D_MODEL), 1.0),
        "mix_norm_g": 1.0 + nrm(ks[2], (DEPTH, D_MODEL), 0.02),
        "w_in": nrm(ks[3], (DEPTH, D_MODEL, IN_COLS), D_MODEL ** -0.5),
        "b_gate": nrm(ks[4], (DEPTH, 2 * D_MODEL), 0.02),
        "hg_lb_logits": nrm(ks[5], (DEPTH + 1, HG_WIDTH), 0.1),
        "hg_norm_g": 1.0 + nrm(ks[6], (DEPTH, HG_HEADS * HG_DV), 0.02),
        "attn_sinks": nrm(ks[7], (DEPTH, AT_QHEADS), 0.5),
        "w_branch_hg": nrm(ks[8], (DEPTH, HG_HEADS * HG_DV, D_MODEL), (HG_HEADS * HG_DV) ** -0.5),
        "w_branch_attn": nrm(ks[9], (DEPTH, AT_WIDTH, D_MODEL), AT_WIDTH ** -0.5),
        "w_out": nrm(ks[10], (DEPTH, D_MODEL, D_MODEL), D_MODEL ** -0.5),
        "ffn_norm_g": 1.0 + nrm(ks[11], (DEPTH, D_MODEL), 0.02),
        "peer_w_q": nrm(ks[12], (DEPTH, D_MODEL, PK_HEADS * D_QUERY), D_MODEL ** -0.5),
        "peer_subkeys": nrm(ks[13], (DEPTH, PK_HEADS, 2, N_KEYS, D_HALF), D_HALF ** -0.5),
        "peer_u": nrm(ks[14], (DEPTH, N_EXPERTS, D_MODEL), D_MODEL ** -0.5),
        "peer_v": nrm(ks[15], (DEPTH, N_EXPERTS, D_MODEL), 0.5),
        "final_norm_g": 1.0 + nrm(ks[16], (D_MODEL,), 0.02),
    }

def reference(x, meta_tokens, mix_norm_g, w_in, b_gate, hg_lb_logits, hg_norm_g, attn_sinks,
              w_branch_hg, w_branch_attn, w_out, ffn_norm_g, peer_w_q, peer_subkeys,
              peer_u, peer_v, final_norm_g):
    B = x.shape[0]
    h = jnp.concatenate(
        [jnp.broadcast_to(meta_tokens[None].astype(x.dtype), (B, N_META, D_MODEL)), x], axis=1)
    L = h.shape[1]
    lbs = jnp.cumsum(jax.nn.softmax(hg_lb_logits.astype(jnp.float32), axis=0), axis=0)
    sizes = (HG_WIDTH, HG_WIDTH, HG_WIDTH, HG_HEADS * HG_DV, AT_WIDTH, AT_KV_WIDTH, AT_KV_WIDTH, D_MODEL, D_MODEL)
    offsets = [int(o) for o in np.cumsum(sizes)[:-1]]
    for l in range(DEPTH):
        y = _rmsnorm(h, mix_norm_g[l])
        z = y @ w_in[l]
        hq, hf, hi, hgate, aq, ak, av, ga, gb = jnp.split(z, offsets, axis=-1)
        o_hg = _hgrn2(hq.reshape(B, L, HG_HEADS, HG_DK), hf.reshape(B, L, HG_HEADS, HG_DK),
                      hi.reshape(B, L, HG_HEADS, HG_DV), lbs[l])
        o_hg = _rmsnorm(o_hg, hg_norm_g[l].reshape(HG_HEADS, HG_DV)).astype(h.dtype)
        o_hg = o_hg.reshape(B, L, HG_HEADS * HG_DV) * jax.nn.silu(hgate)
        o_at = _swa_sinks(aq.reshape(B, L, AT_QHEADS, AT_HDIM), ak.reshape(B, L, AT_KVHEADS, AT_HDIM),
                          av.reshape(B, L, AT_KVHEADS, AT_HDIM), attn_sinks[l])
        gl = (jnp.concatenate([ga, gb], axis=-1) + b_gate[l]).astype(jnp.float32)
        g_hg = jax.nn.sigmoid(gl[..., :D_MODEL]).astype(h.dtype)
        g_at = jax.nn.sigmoid(gl[..., D_MODEL:]).astype(h.dtype)
        m = g_hg * (o_hg @ w_branch_hg[l]) + g_at * (o_at @ w_branch_attn[l])
        h = h + m @ w_out[l]
        h = h + _peer(_rmsnorm(h, ffn_norm_g[l]), peer_w_q[l], peer_subkeys[l], peer_u[l], peer_v[l])
    return _rmsnorm(h, final_norm_g)[:, N_META:]


_drawn_inputs = setup_inputs


def setup_inputs(seed=0):
    import zlib

    import numpy as np

    out = dict(_drawn_inputs(seed))
    spreads = {}
    factors = {'b_gate': 4.14, 'hg_norm_g': 2.715, 'attn_sinks': 61.629, 'final_norm_g': 8.19}
    for name, (base, spread) in spreads.items():
        noise = np.random.default_rng([zlib.crc32(name.encode()), seed]).standard_normal(out[name].shape)
        drawn = base * np.exp(spread * noise) if base else spread * noise
        out[name] = __import__('jax').numpy.asarray(drawn.astype(out[name].dtype))
    for name, factor in factors.items():
        out[name] = (out[name] * factor).astype(out[name].dtype)
    return out
```

```python
from contextlib import ExitStack

import concourse.bass as bass
from concourse import mybir

F32 = mybir.dt.float32
F32R = mybir.dt.float32r
U32 = mybir.dt.uint32
ALU = mybir.AluOpType
ACT = mybir.ActivationFunctionType
AX_X = mybir.AxisListType.X

P = 128
D = 1024
DC = D // P
TOK = 512
TT = TOK // P
META = 16
LEN = META + TOK
EPS = 1e-6
HH = 4
CH = 32
HALF = CH // 2
NCH = TOK // CH
NBLK = LEN // HALF
TINY = 1e-37
AQ = 8
HD = 64
BAND = 2 * P
KEYS = BAND + META
HIDDEN = -1e30
RH = 8
RS = 2 * RH
NK = 128
TOP = 16
PAIRS = [TOP // (a + 1) for a in range(TOP)]
STARTS = [sum(PAIRS[:a]) for a in range(TOP)]
CAND = sum(PAIRS)
LOWEST = -3.0e38

Z_META = 10
Z_REST = 12
N_Z = Z_META + Z_REST
N_GATE = 16
T_GATE = N_Z
T_BRANCH = T_GATE + N_GATE
T_OUT = T_BRANCH + DC
T_KEYS = T_OUT + DC
T_WQ = T_KEYS + 2
N_TILES = T_WQ + RS

GRP = 4
NGRP = NK // GRP
GT = 64
NPIECE = TOK // GT
BATCH = 16
GATES_HG = 6
GATES_AT = 9
assert NCH * GATES_HG + TT * AQ * GATES_AT == N_GATE * 3 * DC
GATES_AT0 = NCH * GATES_HG
V_SPLITS = ((0, 1), (2,), (3,), ())

SPLIT = (("hi", "hi"), ("hi", "lo"), ("lo", "hi"))


def need(eng, semaphore, value):
    if not (isinstance(value, int) and value <= 0):
        eng.wait_ge(semaphore, value)


def gate_blocks_done(first, last):
    return range(first // (3 * DC), last // (3 * DC))


class Chain:

    def __init__(self, eng, sem):
        self.eng, self.sem, self.count = eng, sem, 0

    def done(self, ins):
        ins.then_inc(self.sem, 1)
        self.count += 1
        self.eng.wait_ge(self.sem, self.count)


def build(nc, xT, x, params, sinks, final_g, wstream, uT, v, gates_dram, out):
    ctx = ExitStack()
    with ctx:
        BASE = 16512

        def at(name, shape, dt, offset):
            return nc.alloc_sbuf_tensor_at(name, shape, dt, offset=BASE + offset)

        def sem(name):
            return ctx.enter_context(nc.semaphore(name))

        C, A, B, Z, G0, RING, E, X = 0, 8192, 41984, 58880, 105344, 138112, 162688, 179584
        ident = at("ident", [P, P], F32, C)
        ones = at("ones", [P, P], F32, C + 512)
        iota = at("iota", [P, P], F32, C + 1024)
        bandmask = at("bandmask", [P, KEYS], F32, C + 1536)
        chunkmask = at("chunkmask", [P, CH], F32, C + 2624)
        par = at("par", [P, 44], F32, C + 2752)
        sink = at("sink", [P, AQ], F32, C + 2944)
        eps = at("eps", [P, 1], F32, C + 2976)
        lbw = at("lbw", [P, 6, HH], F32, C + 3008)
        rowstat = at("rowstat", [P, 3, TT], F32, C + 3104)
        atstat = at("atstat", [P, 3, 2], F32, C + 3168)
        ecol = at("ecol", [P, HH, NCH], F32, C + 3200)
        sd = at("sd", [P, LEN], F32, C + 3456)
        rstd = at("rstd", [P, LEN], F32, C + 5568)
        mix_g, ffn_g, hg_g = par[:, 0:8], par[:, 8:16], par[:, 16:20]
        lb_logits = par[:, 20:28].rearrange("p (r h) -> p r h", r=2)
        b_gate = par[:, 28:44]

        y = {k: at("y" + k, [P, DC, LEN], F32R, A + i * DC * LEN * 4) for i, k in enumerate(("hi", "lo"))}
        xt = at("xt", [P, DC, LEN], F32, B)
        xsq = at("xsq", [P, DC, LEN], F32, Z)
        zm = at("zm", [P, Z_META, LEN], F32, Z)
        zr = at("zr", [P, Z_REST, TOK], F32, Z + Z_META * LEN * 4)
        f_z, v_z, ak_z, av_z = zm[:, 0:4], zm[:, 4:8], zm[:, 8], zm[:, 9]
        q_z, og_z, aq_z = zr[:, 0:4], zr[:, 4:8], zr[:, 8:12]
        gates = at("gates", [P, N_GATE, TOK], F32, G0)
        raw = at("raw", [P, 2, D], F32, RING)
        w = {k: at("w" + k, [P, 2, D], F32R, RING + 8192 + i * 8192) for i, k in enumerate(("hi", "lo"))}
        decay = at("decay", [P, HH, LEN], F32, B)
        inv = at("inv", [P, HH, LEN], F32, B + 8448)
        starts = at("starts", [P, HH, LEN], F32, B + 8448)
        kk = at("kk", [P, HH, LEN], F32, E)
        qi = at("qi", [P, HH, TOK], F32, E + 8448)
        knat = at("knat", [P, TT, 512], F32, Z)
        vnat = at("vnat", [P, TT, 512], F32, X + 12288)
        znat = at("znat", [META, Z_META, P], F32, X + 20480)
        vmeta = znat[:, 4:8, :].rearrange("p h d -> p (h d)")
        avmeta = znat[:, 9, :]
        kmeta = at("kmeta", [META, 512], F32, X + 25600)
        avnat = at("avnat", [P, TT, P], F32, X + 27648)
        atsc = at("atsc", [P, 2, KEYS + 8], F32, X)
        atp = at("atp", [P, 2, KEYS + 8], F32, X + 2240)
        atpT = at("atpT", [P, 2, BAND], F32, X + 4480)
        atpTm = at("atpTm", [META, 2, P], F32, X + 6528)
        state = at("state", [P, 4, 512], F32, X)
        within = at("within", [P, 2, HH, P], F32, X + 8192)
        osq = at("osq", [P, HH, TOK], F32, Z)
        o_hg = at("o_hg", [P, HH, TOK], F32, B)
        orstd = at("orstd", [P, HH, TOK], F32, B + 8192)
        ohg = {k: at("ohg" + k, [P, HH, TOK], F32R, Z + i * 8192) for i, k in enumerate(("hi", "lo"))}
        oat = {k: at("oat" + k, [P, 4, TOK], F32R, E + i * 8192) for i, k in enumerate(("hi", "lo"))}
        m = {k: at("m" + k, [P, DC, TOK], F32R, A + i * 16384) for i, k in enumerate(("hi", "lo"))}
        mtmp = at("mtmp", [P, 2, 2, TOK], F32, B)
        acc = at("acc", [P, TT, D], F32, Z + Z_META * LEN * 4 + 8192)
        ynat = at("ynat", [P, TT, D], F32, E)
        ysq = at("ysq", [P, 2, D], F32, A)
        hT = {k: at("hT" + k, [P, DC, TOK], F32R, G0 + i * 16384) for i, k in enumerate(("hi", "lo"))}
        keys = {k: at("keys" + k, [P, RS, NK], F32R, E + 16384 + i * 8192) for i, k in enumerate(("hi", "lo"))}
        q2 = {k: at("q2" + k, [P, 2, TOK], F32R, A + i * 4096) for i, k in enumerate(("hi", "lo"))}
        score = at("score", [P, 2, TT, NK], F32, A + 8192)
        scut = at("scut", [P, 2, TT, NK], F32, A + 12288)
        top_v = at("top_v", [P, TT, RS, TOP], F32, A + 16384)
        top_i = at("top_i", [P, TT, RS, TOP], U32, A + 20480)
        top_f = at("top_f", [P, TT, RS, TOP], F32, A + 24576)
        step_f = at("step_f", [P, TT, RS, TOP], F32, A + 28672)
        cand = at("cand", [P, TT * RH, CAND], F32, A + 32768)
        ccut = at("ccut", [P, TT * RH, CAND], F32, A + 39168)
        best = at("best", [P, TT, RH, TOP], F32, E)
        pos_u = at("pos_u", [P, TT * RH, TOP], U32, E + 2048)
        pos = at("pos", [P, TT, RH, TOP], F32, E + 4096)
        gate = at("gate", [P, TT, RH, TOP], F32, E + 6144)
        tot = at("tot", [P, 2, TT * RH], F32, E + 8192)
        ei = at("ei", [P, TT, RH, TOP], F32, E + 8448)
        ej = at("ej", [P, TT, RH, TOP], F32, E + 10496)
        posb = at("posb", [P, TT, RH, TOP], F32, E + 12544)
        tmp_i = at("tmp_i", [P, TT, RH, TOP], F32, A + 47616)
        tmp_j = at("tmp_j", [P, TT, RH, TOP], F32, A + 45568)
        cols = at("cols", [P, 3, TOK], F32, E + 40960)
        hot_i = at("hot_i", [P, 2, BATCH, NK], F32, E + 0)
        hot_g = at("hot_g", [P, 2, BATCH, NK], F32, E + 16384)
        hot_j = at("hot_j", [P, BATCH, NK], F32, E + 32768)
        piece = at("piece", [P, 2, NK, GT], F32, A)
        vw = {k: at("vw" + k, [P, GRP, D], F32R, A + i * 16384) for i, k in enumerate(("hi", "lo"))}
        act_w = {k: at("aw" + k, [P, 2, GRP, TOK], F32R, A + 32768 + i * 16384) for i, k in enumerate(("hi", "lo"))}
        gelu = at("gelu", [P, 2, TOK], F32, A + 65536)
        prod = at("prod", [P, 2, TOK], F32, A + 69632)
        uraw = at("uraw", [P, 2, D], F32, RING)
        uw = {k: at("uw" + k, [P, 2, D], F32R, RING + 8192 + i * 8192) for i, k in enumerate(("hi", "lo"))}
        vraw = at("vraw", [P, GRP, D], F32, E)
        gmat = at("gmat", [P, 2, NPIECE, GRP, GT], F32, E + 16384)
        fin_g = at("fin_g", [P, D], F32, E)
        fin_o = at("fin_o", [P, TT, D], F32, A)

        ps = ctx.enter_context(nc.psum_tensor("ps", [P, 8, 512], F32))

        vec, sca, poo = sem("vec"), sem("sca"), sem("poo")
        names = """xt_in par_in acc_in fin_in consts xsq_ok xsum_ok sd_ok yf_ok yhi_ok y_ok w_hi w_lo w_used z_out
            gate_out lb_exp lb_max f_sig og_sig og_used hg_ok tr_mm tr_out_v tr_out_s upd_mm state_ok wsc_mm within_ok
            o_mm o_out osq_ok osum_mm osd_ok mt_mm mt_out gate_sig ohg_f ohg_hi ohg_ok asc_mm amax aexp anorm atr_mm atr_out apv_mm
            oat_hi oat_ok br_f m_hi m_ok acc_ok ss_ok ysd_ok ynat_ok ht_mm ht_hi ht_ok q_hi q_ok s_mm s_out
            s_used pos_ok soft soft_exp gate_ok ei_ok ej_ok col_mm col_ok hoti_ok hotj_ok hotg_ok g_mm g_out
            v_in u_hi u_lo v_hi v_lo u_mm gelu_ok prod_ok aw_hi aw_ok o2_mm o2_out fss_ok fsd_ok fin_ok stored"""
        S = {n: sem(n) for n in names.split()}
        w_in, g_store, u_in, gm_in = ([sem(f"{n}{k}") for k in range(2)] for n in ("w_in", "g_store", "u_in", "gm_in"))

        block = ctx.enter_context(nc.Block())


        def key_step(c, a):
            return step_f[:].rearrange("p t (h c) a -> p t h c a", c=2)[:, :, :, c, a:a + 1].to_broadcast([P, TT, RH, TOP])

        @block.sync
        def _(sp):
            sp.dma_start(xt[:], xT).then_inc(S["xt_in"], 16)
            sp.dma_start(par[:], params).then_inc(S["par_in"], 16)
            sp.dma_start(sink[:], sinks.to_broadcast([P, AQ])).then_inc(S["par_in"], 16)
            for k in range(2):
                sp.dma_start(raw[:, k, :], wstream[k]).then_inc(w_in[k], 16)
            with sp.Fori(1, N_TILES // 2, 1) as it:
                for k in range(2):
                    sp.wait_ge(S["w_lo"], it * 2 + (k - 1))
                    sp.dma_start(raw[:, k, :], wstream[bass.ds(it * 2 + k, 1)].rearrange("o p d -> p (o d)")
                                 ).then_inc(w_in[k], 16)
            for k in range(2):
                sp.wait_ge(S["w_lo"], N_TILES - 1 + k)
                sp.dma_start(uraw[:, k, :], uT[k]).then_inc(u_in[k], 16)
            for c in range(NPIECE):
                sp.wait_ge(S["g_out"], (c + 1) * GT // 4)
                sp.dma_start(gates_dram[:, c].rearrange("g j r -> j g r"),
                             piece[:, c % 2].rearrange("p (g i) t -> p g (i t)", i=GRP)).then_inc(g_store[c % 2], 16)
            for k in range(2):
                sp.wait_ge(g_store[k], 16 * NPIECE // 2)
            sp.wait_ge(S["g_mm"], TOK // 4)
            sp.dma_start(gmat[:, 0], gates_dram[0].rearrange("c j r -> j c r")).then_inc(gm_in[0], 16)
            for n in (2, 3):
                sp.wait_ge(S["u_lo"], n - 1)
                sp.dma_start(uraw[:, n % 2, :], uT[n]).then_inc(u_in[n % 2], 16)

            def period(g, s, more=True):
                if more:
                    for b in range(GRP):
                        sp.wait_ge(S["u_lo"], g * GRP + (GRP + b - 1))
                        sp.dma_start(uraw[:, b % 2, :], uT[bass.ds(g * GRP + (GRP + b), 1)]
                                     .rearrange("o p d -> p (o d)")).then_inc(u_in[b % 2], 16)
                        if b == 1:
                            need(sp, S["prod_ok"], g * GRP)
                            sp.dma_start(gmat[:, 1 - s], gates_dram[bass.ds(g + 1, 1)]
                                         .rearrange("o c j r -> j (o c) r")).then_inc(gm_in[1 - s], 16)
                need(sp, S["v_lo"], g * GRP)
                sp.dma_start(vraw[:], v[bass.ds(g * GRP, GRP)].rearrange("i j d -> j i d")).then_inc(S["v_in"], 16)

            period(0, 0)
            with sp.Fori(0, NGRP // 2 - 1, 1) as it:
                period(it * 2 + 1, 1)
                period(it * 2 + 2, 0)
            period(NGRP - 1, 1, more=False)
            sp.wait_ge(S["v_lo"], NGRP * GRP)
            sp.dma_start(fin_g[:], final_g.to_broadcast([P, D])).then_inc(S["fin_in"], 16)
            for tt in range(TT):
                sp.wait_ge(S["fin_ok"], tt + 1)
                sp.dma_start(out[tt * P:(tt + 1) * P, :], fin_o[:, tt, :]).then_inc(S["stored"], 16)
            sp.wait_ge(S["stored"], 16 * TT)

        @block.gpsimd
        def _(pool):
            chain = Chain(pool, poo)
            pool.memset(ones[:], 1.0)
            pool.memset(eps[:], EPS)
            pool.iota(iota[:], [[1, P]], base=0, channel_multiplier=0, allow_small_or_imprecise_dtypes=True)
            pool.memset(ident[:], 0.0)
            pool.memset(bandmask[:], 0.0)
            pool.memset(within[:], 0.0)
            chain.done(pool.memset(chunkmask[:], 1.0))
            chain.done(pool.affine_select(out=ident[:], in_=ident[:], compare_op=ALU.not_equal, fill=1.0,
                                          base=0, pattern=[[-1, P]], channel_multiplier=1))
            chain.done(pool.affine_select(out=bandmask[:, 0:P], in_=bandmask[:, 0:P], compare_op=ALU.is_gt,
                                          fill=HIDDEN, base=0, pattern=[[1, P]], channel_multiplier=-1))
            chain.done(pool.affine_select(out=bandmask[:, P:BAND], in_=bandmask[:, P:BAND], compare_op=ALU.is_ge,
                                          fill=HIDDEN, base=0, pattern=[[-1, P]], channel_multiplier=1))
            for r in range(P // CH):
                band = chunkmask[r * CH:(r + 1) * CH, :]
                chain.done(pool.affine_select(out=band, in_=band, compare_op=ALU.is_ge, fill=0.0,
                                              base=0, pattern=[[1, CH]], channel_multiplier=-1))
            pool.sem_inc(S["consts"], 1)

            def split_lo(n, k, dst):
                pool.wait_ge(S["w_hi"], n + 1)
                pool.tensor_tensor(dst["lo"], raw[:, k, :], dst["hi"].bitcast(F32), ALU.subtract).then_inc(S["w_lo"], 1)

            def slot(k):
                return {part: w[part][:, k, :] for part in w}

            with pool.Fori(0, T_KEYS // 2, 1) as it:
                for k in range(2):
                    split_lo(it * 2 + k, k, slot(k))
            for k in range(2):
                split_lo(T_KEYS + k, k, {p: keys[p][:, k * RH:(k + 1) * RH, :].rearrange("p r n -> p (r n)") for p in keys})
            with pool.Fori(T_WQ // 2, N_TILES // 2, 1) as it:
                for k in range(2):
                    split_lo(it * 2 + k, k, slot(k))

            pool.wait_ge(S["pos_ok"], 1)
            chain.done(pool.tensor_copy(ei[:], key_step(0, 0)))
            for a in range(1, TOP):
                chain.done(pool.tensor_scalar(tmp_i[:], pos[:], float(STARTS[a]), None, ALU.is_ge))
                chain.done(pool.tensor_tensor(tmp_i[:], tmp_i[:], key_step(0, a), ALU.mult))
                ins = pool.tensor_tensor(ei[:], ei[:], tmp_i[:], ALU.add)
                if a < TOP - 1:
                    chain.done(ins)
            ins.then_inc(S["ei_ok"], 1)

            def weigh(it):
                for s in range(2):
                    n = it * 2 + s
                    pool.wait_ge(S["hotj_ok"], n + 1)
                    need(pool, S["g_mm"], it * 8 + (4 * s - 4))
                    pool.tensor_tensor(hot_g[:, s], hot_j[:],
                                       cols[:, 2, bass.ds(n * BATCH, BATCH)].unsqueeze(2).to_broadcast([P, BATCH, NK]),
                                       ALU.mult).then_inc(S["hotg_ok"], 1)

            pool.wait_ge(S["col_ok"], 3)
            weigh(0)
            with pool.Fori(1, TOK // BATCH // 2, 1) as it:
                weigh(it)

        def transposed_dst(n):
            if n < 4:
                return vnat[:, n, :]
            if n == 4:
                return avnat[:].rearrange("p t c -> p (t c)")
            return knat[:, n - 5, :] if n < 9 else kmeta[:]

        def transposed_src(n):
            dst = transposed_dst(n)
            return ps[0:dst.shape[0], 2 + n % 2, 0:dst.shape[1]]

        @block.scalar
        def _(act):
            def split_hi(n, k, dst=None):
                act.wait_ge(w_in[k], (n - k) * 8 + 16)
                if not isinstance(n, int) or n < T_KEYS:
                    need(act, S["w_used"], n - 1)
                elif n >= T_WQ:
                    act.wait_ge(S["w_used"], n - 3)
                act.activation(w["hi"][:, k, :] if dst is None else dst, raw[:, k, :], ACT.Copy).then_inc(S["w_hi"], 1)

            act.wait_ge(S["lb_max"], 1)
            act.activation(lbw[:, 3:5], lbw[:, 1:3], ACT.Exp).then_inc(S["lb_exp"], 1)
            act.wait_ge(S["xt_in"], 16)
            act.activation(xsq[:], xt[:], ACT.Square).then_inc(S["xsq_ok"], 1)
            split_hi(0, 0)
            split_hi(1, 1)
            act.wait_ge(S["xsum_ok"], 1)
            act.activation(sd[:, META:LEN], ps[:, 4, :], ACT.Sqrt, bias=eps[:], scale=1.0 / D).then_inc(S["sd_ok"], 1)
            act.activation(sd[:, 0:META], ps[:, 5, 0:META], ACT.Sqrt, bias=eps[:], scale=1.0 / D).then_inc(S["sd_ok"], 1)
            for c in range(DC):
                act.wait_ge(S["yf_ok"], c + 1)
                act.activation(y["hi"][:, c, :], xt[:, c, :], ACT.Copy).then_inc(S["yhi_ok"], 1)
            def z_tiles(first, last, shift, dst, meta):
                with act.Fori(first // 2, last // 2, 1) as it:
                    for k in range(2):
                        own = bass.ds(it * 2 + (k - shift), 1)
                        act.wait_ge(S["w_used"], it * 2 + (k + 1))
                        if meta:
                            act.activation(znat[:, own, :], ps[0:META, 2 + k:3 + k, 0:P], ACT.Copy)
                            act.activation(dst[:, own, META:LEN], ps[:, k:k + 1, :], ACT.Copy).then_inc(S["z_out"], 1)
                        else:
                            act.activation(dst[:, own, :], ps[:, k:k + 1, :], ACT.Copy).then_inc(S["z_out"], 1)
                        split_hi(it * 2 + (k + 2), k)

            z_tiles(0, 4, 0, zm, True)
            act.wait_ge(S["mt_mm"], 1)
            act.activation(f_z[:, :, 0:META], ps[:, 4, 0:HH * META].rearrange("p (h t) -> p h t", h=HH),
                           ACT.Copy).then_inc(S["mt_out"], 1)
            act.wait_ge(S["mt_out"], 1)
            act.activation(f_z, f_z, ACT.Sigmoid).then_inc(S["f_sig"], 1)
            z_tiles(4, 8, 4, zr, False)
            z_tiles(8, 14, 4, zm, True)
            act.wait_ge(S["mt_mm"], 2)
            act.activation(ak_z[:, 0:META], ps[:, 5, 0:META], ACT.Copy).then_inc(S["mt_out"], 1)
            z_tiles(14, N_Z, 10, zr, False)

            def gate_out(t):
                act.wait_ge(S["w_used"], T_GATE + t + 1)
                act.activation(gates[:, t, :], ps[:, 2 + t % 2, :], ACT.Identity, bias=b_gate[:, t:t + 1]
                               ).then_inc(S["gate_out"], 1)
                split_hi(T_GATE + t + 2, t % 2)

            for n in range(1, 10, 2):
                act.wait_ge(S["tr_mm"], n + 1)
                act.activation(transposed_dst(n), transposed_src(n), ACT.Copy).then_inc(S["tr_out_s"], 1)
            act.wait_ge(S["hg_ok"], 1)
            act.activation(orstd[:], og_z, ACT.Sigmoid).then_inc(S["og_sig"], 1)
            for tt in range(TT):
                act.wait_ge(S["o_mm"], (tt + 1) * P // CH)
                act.activation(o_hg[:, :, tt * P:(tt + 1) * P], ps[:, tt % 2, :].rearrange("p (h t) -> p h t", h=HH),
                               ACT.Copy).then_inc(S["o_out"], 1)
                for t in gate_blocks_done(tt * P // CH * GATES_HG, (tt + 1) * P // CH * GATES_HG):
                    gate_out(t)
            act.wait_ge(S["o_out"], TT)
            act.activation(osq[:], o_hg[:], ACT.Square).then_inc(S["osq_ok"], 1)
            act.wait_ge(S["og_used"], 1)
            for h in range(HH):
                act.wait_ge(S["osum_mm"], h + 1)
                act.activation(orstd[:, h, :], ps[:, 4 + h % 2, :], ACT.Sqrt, bias=eps[:],
                               scale=1.0 / P).then_inc(S["osd_ok"], 1)

            def exponentials(n):
                s, lo = n % 2, P if n < AQ else 0
                act.wait_ge(S["amax"], n + 1)
                need(act, S["atr_mm"], n - 1)
                act.activation(atp[:, s, lo:KEYS + 1], atsc[:, s, lo:KEYS + 1], ACT.Exp, bias=atstat[:, 0, s:s + 1],
                               accum_out=atstat[:, 1, s:s + 1]).then_inc(S["aexp"], 1)

            def turned(n):
                s, lo = n % 2, P if n < AQ else 0
                act.wait_ge(S["atr_mm"], n + 1)
                need(act, S["apv_mm"], n - 1)
                act.activation(atpT[:, s, lo:BAND], ps[:, 4 + s, lo:BAND], ACT.Copy).then_inc(S["atr_out"], 1)
                act.activation(atpTm[:, s, :], ps[0:META, 4 + s, BAND:BAND + P], ACT.Copy).then_inc(S["atr_out"], 1)

            for n in range(TT * AQ + 1):
                if n >= 1:
                    for t in gate_blocks_done(GATES_AT0 + (n - 1) * GATES_AT, GATES_AT0 + n * GATES_AT):
                        gate_out(t)
                if n < TT * AQ:
                    exponentials(n)
                if n >= 1:
                    turned(n - 1)
                if n >= 1 and n % AQ == 0:
                    tt = n // AQ - 1
                    act.wait_ge(S["apv_mm"], n)
                    act.activation(oat["hi"][:, :, tt * P:(tt + 1) * P],
                                   ps[:, tt % 2, :].rearrange("p (c t) -> p c t", c=4), ACT.Copy).then_inc(S["oat_hi"], 1)
            for h in range(HH):
                act.wait_ge(S["ohg_f"], h + 1)
                act.activation(ohg["hi"][:, h, :], o_hg[:, h, :], ACT.Copy).then_inc(S["ohg_hi"], 1)
            act.wait_ge(S["gate_out"], N_GATE)
            for c in range(DC):
                act.activation(gates[:, c:N_GATE:DC, :], gates[:, c:N_GATE:DC, :], ACT.Sigmoid).then_inc(S["gate_sig"], 1)
            act.wait_ge(S["asc_mm"], TT * AQ)
            act.dma_start(acc[:], x.rearrange("(t p) d -> p t d", p=P)).then_inc(S["acc_in"], 16)
            for c in range(DC):
                split_hi(T_BRANCH + c + 2, c % 2)
                act.wait_ge(S["br_f"], c + 1)
                act.activation(m["hi"][:, c, :], mtmp[:, c % 2, 0, :], ACT.Copy).then_inc(S["m_hi"], 1)
            for c in range(DC):
                n = T_OUT + c + 2
                half = slice((n - T_KEYS) * RH, (n - T_KEYS + 1) * RH)
                split_hi(n, c % 2, None if n < T_KEYS else keys["hi"][:, half, :].rearrange("p r n -> p (r n)"))
            for tt in range(TT):
                act.wait_ge(S["acc_ok"], 2 * tt + 2)
                need(act, S["ss_ok"], tt - 1)
                act.activation(ysq[:, tt % 2, :], acc[:, tt, :], ACT.Square,
                               accum_out=rowstat[:, 0, tt:tt + 1]).then_inc(S["ss_ok"], 1)
            act.wait_ge(S["ss_ok"], TT)
            act.activation(rowstat[:, 1, :], rowstat[:, 0, :], ACT.Sqrt, bias=eps[:], scale=1.0 / D).then_inc(S["ysd_ok"], 1)
            split_hi(T_WQ, 0)
            split_hi(T_WQ + 1, 1)
            for c in range(DC):
                act.wait_ge(S["ht_mm"], c + 1)
                act.activation(hT["hi"][:, c, :], ps[:, c % 2, :], ACT.Copy, scale=ffn_g[:, c:c + 1]).then_inc(S["ht_hi"], 1)
            for n in range(RS + 1):
                if n < RS:
                    act.wait_ge(S["w_used"], T_KEYS + n + 1)
                    need(act, S["s_mm"], n - 1)
                    act.activation(q2["hi"][:, n % 2, :], ps[:, n % 2, :], ACT.Copy).then_inc(S["q_hi"], 1)
                    if T_WQ + n + 2 < N_TILES:
                        split_hi(T_WQ + n + 2, n % 2)
                if n >= 1:
                    act.wait_ge(S["s_mm"], n)
                    need(act, S["s_used"], n - 2)
                    act.activation(score[:, (n - 1) % 2], ps[:, 2 + (n - 1) % 2, :].rearrange("p (t n) -> p t n", t=TT),
                                   ACT.Copy).then_inc(S["s_out"], 1)
            act.wait_ge(S["soft"], 1)
            act.activation(gate[:], best[:], ACT.Exp).then_inc(S["soft_exp"], 1)

            def pieces(it):
                for c in range(2):
                    for q in range(GT // 4):
                        act.wait_ge(S["g_mm"], it * (2 * GT // 4) + (c * (GT // 4) + q + 1))
                        if q == 0:
                            need(act, g_store[c], it * 16)
                        act.activation(piece[:, c, :, q * 4:q * 4 + 4].rearrange("p i t -> p t i"),
                                       ps[:, q % 8, :].rearrange("p (t i) -> p t i", t=4), ACT.Copy).then_inc(S["g_out"], 1)

            pieces(0)
            with act.Fori(1, NPIECE // 2, 1) as it:
                pieces(it)

            def u_split(n, k):
                act.wait_ge(u_in[k], (n - k) * 8 + 16)
                need(act, S["u_mm"], n - 1)
                act.activation(uw["hi"][:, k, :], uraw[:, k, :], ACT.Copy).then_inc(S["u_hi"], 1)

            def v_split(g, b):
                if b == 0:
                    act.wait_ge(S["v_in"], g * 16 + 16)
                    need(act, S["o2_mm"], g * 8)
                act.activation(vw["hi"][:, b, :], vraw[:, b, :], ACT.Copy).then_inc(S["v_hi"], 1)

            def period(g, s, more_u=True, first=False):
                for b in range(GRP):
                    n = g * GRP + b
                    for vb in V_SPLITS[b] if not first else ():
                        v_split(g - 1, vb)
                    if more_u or b < 2:
                        u_split(n + 2, b % 2)
                    act.wait_ge(S["u_mm"], n + 1)
                    need(act, S["prod_ok"], n - 1)
                    act.activation(gelu[:, b % 2, :], ps[:, b % 2, :], ACT.Gelu).then_inc(S["gelu_ok"], 1)
                    act.wait_ge(S["prod_ok"], n + 1)
                    if b == 0:
                        need(act, S["o2_mm"], g * 8 - 8)
                    act.activation(act_w["hi"][:, s, b, :], prod[:, b % 2, :], ACT.Copy).then_inc(S["aw_hi"], 1)

            u_split(0, 0)
            u_split(1, 1)
            for k in range(2):
                act.wait_ge(g_store[k], 16 * NPIECE // 2)
            period(0, 0, first=True)
            period(1, 1)
            with act.Fori(1, NGRP // 2 - 1, 1) as it:
                period(it * 2, 0)
                period(it * 2 + 1, 1)
            period(NGRP - 2, 0)
            period(NGRP - 1, 1, more_u=False)
            for b in range(GRP):
                v_split(NGRP - 1, b)
            for tt in range(TT):
                act.wait_ge(S["o2_out"], NGRP * 8 - 8 + 2 * tt + 2)
                need(act, S["fss_ok"], tt)
                act.activation(gelu[:].rearrange("p s t -> p (s t)"), acc[:, tt, :], ACT.Square,
                               accum_out=rowstat[:, 0, tt:tt + 1]).then_inc(S["fss_ok"], 1)
            act.wait_ge(S["fss_ok"], TT)
            act.activation(rowstat[:, 1, :], rowstat[:, 0, :], ACT.Sqrt, bias=eps[:], scale=1.0 / D).then_inc(S["fsd_ok"], 1)

        @block.vector
        def _(dve):
            chain = Chain(dve, vec)
            dve.wait_ge(S["par_in"], 32)
            chain.done(dve.tensor_tensor(lbw[:, 0], lb_logits[:, 0], lb_logits[:, 1], ALU.max))
            for r in range(2):
                ins = dve.tensor_tensor(lbw[:, 1 + r], lb_logits[:, r], lbw[:, 0], ALU.subtract)
            ins.then_inc(S["lb_max"], 1)
            dve.wait_ge(S["lb_exp"], 1)
            chain.done(dve.tensor_tensor(lbw[:, 1], lbw[:, 3], lbw[:, 4], ALU.add))
            chain.done(dve.reciprocal(lbw[:, 2], lbw[:, 1]))
            chain.done(dve.tensor_tensor(lbw[:, 0], lbw[:, 3], lbw[:, 2], ALU.mult))
            chain.done(dve.tensor_scalar(lbw[:, 5], lbw[:, 0], -1.0, 1.0, ALU.mult, ALU.add))
            dve.wait_ge(S["sd_ok"], 2)
            chain.done(dve.reciprocal(rstd[:], sd[:]))
            for c in range(DC):
                dve.scalar_tensor_tensor(out=xt[:, c, :], in0=xt[:, c, :], scalar=mix_g[:, c:c + 1], in1=rstd[:],
                                         op0=ALU.mult, op1=ALU.mult).then_inc(S["yf_ok"], 1)
            for c in range(DC):
                dve.wait_ge(S["yhi_ok"], c + 1)
                dve.tensor_tensor(y["lo"][:, c, :], xt[:, c, :], y["hi"][:, c, :].bitcast(F32),
                                  ALU.subtract).then_inc(S["y_ok"], 1)
            dve.wait_ge(S["f_sig"], 1)
            for h in range(HH):
                ins = dve.tensor_scalar(f_z[:, h, :], f_z[:, h, :], lbw[:, 5, h:h + 1], lbw[:, 0, h:h + 1],
                                        ALU.mult, ALU.add)
            chain.done(ins)
            chain.done(dve.tensor_scalar(kk[:], f_z, -1.0, 1.0, ALU.mult, ALU.add))
            halves = lambda ap: ap.rearrange("p h (b i) -> p (h b) i", i=HALF)
            flat = lambda ap: ap.rearrange("p h l -> p (h l)")
            chain.done(dve.memset(starts[:], 0.0))
            chain.done(dve.tensor_copy(halves(starts[:])[:, :, 0:1], halves(f_z)[:, :, 0:1]))
            chain.done(dve.memset(halves(f_z)[:, :, 0:1], 0.0))
            chain.done(dve.tensor_tensor_scan(flat(decay[:]), flat(f_z), flat(starts[:]), 0.0, ALU.mult, ALU.add))
            chain.done(dve.tensor_scalar(decay[:], decay[:], TINY, None, ALU.max))
            chain.done(dve.reciprocal(inv[:], decay[:]))
            chunks = lambda ap: ap.rearrange("p (c i) -> p c i", i=CH)
            at_mid = lambda ap: chunks(ap)[:, :, HALF - 1:HALF].to_broadcast([P, NCH, HALF])
            dve.wait_ge(S["z_out"], 8)
            chain.done(dve.tensor_tensor(q_z, q_z, decay[:, :, META:LEN], ALU.mult))
            for h in range(HH):
                part = chunks(q_z[:, h, :])[:, :, 0:HALF]
                ins = dve.tensor_tensor(part, part, at_mid(inv[:, h, META:LEN]), ALU.mult)
            chain.done(ins)
            chain.done(dve.tensor_tensor(kk[:], kk[:], inv[:], ALU.mult))
            for h in range(HH):
                part = chunks(kk[:, h, META:LEN])[:, :, 0:HALF]
                ins = dve.tensor_tensor(part, part, at_mid(decay[:, h, META:LEN]), ALU.mult)
            chain.done(ins)
            for h in range(HH):
                ends = decay[:, h, :].rearrange("p (b i) -> p b i", i=HALF)[:, :, HALF - 1]
                ins = dve.tensor_tensor(ecol[:, h, :], ends[:, 0:NBLK - 1:2], ends[:, 1:NBLK:2], ALU.mult)
            chain.done(ins)
            for h in range(HH):
                ins = dve.tensor_tensor(chunks(qi[:, h, :]), chunks(q_z[:, h, :]),
                                        ecol[:, h, :].unsqueeze(2).to_broadcast([P, NCH, CH]), ALU.mult)
            ins.then_inc(S["hg_ok"], 1)
            for n in range(0, 10, 2):
                dve.wait_ge(S["tr_mm"], n + 1)
                dve.tensor_copy(transposed_dst(n), transposed_src(n)).then_inc(S["tr_out_v"], 1)
            dve.wait_ge(S["upd_mm"], 1)
            dve.tensor_copy(state[:, 0, :], ps[:, 4, :]).then_inc(S["state_ok"], 1)
            for c in range(NCH):
                if c * CH % P == 0:
                    tt = c * CH // P
                    dve.wait_ge(S["wsc_mm"], tt + 1)
                    need(dve, S["o_mm"], (tt - 1) * P // CH)
                    for r in range(P // CH):
                        own = slice(r * CH, (r + 1) * CH)
                        ins = dve.tensor_tensor(within[own, tt % 2, :, own],
                                                ps[own, 6 + tt % 2, 0:HH * CH].rearrange("p (h t) -> p h t", h=HH),
                                                chunkmask[own].unsqueeze(1).to_broadcast([CH, HH, CH]), ALU.mult)
                    ins.then_inc(S["within_ok"], 1)
                if c < NCH - 1:
                    dve.wait_ge(S["upd_mm"], c + 2)
                    dve.wait_ge(S["state_ok"], c + 1)
                    need(dve, S["o_mm"], c - 2)
                    for h in range(HH):
                        head = slice(h * P, (h + 1) * P)
                        ins = dve.scalar_tensor_tensor(out=state[:, (c + 1) % 4, head], in0=state[:, c % 4, head],
                                                       scalar=ecol[:, h, c:c + 1], in1=ps[:, 4 + (c + 1) % 2, head],
                                                       op0=ALU.mult, op1=ALU.add)
                    ins.then_inc(S["state_ok"], 1)
            dve.wait_ge(S["og_sig"], 1)
            for h in range(HH):
                ins = dve.scalar_tensor_tensor(out=og_z[:, h, :], in0=og_z[:, h, :], scalar=hg_g[:, h:h + 1],
                                               in1=orstd[:, h, :], op0=ALU.mult, op1=ALU.mult)
            ins.then_inc(S["og_used"], 1)
            dve.wait_ge(S["og_used"], 1)
            dve.wait_ge(S["o_out"], TT)
            chain.done(dve.tensor_tensor(og_z, og_z, o_hg[:], ALU.mult))

            def logits(n):
                s, lo = n % 2, P if n < AQ else 0
                dve.wait_ge(S["asc_mm"], n + 1)
                need(dve, S["aexp"], n - 1)
                head = n % 2 * 4 + n % AQ // 2
                dve.tensor_copy(atsc[:, s, KEYS:KEYS + 1], sink[:, head:head + 1])
                chain.done(dve.scalar_tensor_tensor(out=atsc[:, s, lo:KEYS], in0=ps[:, 6 + s, lo:KEYS],
                                                    scalar=HD ** -0.5, in1=bandmask[:, lo:KEYS],
                                                    op0=ALU.mult, op1=ALU.add))
                dve.tensor_reduce(atstat[:, 0, s:s + 1], atsc[:, s, lo:KEYS + 1], AX_X, ALU.max,
                                  negate=True).then_inc(S["amax"], 1)

            def normalise(n):
                s, lo = n % 2, P if n < AQ else 0
                dve.wait_ge(S["aexp"], n + 1)
                chain.done(dve.reciprocal(atstat[:, 2, s:s + 1], atstat[:, 1, s:s + 1]))
                dve.tensor_scalar(atp[:, s, lo:KEYS], atp[:, s, lo:KEYS], atstat[:, 2, s:s + 1], None,
                                  ALU.mult).then_inc(S["anorm"], 1)

            def attention_lo(tt):
                own = slice(tt * P, (tt + 1) * P)
                dve.wait_ge(S["oat_hi"], tt + 1)
                dve.tensor_tensor(oat["lo"][:, :, own], ps[:, tt % 2, :].rearrange("p (c t) -> p c t", c=4),
                                  oat["hi"][:, :, own].bitcast(F32), ALU.subtract).then_inc(S["oat_ok"], 1)

            dve.wait_ge(S["consts"], 1)
            for n in range(TT * AQ + 1):
                if n < TT * AQ:
                    logits(n)
                if n >= 1:
                    normalise(n - 1)
                if n in (4, 8, 12, 16):
                    h = n // 4 - 1
                    dve.wait_ge(S["osd_ok"], h + 1)
                    chain.done(dve.reciprocal(orstd[:, h, :], orstd[:, h, :]))
                    dve.tensor_tensor(o_hg[:, h, :], og_z[:, h, :], orstd[:, h, :], ALU.mult).then_inc(S["ohg_f"], 1)
                if n > AQ and n % AQ == 2:
                    attention_lo(n // AQ - 1)
            attention_lo(TT - 1)
            for h in range(HH):
                dve.wait_ge(S["ohg_hi"], h + 1)
                dve.tensor_tensor(ohg["lo"][:, h, :], o_hg[:, h, :], ohg["hi"][:, h, :].bitcast(F32),
                                  ALU.subtract).then_inc(S["ohg_ok"], 1)

            dve.wait_ge(S["ohg_ok"], HH)
            for c in range(DC):
                s = c % 2
                dve.wait_ge(S["w_used"], T_BRANCH + c + 1)
                need(dve, S["m_ok"], c - 1)
                dve.wait_ge(S["gate_sig"], c + 1)
                dve.tensor_tensor(mtmp[:, s, 0, :], gates[:, c, :], ps[:, 2 * s, :], ALU.mult)
                chain.done(dve.tensor_tensor(mtmp[:, s, 1, :], gates[:, DC + c, :], ps[:, 2 * s + 1, :], ALU.mult))
                dve.tensor_tensor(mtmp[:, s, 0, :], mtmp[:, s, 0, :], mtmp[:, s, 1, :], ALU.add).then_inc(S["br_f"], 1)
                dve.wait_ge(S["m_hi"], c + 1)
                dve.tensor_tensor(m["lo"][:, c, :], mtmp[:, s, 0, :], m["hi"][:, c, :].bitcast(F32),
                                  ALU.subtract).then_inc(S["m_ok"], 1)
            dve.wait_ge(S["acc_in"], 16)
            dve.wait_ge(S["w_used"], T_OUT + DC)
            for n in range(2 * TT):
                own = acc[:, n // 2, n % 2 * 512:(n % 2 + 1) * 512]
                dve.tensor_tensor(own, own, ps[:, n, :], ALU.add).then_inc(S["acc_ok"], 1)
            dve.wait_ge(S["ysd_ok"], 1)
            chain.done(dve.reciprocal(rowstat[:, 2, :], rowstat[:, 1, :]))
            for tt in range(TT):
                dve.tensor_scalar(ynat[:, tt, :], acc[:, tt, :], rowstat[:, 2, tt:tt + 1], None,
                                  ALU.mult).then_inc(S["ynat_ok"], 1)
            for c in range(DC):
                dve.wait_ge(S["ht_hi"], c + 1)
                dve.scalar_tensor_tensor(out=hT["lo"][:, c, :], in0=ps[:, c % 2, :], scalar=ffn_g[:, c:c + 1],
                                         in1=hT["hi"][:, c, :].bitcast(F32), op0=ALU.mult, op1=ALU.subtract
                                         ).then_inc(S["ht_ok"], 1)

            def set_tops(n):
                s = n % 2
                dve.wait_ge(S["s_out"], n + 1)
                for tt in range(TT):
                    ins = dve.max(top_v[:, tt, n, 0:8], score[:, s, tt, :])
                chain.done(ins)
                for tt in range(TT):
                    dve.max_index(top_i[:, tt, n, 0:8], top_v[:, tt, n, 0:8], score[:, s, tt, :])
                for tt in range(TT):
                    ins = dve.match_replace(scut[:, s, tt, :], top_v[:, tt, n, 0:8], score[:, s, tt, :], LOWEST)
                ins.then_inc(S["s_used"], 1)
                dve.wait_ge(S["s_used"], n + 1)
                for tt in range(TT):
                    ins = dve.max(top_v[:, tt, n, 8:16], scut[:, s, tt, :])
                chain.done(ins)
                for tt in range(TT):
                    ins = dve.max_index(top_i[:, tt, n, 8:16], top_v[:, tt, n, 8:16], scut[:, s, tt, :])
                chain.done(ins)

            for n in range(RS + 1):
                if n < RS:
                    dve.wait_ge(S["q_hi"], n + 1)
                    dve.tensor_tensor(q2["lo"][:, n % 2, :], ps[:, n % 2, :], q2["hi"][:, n % 2, :].bitcast(F32),
                                      ALU.subtract).then_inc(S["q_ok"], 1)
                if n >= 1:
                    set_tops(n - 1)
            tv = top_v[:].rearrange("p t (h c) a -> p (t h) c a", c=2)
            a = 0
            while a < TOP:
                same = PAIRS.count(PAIRS[a])
                wide = PAIRS[a]
                dst = cand[:, :, STARTS[a]:STARTS[a] + same * wide].rearrange("p n (a b) -> p n a b", b=wide)
                ins = dve.tensor_tensor(dst, tv[:, :, 0, a:a + same].unsqueeze(3).to_broadcast([P, TT * RH, same, wide]),
                                        tv[:, :, 1, 0:wide].unsqueeze(2).to_broadcast([P, TT * RH, same, wide]), ALU.add)
                a += same
            chain.done(ins)
            bests = best[:].rearrange("p t h k -> p (t h) k")
            for n in range(TT * RH):
                ins = dve.max(bests[:, n, 0:8], cand[:, n, :])
            chain.done(ins)
            for n in range(TT * RH):
                dve.max_index(pos_u[:, n, 0:8], bests[:, n, 0:8], cand[:, n, :])
            for n in range(TT * RH):
                ins = dve.match_replace(ccut[:, n, :], bests[:, n, 0:8], cand[:, n, :], LOWEST)
            chain.done(ins)
            for n in range(TT * RH):
                ins = dve.max(bests[:, n, 8:16], ccut[:, n, :])
            chain.done(ins)
            for n in range(TT * RH):
                ins = dve.max_index(pos_u[:, n, 8:16], bests[:, n, 8:16], ccut[:, n, :])
            chain.done(ins)
            dve.tensor_copy(top_f[:], top_i[:])
            chain.done(dve.tensor_copy(pos[:].rearrange("p t h k -> p (t h) k"), pos_u[:]))
            dve.tensor_copy(step_f[:, :, :, 0:1], top_f[:, :, :, 0:1])
            dve.tensor_tensor(step_f[:, :, :, 1:TOP], top_f[:, :, :, 1:TOP], top_f[:, :, :, 0:TOP - 1],
                              ALU.subtract).then_inc(S["pos_ok"], 1)
            chain.done(dve.tensor_copy(tot[:, 0, :], bests[:, :, 0]))
            dve.tensor_tensor(bests, bests, tot[:, 0, :].unsqueeze(2).to_broadcast([P, TT * RH, TOP]),
                              ALU.subtract).then_inc(S["soft"], 1)
            dve.wait_ge(S["pos_ok"], 1)
            chain.done(dve.tensor_copy(posb[:], pos[:]))
            for a in range(1, TOP):
                chain.done(dve.tensor_scalar(tmp_j[:], pos[:], float(STARTS[a]), float(PAIRS[a - 1]), ALU.is_ge, ALU.mult))
                chain.done(dve.tensor_tensor(posb[:], posb[:], tmp_j[:], ALU.subtract))
            chain.done(dve.tensor_copy(ej[:], key_step(1, 0)))
            for b in range(1, TOP):
                chain.done(dve.tensor_scalar(tmp_j[:], posb[:], float(b), None, ALU.is_ge))
                chain.done(dve.tensor_tensor(tmp_j[:], tmp_j[:], key_step(1, b), ALU.mult))
                chain.done(dve.tensor_tensor(ej[:], ej[:], tmp_j[:], ALU.add))
            dve.wait_ge(S["soft_exp"], 1)
            gs = gate[:].rearrange("p t h k -> p (t h) k")
            chain.done(dve.tensor_reduce(tot[:, 0, :], gs, AX_X, ALU.add))
            chain.done(dve.reciprocal(tot[:, 1, :], tot[:, 0, :]))
            dve.tensor_tensor(gs, gs, tot[:, 1, :].unsqueeze(2).to_broadcast([P, TT * RH, TOP]),
                              ALU.mult).then_inc(S["gate_ok"], 1)
            for q in range(3):
                dve.wait_ge(S["col_mm"], q + 1)
                dve.tensor_copy(cols[:, q, :], ps[:, 4 + q, :]).then_inc(S["col_ok"], 1)

            def one_hot(it):
                for s in range(2):
                    n = it * 2 + s
                    own = bass.ds(n * BATCH, BATCH)
                    spread = lambda q: cols[:, q, own].unsqueeze(2).to_broadcast([P, BATCH, NK])
                    every = iota[:].unsqueeze(1).to_broadcast([P, BATCH, NK])
                    need(dve, S["hotg_ok"], n)
                    dve.tensor_tensor(hot_j[:], every, spread(1), ALU.is_equal).then_inc(S["hotj_ok"], 1)
                    need(dve, S["g_mm"], it * 8 + (4 * s - 4))
                    dve.tensor_tensor(hot_i[:, s], every, spread(0), ALU.is_equal).then_inc(S["hoti_ok"], 1)

            dve.wait_ge(S["col_ok"], 3)
            one_hot(0)
            with dve.Fori(1, TOK // BATCH // 2, 1) as it:
                one_hot(it)

            def u_split(n, k):
                dve.wait_ge(S["u_hi"], n + 1)
                dve.tensor_tensor(uw["lo"][:, k, :], uraw[:, k, :], uw["hi"][:, k, :].bitcast(F32),
                                  ALU.subtract).then_inc(S["u_lo"], 1)

            def v_split(g, b):
                dve.wait_ge(S["v_hi"], g * GRP + (b + 1))
                dve.tensor_tensor(vw["lo"][:, b, :], vraw[:, b, :], vw["hi"][:, b, :].bitcast(F32),
                                  ALU.subtract).then_inc(S["v_lo"], 1)

            def group(g, s, more_u=True, first=False):
                for b in range(GRP):
                    n = g * GRP + b
                    for vb in V_SPLITS[b] if not first else ():
                        v_split(g - 1, vb)
                    if more_u or b < 2:
                        u_split(n + 2, b % 2)
                    if b == 0:
                        dve.wait_ge(gm_in[s], g * 8 + (16 - 8 * s))
                    dve.wait_ge(S["gelu_ok"], n + 1)
                    need(dve, S["aw_ok"], n - 1)
                    dve.tensor_tensor(prod[:, b % 2, :].rearrange("p (c t) -> p c t", c=NPIECE),
                                      gelu[:, b % 2, :].rearrange("p (c t) -> p c t", c=NPIECE),
                                      gmat[:, s, :, b, :], ALU.mult).then_inc(S["prod_ok"], 1)
                    dve.wait_ge(S["aw_hi"], n + 1)
                    dve.tensor_tensor(act_w["lo"][:, s, b, :], prod[:, b % 2, :], act_w["hi"][:, s, b, :].bitcast(F32),
                                      ALU.subtract).then_inc(S["aw_ok"], 1)

            def add_up(g):
                for j in range(8):
                    own = acc[:, j // 2, j % 2 * 512:(j % 2 + 1) * 512]
                    dve.wait_ge(S["o2_mm"], g * 8 + (j + 1))
                    dve.tensor_tensor(own, own, ps[:, 2 + j % 4, :], ALU.add).then_inc(S["o2_out"], 1)

            u_split(0, 0)
            u_split(1, 1)
            group(0, 0, first=True)
            with dve.Fori(0, NGRP // 2 - 1, 1) as it:
                group(it * 2 + 1, 1)
                add_up(it * 2)
                group(it * 2 + 2, 0)
                add_up(it * 2 + 1)
            group(NGRP - 1, 1, more_u=False)
            for b in range(GRP):
                if b == 0:
                    add_up(NGRP - 2)
                v_split(NGRP - 1, b)
            add_up(NGRP - 1)
            dve.wait_ge(S["fsd_ok"], 1)
            dve.wait_ge(S["fin_in"], 16)
            chain.done(dve.reciprocal(rowstat[:, 2, :], rowstat[:, 1, :]))
            for tt in range(TT):
                dve.scalar_tensor_tensor(out=fin_o[:, tt, :], in0=acc[:, tt, :], scalar=rowstat[:, 2, tt:tt + 1],
                                         in1=fin_g[:], op0=ALU.mult, op1=ALU.mult).then_inc(S["fin_ok"], 1)

        @block.tensor
        def _(pe):
            def three(dst, lhs, rhs, first, last):
                for i, (a, b) in enumerate(SPLIT):
                    ins = pe.matmul(dst, lhs[a], rhs[b], start=first and i == 0, stop=last and i == 2)
                return ins

            def parts(t, *index):
                return {k: t[k].__getitem__((slice(None),) + index) for k in t}

            def project(k, rhs, dst):
                for c in range(DC):
                    own = parts(rhs, c, slice(META, LEN)) if rhs is y else parts(rhs, c)
                    ins = three(dst, parts(w, k, slice(c * P, (c + 1) * P)), own, c == 0, c == DC - 1)
                return ins

            pe.wait_ge(S["consts"], 1)
            pe.wait_ge(S["xsq_ok"], 1)
            for c in range(DC):
                pe.matmul(ps[:, 4, :], ones[:], xsq[:, c, META:LEN], start=c == 0, stop=c == DC - 1)
            for c in range(DC):
                ins = pe.matmul(ps[:, 5, 0:META], ones[:], xsq[:, c, 0:META], start=c == 0, stop=c == DC - 1)
            ins.then_inc(S["xsum_ok"], 1)
            pe.wait_ge(S["y_ok"], DC)

            def z_pair(it, meta):
                for k in range(2):
                    pe.wait_ge(S["w_lo"], it * 2 + (k + 1))
                    need(pe, S["z_out"], it * 2 + (k - 1))
                    ins = project(k, y, ps[:, k, :])
                    if meta:
                        for c in range(DC):
                            ins = three(ps[0:META, 2 + k, 0:P], parts(y, c, slice(0, META)),
                                        parts(w, k, slice(c * P, (c + 1) * P)), c == 0, c == DC - 1)
                    ins.then_inc(S["w_used"], 1)

            def turn_meta(blocks, bank):
                for q, n in enumerate(blocks):
                    ins = pe.transpose(ps[:, bank, q * META:(q + 1) * META], znat[:, n, :], ident[0:META, 0:META])
                ins.then_inc(S["mt_mm"], 1)

            z_pair(0, True)
            z_pair(1, True)
            pe.wait_ge(S["z_out"], 4)
            turn_meta(range(4), 4)
            with pe.Fori(2, 4, 1) as it:
                z_pair(it, False)
            with pe.Fori(4, 7, 1) as it:
                z_pair(it, True)
            pe.wait_ge(S["z_out"], 14)
            turn_meta([8], 5)
            with pe.Fori(7, N_Z // 2, 1) as it:
                z_pair(it, False)

            def gate_products(first, last):
                for i in range(first, last):
                    t, c, (a, b) = i // (3 * DC), i // 3 % DC, SPLIT[i % 3]
                    if i % (3 * DC) == 0:
                        pe.wait_ge(S["w_lo"], T_GATE + t + 1)
                        need(pe, S["gate_out"], t - 1)
                    ins = pe.matmul(ps[:, 2 + t % 2, :], w[a][:, t % 2, c * P:(c + 1) * P], y[b][:, c, META:LEN],
                                    start=i % (3 * DC) == 0, stop=(i + 1) % (3 * DC) == 0)
                    if (i + 1) % (3 * DC) == 0:
                        ins.then_inc(S["w_used"], 1)

            pe.wait_ge(S["z_out"], N_Z)
            for n in range(10):
                need(pe, S["tr_out_s" if n % 2 else "tr_out_v"], n // 2)
                if n == 5:
                    pe.wait_ge(S["hg_ok"], 1)
                tile = lambda tt: slice(META + tt * P, META + (tt + 1) * P)
                if n < 4:
                    srcs = [v_z[:, h, tile(n)] for h in range(HH)]
                elif n == 4:
                    srcs = [av_z[:, tile(tt)] for tt in range(TT)]
                else:
                    srcs = [kk[:, h, tile(n - 5) if n < 9 else slice(0, META)] for h in range(HH)]
                rows = P if n < 9 else META
                for q, src in enumerate(srcs):
                    ins = pe.transpose(ps[0:rows, 2 + n % 2, q * P:(q + 1) * P], src, ident[:])
                ins.then_inc(S["tr_mm"], 1)
            for k in ("tr_out_v", "tr_out_s"):
                pe.wait_ge(S[k], 5)

            def chunk(c):
                return slice(c * CH, (c + 1) * CH)

            def rows(c):
                return slice(c * CH % P, c * CH % P + CH)

            def update(j):
                need(pe, S["state_ok"], j - 1)
                for h in range(HH):
                    head = slice(h * P, (h + 1) * P)
                    if j == 0:
                        k_, v_ = kmeta[:, head], vmeta[:, head]
                    else:
                        k_, v_ = (t[rows(j - 1), (j - 1) * CH // P, head] for t in (knat, vnat))
                    ins = pe.matmul(ps[:, 4 + j % 2, head], k_, v_, start=True, stop=True)
                ins.then_inc(S["upd_mm"], 1)

            update(0)
            for c in range(NCH):
                tt = c * CH // P
                if c * CH % P == 0:
                    need(pe, S["within_ok"], tt - 1)
                    for cc in range(c, c + P // CH):
                        for h in range(HH):
                            ins = pe.matmul(ps[rows(cc), 6 + tt % 2, h * CH:(h + 1) * CH],
                                            kk[:, h, META + cc * CH:META + (cc + 1) * CH], q_z[:, h, chunk(cc)],
                                            start=True, stop=True)
                    ins.then_inc(S["wsc_mm"], 1)
                if c < NCH - 1:
                    update(c + 1)
                if c * CH % P == 0:
                    pe.wait_ge(S["within_ok"], tt + 1)
                    need(pe, S["o_out"], tt - 1)
                    for h in range(HH):
                        pe.matmul(ps[:, tt % 2, h * P:(h + 1) * P], vnat[:, tt, h * P:(h + 1) * P],
                                  within[:, tt % 2, h, :], start=h == 0, stop=False)
                pe.wait_ge(S["state_ok"], c + 1)
                for h in range(HH):
                    head = slice(h * P, (h + 1) * P)
                    dst = ps[:, tt % 2, h * P + c * CH % P:h * P + c * CH % P + CH]
                    ins = pe.matmul(dst, state[:, c % 4, head], qi[:, h, chunk(c)], start=False,
                                    stop=h == HH - 1 and (c + 1) * CH % P == 0)
                ins.then_inc(S["o_mm"], 1)
                gate_products(c * GATES_HG, (c + 1) * GATES_HG)
            pe.wait_ge(S["osq_ok"], 1)
            for h in range(HH):
                need(pe, S["osd_ok"], h - 1)
                pe.matmul(ps[:, 4 + h % 2, :], ones[:], osq[:, h, :], start=True, stop=True).then_inc(S["osum_mm"], 1)

            pe.wait_ge(S["state_ok"], NCH)
            pe.wait_ge(S["o_out"], TT)
            pe.wait_ge(S["osd_ok"], HH)
            pe.wait_ge(S["mt_out"], 2)

            def scores(n):
                tt, c, kv, s = n // AQ, n % AQ // 2, slice(n % 2 * HD, (n % 2 + 1) * HD), n % 2
                need(pe, S["amax"], n - 1)
                lo = P if tt == 0 else 0
                q_ = aq_z[kv, c, tt * P:(tt + 1) * P]
                pe.matmul(ps[:, 6 + s, lo:BAND], q_, ak_z[kv, META + (tt - 1) * P + lo:META + (tt + 1) * P],
                          start=True, stop=True)
                pe.matmul(ps[:, 6 + s, BAND:KEYS], q_, ak_z[kv, 0:META], start=True, stop=True).then_inc(S["asc_mm"], 1)

            def turn(n):
                tt, s = n // AQ, n % 2
                pe.wait_ge(S["anorm"], n + 1)
                need(pe, S["atr_out"], 2 * (n - 1))
                for q in range(0 if tt else 1, 2):
                    pe.transpose(ps[:, 4 + s, q * P:(q + 1) * P], atp[:, s, q * P:(q + 1) * P], ident[:])
                pe.transpose(ps[0:META, 4 + s, BAND:BAND + P], atp[:, s, BAND:KEYS], ident[:]).then_inc(S["atr_mm"], 1)

            def values(n):
                tt, c, kv, s = n // AQ, n % AQ // 2, slice(n % 2 * HD, (n % 2 + 1) * HD), n % 2
                pe.wait_ge(S["atr_out"], 2 * (n + 1))
                if n % AQ == 0:
                    need(pe, S["oat_ok"], tt - 1)
                dst = ps[kv, tt % 2, c * P:(c + 1) * P]
                if tt:
                    pe.matmul(dst, avnat[:, tt - 1, kv], atpT[:, s, 0:P], start=True, stop=False)
                pe.matmul(dst, avnat[:, tt, kv], atpT[:, s, P:BAND], start=tt == 0, stop=False)
                pe.matmul(dst, avmeta[:, kv], atpTm[:, s, :], start=False, stop=True).then_inc(S["apv_mm"], 1)

            for n in range(TT * AQ + 2):
                if n < TT * AQ:
                    scores(n)
                if 1 <= n <= TT * AQ:
                    turn(n - 1)
                if n >= 2:
                    values(n - 2)
                if n < TT * AQ:
                    gate_products(GATES_AT0 + n * GATES_AT, GATES_AT0 + (n + 1) * GATES_AT)

            pe.wait_ge(S["ohg_ok"], HH)
            pe.wait_ge(S["oat_ok"], TT)
            for c in range(DC):
                pe.wait_ge(S["w_lo"], T_BRANCH + c + 1)
                need(pe, S["br_f"], c - 1)
                if c == 0:
                    pe.wait_ge(S["gate_out"], N_GATE)
                s = c % 2
                for side, src in enumerate((ohg, oat)):
                    for q in range(4):
                        ins = three(ps[:, 2 * s + side, :], parts(w, s, slice((side * 4 + q) * P, (side * 4 + q + 1) * P)),
                                    parts(src, q), q == 0, q == 3)
                    if side == 0:
                        continue
                    ins.then_inc(S["w_used"], 1)
            pe.wait_ge(S["m_ok"], DC)
            for c in range(DC):
                pe.wait_ge(S["w_lo"], T_OUT + c + 1)
                for n in range(2 * TT):
                    ins = three(ps[:, n, :], parts(m, c, slice(n // 2 * P, (n // 2 + 1) * P)),
                                parts(w, c % 2, slice(n % 2 * 512, (n % 2 + 1) * 512)), c == 0, c == DC - 1)
                ins.then_inc(S["w_used"], 1)
            pe.wait_ge(S["ynat_ok"], TT)
            for c in range(DC):
                need(pe, S["ht_ok"], c - 1)
                for tt in range(TT):
                    ins = pe.transpose(ps[:, c % 2, tt * P:(tt + 1) * P], ynat[:, tt, c * P:(c + 1) * P], ident[:])
                ins.then_inc(S["ht_mm"], 1)
            pe.wait_ge(S["ht_ok"], DC)
            for n in range(RS + 1):
                if n < RS:
                    pe.wait_ge(S["w_lo"], T_WQ + n + 1)
                    need(pe, S["q_ok"], n - 1)
                    project(n % 2, hT, ps[:, n % 2, :]).then_inc(S["w_used"], 1)
                if n >= 1:
                    r = n - 1
                    pe.wait_ge(S["q_ok"], n)
                    need(pe, S["s_out"], r - 1)
                    for tt in range(TT):
                        ins = three(ps[:, 2 + r % 2, tt * P:(tt + 1) * P], parts(q2, r % 2, slice(tt * P, (tt + 1) * P)),
                                    parts(keys, r), True, True)
                    ins.then_inc(S["s_mm"], 1)
            for q, (t, ok) in enumerate(((ei, "ei_ok"), (ej, None), (gate, "gate_ok"))):
                if q == 0:
                    pe.wait_ge(S["gate_ok"], 1)
                if ok:
                    pe.wait_ge(S[ok], 1)
                for tt in range(TT):
                    ins = pe.transpose(ps[:, 4 + q, tt * P:(tt + 1) * P],
                                       t[:, tt].rearrange("p h k -> p (h k)"), ident[:])
                ins.then_inc(S["col_mm"], 1)

            def gate_matrices(it):
                for s in range(2):
                    n = it * 2 + s
                    pe.wait_ge(S["hotg_ok"], n + 1)
                    pe.wait_ge(S["hoti_ok"], n + 1)
                    for q in range(BATCH // 4):
                        bank = s * 4 + q
                        need(pe, S["g_out"], it * 8 + (bank - 7))
                        for t in range(4):
                            ins = pe.matmul(ps[:, bank, t * P:(t + 1) * P], hot_g[:, s, q * 4 + t, :],
                                            hot_i[:, s, q * 4 + t, :], start=True, stop=True)
                        ins.then_inc(S["g_mm"], 1)

            pe.wait_ge(S["col_ok"], 3)
            gate_matrices(0)
            with pe.Fori(1, TOK // BATCH // 2, 1) as it:
                gate_matrices(it)

            def u_group(g):
                for b in range(GRP):
                    n = g * GRP + b
                    pe.wait_ge(S["u_lo"], n + 1)
                    need(pe, S["gelu_ok"], n - 1)
                    for c in range(DC):
                        ins = three(ps[:, b % 2, :], parts(uw, b % 2, slice(c * P, (c + 1) * P)), parts(hT, c),
                                    c == 0, c == DC - 1)
                    ins.then_inc(S["u_mm"], 1)

            def v_group(g, s):
                pe.wait_ge(S["aw_ok"], g * GRP + GRP)
                pe.wait_ge(S["v_lo"], g * GRP + GRP)
                for j in range(2 * TT):
                    need(pe, S["o2_out"], g * 8 + (j - 3))
                    for b in range(GRP):
                        ins = three(ps[:, 2 + j % 4, :], parts(act_w, s, b, slice(j // 2 * P, (j // 2 + 1) * P)),
                                    parts(vw, b, slice(j % 2 * 512, (j % 2 + 1) * 512)), b == 0, b == GRP - 1)
                    ins.then_inc(S["o2_mm"], 1)

            pe.wait_ge(S["g_out"], TOK // 4)
            u_group(0)
            u_group(1)
            v_group(0, 0)
            with pe.Fori(0, NGRP // 2 - 1, 1) as it:
                u_group(it * 2 + 2)
                v_group(it * 2 + 1, 1)
                u_group(it * 2 + 3)
                v_group(it * 2 + 2, 0)
            v_group(NGRP - 1, 1)


def kernel(x, meta_tokens, mix_norm_g, w_in, b_gate, hg_lb_logits, hg_norm_g, attn_sinks, w_branch_hg,
           w_branch_attn, w_out, ffn_norm_g, peer_w_q, peer_subkeys, peer_u, peer_v, final_norm_g):
    import numpy as np
    from concourse import bacc
    from concourse.bass_utils import run_bass_kernel_spmd

    a = np.asarray

    def columns(t):
        return a(t).reshape(-1, P).T

    def blocks(t):
        t = a(t)
        return t.reshape(DC, P, t.shape[1] // P, P).transpose(2, 1, 0, 3).reshape(-1, P, D)

    tokens = a(x)[0]
    both = np.concatenate([a(meta_tokens), tokens], axis=0)
    w = a(w_in)[0]
    width = HH * P
    f, q, v_, og = w[:, width:2 * width], w[:, 0:width], w[:, 2 * width:3 * width], w[:, 3 * width:4 * width]
    at0 = 4 * width
    aq, ak, av = w[:, at0:at0 + AQ * HD], w[:, at0 + 512:at0 + 640], w[:, at0 + 640:at0 + 768]
    aq = aq.reshape(D, 2, 4, HD).transpose(0, 2, 1, 3).reshape(D, AQ * HD)
    wb_at = a(w_branch_attn)[0].reshape(2, 4, HD, D).transpose(1, 0, 2, 3).reshape(AQ * HD, D)
    gates = w[:, at0 + 768:]
    branch = np.concatenate([a(w_branch_hg)[0], wb_at], axis=0)
    keys = a(peer_subkeys)[0].reshape(RS, NK, P).transpose(2, 0, 1).reshape(P, 2, RH * NK).transpose(1, 0, 2)
    wstream = np.concatenate([blocks(f), blocks(q), blocks(v_), blocks(ak), blocks(av), blocks(og), blocks(aq),
                              blocks(gates), blocks(branch), a(w_out)[0].reshape(DC, P, D), keys,
                              blocks(a(peer_w_q)[0])], axis=0)
    assert wstream.shape == (N_TILES, P, D)
    params = np.concatenate([columns(mix_norm_g), columns(ffn_norm_g), columns(hg_norm_g),
                             columns(hg_lb_logits), columns(b_gate)], axis=1)
    arrays = {
        "xT": both.T.reshape(DC, P, LEN).transpose(1, 0, 2),
        "x": tokens,
        "params": params,
        "sinks": a(attn_sinks),
        "final_g": a(final_norm_g)[None],
        "wstream": wstream,
        "uT": a(peer_u)[0].reshape(NK, NK, DC, P).transpose(0, 3, 2, 1).reshape(NK, P, D),
        "v": a(peer_v)[0].reshape(NK, NK, D),
    }
    nc = bacc.Bacc("TRN2", target_bir_lowering=False, num_devices=1)
    arrays = {f"in_{k}": np.ascontiguousarray(t) for k, t in arrays.items()}
    ins = [nc.dram_tensor(k, t.shape, F32, kind="ExternalInput").ap() for k, t in arrays.items()]
    gates_dram = nc.dram_tensor("gates_dram", [NGRP, NPIECE, P, GRP * GT], F32, kind="Internal").ap()
    out = nc.dram_tensor("out", (TOK, D), F32, kind="ExternalOutput").ap()
    build(nc, *ins, gates_dram, out)
    r = run_bass_kernel_spmd(nc, [arrays], core_ids=[0])
    return r.results[0]["out"].reshape(1, TOK, D)
```

```python
from contextlib import ExitStack

import concourse.bass as bass
from concourse import mybir

F32 = mybir.dt.float32
F32R = mybir.dt.float32r
U32 = mybir.dt.uint32
ALU = mybir.AluOpType
ACT = mybir.ActivationFunctionType
AX_X = mybir.AxisListType.X

P = 128
D = 1024
DC = D // P
TOK = 512
TT = TOK // P
META = 16
LEN = META + TOK
EPS = 1e-6
HH = 4
CH = 32
HALF = CH // 2
NCH = TOK // CH
NBLK = LEN // HALF
TINY = 1e-37
AQ = 8
HD = 64
BAND = 2 * P
KEYS = BAND + META
HIDDEN = -1e30
RH = 8
RS = 2 * RH
NK = 128
TOP = 16
PAIRS = [TOP // (a + 1) for a in range(TOP)]
STARTS = [sum(PAIRS[:a]) for a in range(TOP)]
CAND = sum(PAIRS)
LOWEST = -3.0e38

Z_META = 10
Z_REST = 12
N_Z = Z_META + Z_REST
N_GATE = 16
T_GATE = N_Z
T_BRANCH = T_GATE + N_GATE
T_OUT = T_BRANCH + DC
T_KEYS = T_OUT + DC
T_WQ = T_KEYS + 2
N_TILES = T_WQ + RS

GRP = 4
NGRP = NK // GRP
GT = 64
NPIECE = TOK // GT
BATCH = 8
EARLY_TOP, EARLY_GATES, EARLY_LAST = 4, 2, 2
EARLY = EARLY_TOP + EARLY_GATES + EARLY_LAST
SPILLED = EARLY - 2
NEARLY = EARLY * GRP
NTOP = EARLY_TOP * GRP
NLAST = NEARLY - EARLY_LAST * GRP
assert EARLY_GATES * GRP == NPIECE and EARLY_LAST == 2
EI_POOL = 6
GATES_HG = 6
GATES_AT = 9
assert NCH * GATES_HG + TT * AQ * GATES_AT == N_GATE * 3 * DC
GATES_AT0 = NCH * GATES_HG
V_SPLITS = ((0, 1), (2,), (3,), ())

SPLIT = (("hi", "hi"), ("hi", "lo"), ("lo", "hi"))


def need(eng, semaphore, value):
    if not (isinstance(value, int) and value <= 0):
        eng.wait_ge(semaphore, value)


def gate_blocks_done(first, last):
    return range(first // (3 * DC), last // (3 * DC))


class Chain:

    def __init__(self, eng, sem):
        self.eng, self.sem, self.count = eng, sem, 0

    def done(self, ins):
        ins.then_inc(self.sem, 1)
        self.count += 1
        self.eng.wait_ge(self.sem, self.count)


def build(nc, xT, x, params, sinks, final_g, wstream, uT, v, gates_dram, early_dram, out):
    ctx = ExitStack()
    with ctx:
        BASE = 16512

        def at(name, shape, dt, offset):
            return nc.alloc_sbuf_tensor_at(name, shape, dt, offset=BASE + offset)

        def sem(name):
            return ctx.enter_context(nc.semaphore(name))

        C, A, B, Z, G0, RING, E, X = 0, 8192, 41984, 58880, 105344, 138112, 162688, 179584
        ident = at("ident", [P, P], F32, C)
        ones = at("ones", [P, P], F32, C + 512)
        iota = at("iota", [P, P], F32, C + 1024)
        bandmask = at("bandmask", [P, KEYS], F32, C + 1536)
        chunkmask = at("chunkmask", [P, CH], F32, C + 2624)
        par = at("par", [P, 44], F32, C + 2752)
        sink = at("sink", [P, AQ], F32, C + 2944)
        eps = at("eps", [P, 1], F32, C + 2976)
        lbw = at("lbw", [P, 6, HH], F32, C + 3008)
        rowstat = at("rowstat", [P, 3, TT], F32, C + 3104)
        atstat = at("atstat", [P, 3, 2], F32, C + 3168)
        ecol = at("ecol", [P, HH, NCH], F32, C + 3200)
        sd = at("sd", [P, LEN], F32, C + 3456)
        rstd = at("rstd", [P, LEN], F32, C + 5568)
        mix_g, ffn_g, hg_g = par[:, 0:8], par[:, 8:16], par[:, 16:20]
        lb_logits = par[:, 20:28].rearrange("p (r h) -> p r h", r=2)
        b_gate = par[:, 28:44]

        y = {k: at("y" + k, [P, DC, LEN], F32R, A + i * DC * LEN * 4) for i, k in enumerate(("hi", "lo"))}
        xt = at("xt", [P, DC, LEN], F32, B)
        xsq = at("xsq", [P, DC, LEN], F32, Z)
        zm = at("zm", [P, Z_META, LEN], F32, Z)
        zr = at("zr", [P, Z_REST, TOK], F32, Z + Z_META * LEN * 4)
        f_z, v_z, ak_z, av_z = zm[:, 0:4], zm[:, 4:8], zm[:, 8], zm[:, 9]
        q_z, og_z, aq_z = zr[:, 0:4], zr[:, 4:8], zr[:, 8:12]
        gates = at("gates", [P, N_GATE, TOK], F32, G0)
        raw = at("raw", [P, 2, D], F32, RING)
        w = {k: at("w" + k, [P, 2, D], F32R, RING + 8192 + i * 8192) for i, k in enumerate(("hi", "lo"))}
        decay = at("decay", [P, HH, LEN], F32, B)
        inv = at("inv", [P, HH, LEN], F32, B + 8448)
        starts = at("starts", [P, HH, LEN], F32, B + 8448)
        kk = at("kk", [P, HH, LEN], F32, E)
        qi = at("qi", [P, HH, TOK], F32, E + 8448)
        knat = at("knat", [P, TT, 512], F32, Z)
        vnat = at("vnat", [P, TT, 512], F32, X + 12288)
        znat = at("znat", [META, Z_META, P], F32, X + 20480)
        vmeta = znat[:, 4:8, :].rearrange("p h d -> p (h d)")
        avmeta = znat[:, 9, :]
        kmeta = at("kmeta", [META, 512], F32, X + 25600)
        avnat = at("avnat", [P, TT, P], F32, X + 27648)
        atsc = at("atsc", [P, 2, KEYS + 8], F32, X)
        atp = at("atp", [P, 2, KEYS + 8], F32, X + 2240)
        atpT = at("atpT", [P, 2, BAND], F32, X + 4480)
        atpTm = at("atpTm", [META, 2, P], F32, X + 6528)
        state = at("state", [P, 4, 512], F32, X)
        within = at("within", [P, 2, HH, P], F32, X + 8192)
        osq = at("osq", [P, HH, TOK], F32, Z)
        o_hg = at("o_hg", [P, HH, TOK], F32, B)
        orstd = at("orstd", [P, HH, TOK], F32, B + 8192)
        ohg = {k: at("ohg" + k, [P, HH, TOK], F32R, Z + i * 8192) for i, k in enumerate(("hi", "lo"))}
        oat = {k: at("oat" + k, [P, 4, TOK], F32R, E + i * 8192) for i, k in enumerate(("hi", "lo"))}
        m = {k: at("m" + k, [P, DC, TOK], F32R, A + i * 16384) for i, k in enumerate(("hi", "lo"))}
        mtmp = at("mtmp", [P, 2, 2, TOK], F32, B)
        acc = at("acc", [P, TT, D], F32, Z + Z_META * LEN * 4 + 8192)
        ynat = at("ynat", [P, TT, D], F32, E)
        ysq = at("ysq", [P, 2, D], F32, A)
        hT = {k: at("hT" + k, [P, DC, TOK], F32R, G0 + i * 16384) for i, k in enumerate(("hi", "lo"))}
        keys = {k: at("keys" + k, [P, RS, NK], F32R, E + 16384 + i * 8192) for i, k in enumerate(("hi", "lo"))}
        q2 = {k: at("q2" + k, [P, 2, TOK], F32R, A + i * 4096) for i, k in enumerate(("hi", "lo"))}
        score = at("score", [P, 2, TT, NK], F32, A + 8192)
        scut = at("scut", [P, 2, TT, NK], F32, A + 12288)
        top_v = at("top_v", [P, TT, RS, TOP], F32, A + 16384)
        top_i = at("top_i", [P, TT, RS, TOP], U32, A + 20480)
        top_f = at("top_f", [P, TT, RS, TOP], F32, A + 24576)
        step_f = at("step_f", [P, TT, RS, TOP], F32, A + 28672)
        cand = at("cand", [P, TT * RH, CAND], F32, A + 32768)
        ccut = at("ccut", [P, TT * RH, CAND], F32, A + 39168)
        best = at("best", [P, TT, RH, TOP], F32, E)
        pos_u = at("pos_u", [P, TT * RH, TOP], U32, E + 2048)
        pos = at("pos", [P, TT, RH, TOP], F32, E + 4096)
        gate = at("gate", [P, TT, RH, TOP], F32, E + 6144)
        tot = at("tot", [P, 2, TT * RH], F32, E + 8192)
        ei = at("ei", [P, TT, RH, TOP], F32, E + 8448)
        ej = at("ej", [P, TT, RH, TOP], F32, E + 10496)
        posb = at("posb", [P, TT, RH, TOP], F32, E + 12544)
        tmp_i = at("tmp_i", [P, TT, RH, TOP], F32, A + 47616)
        tmp_j = at("tmp_j", [P, TT, RH, TOP], F32, A + 45568)
        ei_high = at("ei_high", [P, TT, RH, TOP], F32, A + 49664)
        cols = at("cols", [P, 3, TOK], F32, E + 24576)
        hot_i = at("hot_i", [P, 2, BATCH, NK], F32, E + 0)
        hot_g = at("hot_g", [P, 2, BATCH, NK], F32, E + 8192)
        hot_j = at("hot_j", [P, 2, BATCH, NK], F32, E + 16384)
        early = at("early", [P, 2, GRP, TOK], F32, E + 32768)
        piece = at("piece", [P, 2, NK, GT], F32, A)
        vw = {k: at("vw" + k, [P, GRP, D], F32R, A + i * 16384) for i, k in enumerate(("hi", "lo"))}
        act_w = {k: at("aw" + k, [P, 2, GRP, TOK], F32R, A + 32768 + i * 16384) for i, k in enumerate(("hi", "lo"))}
        gelu = at("gelu", [P, 2, TOK], F32, A + 65536)
        prod = at("prod", [P, 2, TOK], F32, A + 69632)
        uraw = at("uraw", [P, 2, D], F32, RING)
        uw = {k: at("uw" + k, [P, 2, D], F32R, RING + 8192 + i * 8192) for i, k in enumerate(("hi", "lo"))}
        vraw = at("vraw", [P, GRP, D], F32, E)
        gmat = at("gmat", [P, 2, NPIECE, GRP, GT], F32, E + 16384)
        fin_g = at("fin_g", [P, D], F32, E)
        fin_o = at("fin_o", [P, TT, D], F32, A)

        ps = ctx.enter_context(nc.psum_tensor("ps", [P, 8, 512], F32))

        vec, sca, poo = sem("vec"), sem("sca"), sem("poo")
        names = """xt_in par_in acc_in fin_in consts xsq_ok xsum_ok sd_ok yf_ok yhi_ok y_ok w_hi w_lo w_used z_out
            gate_out lb_exp lb_max f_sig og_sig og_used hg_ok tr_mm tr_out_v tr_out_s upd_mm state_ok wsc_mm within_ok
            o_mm o_out osq_ok osum_mm osd_ok mt_mm mt_out gate_sig ohg_f ohg_hi ohg_ok asc_mm amax aexp anorm atr_mm atr_out apv_mm
            oat_hi oat_ok br_f m_hi m_ok acc_ok ss_ok ysd_ok ynat_ok ht_mm ht_hi ht_ok early_mm early_in q_hi q_ok s_mm s_out
            s_used pos_ok soft soft_exp gate_ok ei_ok ej_ok col_mm col_ok hoti_ok hotj_ok hotg_ok g_mm g_out
            v_in u_hi u_lo v_hi v_lo u_mm gelu_ok prod_ok aw_hi aw_ok o2_mm o2_out fss_ok fsd_ok fin_ok stored"""
        S = {n: sem(n) for n in names.split()}
        w_in, g_store, u_in, gm_in, early_out = ([sem(f"{n}{k}") for k in range(2)] for n in
                                                 ("w_in", "g_store", "u_in", "gm_in", "early_out"))

        block = ctx.enter_context(nc.Block())


        def key_step(c, a):
            return step_f[:].rearrange("p t (h c) a -> p t h c a", c=2)[:, :, :, c, a:a + 1].to_broadcast([P, TT, RH, TOP])

        @block.sync
        def _(sp):
            sp.dma_start(xt[:], xT).then_inc(S["xt_in"], 16)
            sp.dma_start(par[:], params).then_inc(S["par_in"], 16)
            sp.dma_start(sink[:], sinks.to_broadcast([P, AQ])).then_inc(S["par_in"], 16)
            for k in range(2):
                sp.dma_start(raw[:, k, :], wstream[k]).then_inc(w_in[k], 16)
            with sp.Fori(1, N_TILES // 2, 1) as it:
                for k in range(2):
                    sp.wait_ge(S["w_lo"], it * 2 + (k - 1))
                    sp.dma_start(raw[:, k, :], wstream[bass.ds(it * 2 + k, 1)].rearrange("o p d -> p (o d)")
                                 ).then_inc(w_in[k], 16)
            for k in range(2):
                sp.wait_ge(S["w_lo"], N_TILES - 1 + k)
                sp.dma_start(uraw[:, k, :], uT[k]).then_inc(u_in[k], 16)
            with sp.Fori(1, NTOP // 2 + 2, 1) as it:
                for k in range(2):
                    sp.wait_ge(S["u_lo"], it * 2 + (k - 1))
                    sp.dma_start(uraw[:, k, :], uT[bass.ds(it * 2 + k, 1)].rearrange("o p d -> p (o d)")
                                 ).then_inc(u_in[k], 16)
            for c in range(NPIECE):
                if c:
                    n = NTOP + 3 + c
                    sp.wait_ge(S["u_lo"], n - 1)
                    sp.dma_start(uraw[:, n % 2, :], uT[n]).then_inc(u_in[n % 2], 16)
                sp.wait_ge(S["g_out"], (c + 1) * GT // 4)
                sp.dma_start(gates_dram[:, c].rearrange("g j r -> j g r"),
                             piece[:, c % 2].rearrange("p (g i) t -> p g (i t)", i=GRP)).then_inc(g_store[c % 2], 16)
            for k in range(2):
                sp.wait_ge(g_store[k], 16 * NPIECE // 2)
            sp.wait_ge(S["g_mm"], TOK // 4)
            def early_groups(it):
                for s in range(2):
                    g = NLAST // GRP + s if isinstance(it, int) else it * 2 + (s - 2)
                    need(sp, S["prod_ok"], it * 2 * GRP + (s - 1) * GRP)
                    gates_of = gates_dram[bass.ds(g, 1)].rearrange("o c j r -> j (o c) r")
                    sp.dma_start(gmat[:, s], gates_of).then_inc(gm_in[s], 16)
                    if not isinstance(it, int):
                        sp.dma_start(early[:, s].rearrange("p b t -> p (b t)"), early_dram[bass.ds(g, 1)]
                                     .rearrange("o p d -> p (o d)")).then_inc(S["early_in"], 16)
                    need(sp, S["v_lo"], it * 2 * GRP + s * GRP)
                    sp.dma_start(vraw[:], v[bass.ds(g * GRP, GRP)].rearrange("i j d -> j i d")).then_inc(S["v_in"], 16)

            early_groups(0)
            for k in range(2):
                sp.wait_ge(early_out[k], 16 * SPILLED // 2)
            with sp.Fori(1, EARLY // 2, 1) as it:
                early_groups(it)
            sp.wait_ge(S["prod_ok"], (EARLY - 1) * GRP)
            sp.dma_start(gmat[:, 0], gates_dram[EARLY].rearrange("c j r -> j c r")).then_inc(gm_in[0], 16)
            for n in (2, 3):
                sp.wait_ge(S["u_lo"], NEARLY + n - 1)
                sp.dma_start(uraw[:, n % 2, :], uT[NEARLY + n]).then_inc(u_in[n % 2], 16)

            def load_v(g):
                sp.wait_ge(S["v_lo"], g * GRP)
                sp.dma_start(vraw[:], v[bass.ds(g * GRP, GRP)].rearrange("i j d -> j i d")).then_inc(S["v_in"], 16)

            def period(g, s, more=True):
                if isinstance(g, int) and g == EARLY:
                    load_v(g)
                if more:
                    for b in range(GRP):
                        sp.wait_ge(S["u_lo"], g * GRP + (GRP + b - 1))
                        sp.dma_start(uraw[:, b % 2, :], uT[bass.ds(g * GRP + (GRP + b), 1)]
                                     .rearrange("o p d -> p (o d)")).then_inc(u_in[b % 2], 16)
                        if b == 1:
                            need(sp, S["prod_ok"], g * GRP)
                            sp.dma_start(gmat[:, 1 - s], gates_dram[bass.ds(g + 1, 1)]
                                         .rearrange("o c j r -> j (o c) r")).then_inc(gm_in[1 - s], 16)
                if not (isinstance(g, int) and g == EARLY):
                    load_v(g)

            period(EARLY, 0)
            with sp.Fori(EARLY // 2, NGRP // 2 - 1, 1) as it:
                period(it * 2 + 1, 1)
                period(it * 2 + 2, 0)
            period(NGRP - 1, 1, more=False)
            sp.wait_ge(S["v_lo"], NGRP * GRP)
            sp.dma_start(fin_g[:], final_g.to_broadcast([P, D])).then_inc(S["fin_in"], 16)
            for tt in range(TT):
                sp.wait_ge(S["fin_ok"], tt + 1)
                sp.dma_start(out[tt * P:(tt + 1) * P, :], fin_o[:, tt, :]).then_inc(S["stored"], 16)
            sp.wait_ge(S["stored"], 16 * TT)

        @block.gpsimd
        def _(pool):
            chain = Chain(pool, poo)
            pool.memset(ones[:], 1.0)
            pool.memset(eps[:], EPS)
            pool.iota(iota[:], [[1, P]], base=0, channel_multiplier=0, allow_small_or_imprecise_dtypes=True)
            pool.memset(ident[:], 0.0)
            pool.memset(bandmask[:], 0.0)
            pool.memset(within[:], 0.0)
            chain.done(pool.memset(chunkmask[:], 1.0))
            chain.done(pool.affine_select(out=ident[:], in_=ident[:], compare_op=ALU.not_equal, fill=1.0,
                                          base=0, pattern=[[-1, P]], channel_multiplier=1))
            chain.done(pool.affine_select(out=bandmask[:, 0:P], in_=bandmask[:, 0:P], compare_op=ALU.is_gt,
                                          fill=HIDDEN, base=0, pattern=[[1, P]], channel_multiplier=-1))
            chain.done(pool.affine_select(out=bandmask[:, P:BAND], in_=bandmask[:, P:BAND], compare_op=ALU.is_ge,
                                          fill=HIDDEN, base=0, pattern=[[-1, P]], channel_multiplier=1))
            for r in range(P // CH):
                band = chunkmask[r * CH:(r + 1) * CH, :]
                chain.done(pool.affine_select(out=band, in_=band, compare_op=ALU.is_ge, fill=0.0,
                                              base=0, pattern=[[1, CH]], channel_multiplier=-1))
            pool.sem_inc(S["consts"], 1)

            def split_lo(n, k, dst):
                pool.wait_ge(S["w_hi"], n + 1)
                pool.tensor_tensor(dst["lo"], raw[:, k, :], dst["hi"].bitcast(F32), ALU.subtract).then_inc(S["w_lo"], 1)

            def slot(k):
                return {part: w[part][:, k, :] for part in w}

            with pool.Fori(0, T_KEYS // 2, 1) as it:
                for k in range(2):
                    split_lo(it * 2 + k, k, slot(k))
            for k in range(2):
                split_lo(T_KEYS + k, k, {p: keys[p][:, k * RH:(k + 1) * RH, :].rearrange("p r n -> p (r n)") for p in keys})
            with pool.Fori(T_WQ // 2, N_TILES // 2, 1) as it:
                for k in range(2):
                    split_lo(it * 2 + k, k, slot(k))

            def u_split(n):
                pool.wait_ge(S["u_hi"], n + 1)
                pool.tensor_tensor(uw["lo"][:, n % 2, :], uraw[:, n % 2, :], uw["hi"][:, n % 2, :].bitcast(F32),
                                   ALU.subtract).then_inc(S["u_lo"], 1)

            for n in range(NTOP // 2):
                u_split(n)
            pool.wait_ge(S["pos_ok"], 1)
            chain.done(pool.tensor_copy(ei[:], key_step(0, 0)))
            for a in range(1, EI_POOL):
                if a % 2:
                    u_split(NTOP // 2 + a // 2)
                chain.done(pool.tensor_scalar(tmp_i[:], pos[:], float(STARTS[a]), None, ALU.is_ge))
                chain.done(pool.tensor_tensor(tmp_i[:], tmp_i[:], key_step(0, a), ALU.mult))
                ins = pool.tensor_tensor(ei[:], ei[:], tmp_i[:], ALU.add)
                if a < EI_POOL - 1:
                    chain.done(ins)
            ins.then_inc(S["ei_ok"], 1)
            for n in range(NTOP // 2 + EI_POOL // 2, NTOP + 2):
                u_split(n)

            def weigh(it):
                for c in range(2):
                    for s in range(GT // BATCH):
                        batch = it * (2 * GT // BATCH) + (c * GT // BATCH + s)
                        pool.wait_ge(S["hotj_ok"], batch + 1)
                        need(pool, S["g_mm"], it * (2 * GT // 4) + (c * GT // 4 + 2 * s - 2))
                        pool.tensor_tensor(hot_g[:, s % 2], hot_j[:, s % 2], cols[:, 2, bass.ds(batch * BATCH, BATCH)]
                                           .unsqueeze(2).to_broadcast([P, BATCH, NK]), ALU.mult).then_inc(S["hotg_ok"], 1)
                        if s == 4 and not (isinstance(it, int) and it * 2 + c == 0):
                            pool.wait_ge(S["u_hi"], it * 2 + (NTOP + 2 + c))
                            pool.tensor_tensor(uw["lo"][:, 1 - c, :], uraw[:, 1 - c, :], uw["hi"][:, 1 - c, :].bitcast(F32),
                                               ALU.subtract).then_inc(S["u_lo"], 1)

            pool.wait_ge(S["col_ok"], 3)
            weigh(0)
            with pool.Fori(1, NPIECE // 2, 1) as it:
                weigh(it)
            for n in range(NLAST + 1, NEARLY + 2):
                u_split(n)

        def transposed_dst(n):
            if n < 4:
                return vnat[:, n, :]
            if n == 4:
                return avnat[:].rearrange("p t c -> p (t c)")
            return knat[:, n - 5, :] if n < 9 else kmeta[:]

        def transposed_src(n):
            dst = transposed_dst(n)
            return ps[0:dst.shape[0], 2 + n % 2, 0:dst.shape[1]]

        @block.scalar
        def _(act):
            def split_hi(n, k, dst=None):
                act.wait_ge(w_in[k], (n - k) * 8 + 16)
                if not isinstance(n, int) or n < T_KEYS:
                    need(act, S["w_used"], n - 1)
                elif n >= T_WQ:
                    act.wait_ge(S["w_used"], n - 3)
                act.activation(w["hi"][:, k, :] if dst is None else dst, raw[:, k, :], ACT.Copy).then_inc(S["w_hi"], 1)

            act.wait_ge(S["lb_max"], 1)
            act.activation(lbw[:, 3:5], lbw[:, 1:3], ACT.Exp).then_inc(S["lb_exp"], 1)
            act.wait_ge(S["xt_in"], 16)
            act.activation(xsq[:], xt[:], ACT.Square).then_inc(S["xsq_ok"], 1)
            split_hi(0, 0)
            split_hi(1, 1)
            act.wait_ge(S["xsum_ok"], 1)
            act.activation(sd[:, META:LEN], ps[:, 4, :], ACT.Sqrt, bias=eps[:], scale=1.0 / D).then_inc(S["sd_ok"], 1)
            act.activation(sd[:, 0:META], ps[:, 5, 0:META], ACT.Sqrt, bias=eps[:], scale=1.0 / D).then_inc(S["sd_ok"], 1)
            for c in range(DC):
                act.wait_ge(S["yf_ok"], c + 1)
                act.activation(y["hi"][:, c, :], xt[:, c, :], ACT.Copy).then_inc(S["yhi_ok"], 1)
            def z_tiles(first, last, shift, dst, meta):
                with act.Fori(first // 2, last // 2, 1) as it:
                    for k in range(2):
                        own = bass.ds(it * 2 + (k - shift), 1)
                        act.wait_ge(S["w_used"], it * 2 + (k + 1))
                        if meta:
                            act.activation(znat[:, own, :], ps[0:META, 2 + k:3 + k, 0:P], ACT.Copy)
                            act.activation(dst[:, own, META:LEN], ps[:, k:k + 1, :], ACT.Copy).then_inc(S["z_out"], 1)
                        else:
                            act.activation(dst[:, own, :], ps[:, k:k + 1, :], ACT.Copy).then_inc(S["z_out"], 1)
                        split_hi(it * 2 + (k + 2), k)

            z_tiles(0, 4, 0, zm, True)
            act.wait_ge(S["mt_mm"], 1)
            act.activation(f_z[:, :, 0:META], ps[:, 4, 0:HH * META].rearrange("p (h t) -> p h t", h=HH),
                           ACT.Copy).then_inc(S["mt_out"], 1)
            act.wait_ge(S["mt_out"], 1)
            act.activation(f_z, f_z, ACT.Sigmoid).then_inc(S["f_sig"], 1)
            z_tiles(4, 8, 4, zr, False)
            z_tiles(8, 14, 4, zm, True)
            act.wait_ge(S["mt_mm"], 2)
            act.activation(ak_z[:, 0:META], ps[:, 5, 0:META], ACT.Copy).then_inc(S["mt_out"], 1)
            z_tiles(14, N_Z, 10, zr, False)

            def gate_out(t):
                act.wait_ge(S["w_used"], T_GATE + t + 1)
                act.activation(gates[:, t, :], ps[:, 2 + t % 2, :], ACT.Identity, bias=b_gate[:, t:t + 1]
                               ).then_inc(S["gate_out"], 1)
                split_hi(T_GATE + t + 2, t % 2)

            for n in range(1, 10, 2):
                act.wait_ge(S["tr_mm"], n + 1)
                act.activation(transposed_dst(n), transposed_src(n), ACT.Copy).then_inc(S["tr_out_s"], 1)
            act.wait_ge(S["hg_ok"], 1)
            act.activation(orstd[:], og_z, ACT.Sigmoid).then_inc(S["og_sig"], 1)
            for tt in range(TT):
                act.wait_ge(S["o_mm"], (tt + 1) * P // CH)
                act.activation(o_hg[:, :, tt * P:(tt + 1) * P], ps[:, tt % 2, :].rearrange("p (h t) -> p h t", h=HH),
                               ACT.Copy).then_inc(S["o_out"], 1)
                for t in gate_blocks_done(tt * P // CH * GATES_HG, (tt + 1) * P // CH * GATES_HG):
                    gate_out(t)
            act.wait_ge(S["o_out"], TT)
            act.activation(osq[:], o_hg[:], ACT.Square).then_inc(S["osq_ok"], 1)
            act.wait_ge(S["og_used"], 1)
            for h in range(HH):
                act.wait_ge(S["osum_mm"], h + 1)
                act.activation(orstd[:, h, :], ps[:, 4 + h % 2, :], ACT.Sqrt, bias=eps[:],
                               scale=1.0 / P).then_inc(S["osd_ok"], 1)

            def exponentials(n):
                s, lo = n % 2, P if n < AQ else 0
                act.wait_ge(S["amax"], n + 1)
                need(act, S["atr_mm"], n - 1)
                act.activation(atp[:, s, lo:KEYS + 1], atsc[:, s, lo:KEYS + 1], ACT.Exp, bias=atstat[:, 0, s:s + 1],
                               accum_out=atstat[:, 1, s:s + 1]).then_inc(S["aexp"], 1)

            def turned(n):
                s, lo = n % 2, P if n < AQ else 0
                act.wait_ge(S["atr_mm"], n + 1)
                need(act, S["apv_mm"], n - 1)
                act.activation(atpT[:, s, lo:BAND], ps[:, 4 + s, lo:BAND], ACT.Copy).then_inc(S["atr_out"], 1)
                act.activation(atpTm[:, s, :], ps[0:META, 4 + s, BAND:BAND + P], ACT.Copy).then_inc(S["atr_out"], 1)

            for n in range(TT * AQ + 1):
                if n >= 1:
                    for t in gate_blocks_done(GATES_AT0 + (n - 1) * GATES_AT, GATES_AT0 + n * GATES_AT):
                        gate_out(t)
                if n < TT * AQ:
                    exponentials(n)
                if n >= 1:
                    turned(n - 1)
                if n >= 1 and n % AQ == 0:
                    tt = n // AQ - 1
                    act.wait_ge(S["apv_mm"], n)
                    act.activation(oat["hi"][:, :, tt * P:(tt + 1) * P],
                                   ps[:, tt % 2, :].rearrange("p (c t) -> p c t", c=4), ACT.Copy).then_inc(S["oat_hi"], 1)
            for h in range(HH):
                act.wait_ge(S["ohg_f"], h + 1)
                act.activation(ohg["hi"][:, h, :], o_hg[:, h, :], ACT.Copy).then_inc(S["ohg_hi"], 1)
            act.wait_ge(S["gate_out"], N_GATE)
            for c in range(DC):
                act.activation(gates[:, c:N_GATE:DC, :], gates[:, c:N_GATE:DC, :], ACT.Sigmoid).then_inc(S["gate_sig"], 1)
            act.wait_ge(S["asc_mm"], TT * AQ)
            act.dma_start(acc[:], x.rearrange("(t p) d -> p t d", p=P)).then_inc(S["acc_in"], 16)
            for c in range(DC):
                split_hi(T_BRANCH + c + 2, c % 2)
                act.wait_ge(S["br_f"], c + 1)
                act.activation(m["hi"][:, c, :], mtmp[:, c % 2, 0, :], ACT.Copy).then_inc(S["m_hi"], 1)
            for c in range(DC):
                n = T_OUT + c + 2
                half = slice((n - T_KEYS) * RH, (n - T_KEYS + 1) * RH)
                split_hi(n, c % 2, None if n < T_KEYS else keys["hi"][:, half, :].rearrange("p r n -> p (r n)"))
            for tt in range(TT):
                act.wait_ge(S["acc_ok"], 2 * tt + 2)
                need(act, S["ss_ok"], tt - 1)
                act.activation(ysq[:, tt % 2, :], acc[:, tt, :], ACT.Square,
                               accum_out=rowstat[:, 0, tt:tt + 1]).then_inc(S["ss_ok"], 1)
            act.wait_ge(S["ss_ok"], TT)
            act.activation(rowstat[:, 1, :], rowstat[:, 0, :], ACT.Sqrt, bias=eps[:], scale=1.0 / D).then_inc(S["ysd_ok"], 1)
            split_hi(T_WQ, 0)
            split_hi(T_WQ + 1, 1)
            for c in range(DC):
                act.wait_ge(S["ht_mm"], c + 1)
                act.activation(hT["hi"][:, c, :], ps[:, c % 2, :], ACT.Copy, scale=ffn_g[:, c:c + 1]).then_inc(S["ht_hi"], 1)
            for n in range(RS + 1):
                if n < RS:
                    act.wait_ge(S["w_used"], T_KEYS + n + 1)
                    need(act, S["s_mm"], n - 1)
                    act.activation(q2["hi"][:, n % 2, :], ps[:, n % 2, :], ACT.Copy).then_inc(S["q_hi"], 1)
                    if T_WQ + n + 2 < N_TILES:
                        split_hi(T_WQ + n + 2, n % 2)
                if n >= 1:
                    act.wait_ge(S["s_mm"], n)
                    need(act, S["s_used"], n - 2)
                    act.activation(score[:, (n - 1) % 2], ps[:, 2 + (n - 1) % 2, :].rearrange("p (t n) -> p t n", t=TT),
                                   ACT.Copy).then_inc(S["s_out"], 1)
            def u_split(n, k):
                act.wait_ge(u_in[k], (n - k) * 8 + 16)
                need(act, S["u_mm"], n - 1)
                act.activation(uw["hi"][:, k, :], uraw[:, k, :], ACT.Copy).then_inc(S["u_hi"], 1)

            def early_gelu(n):
                g, b = n // GRP, n % GRP
                act.wait_ge(S["u_mm"], n + 1)
                if g >= 2 and b == 0:
                    act.wait_ge(early_out[g % 2], g // 2 * 16)
                act.activation(early[:, g % 2, b, :], ps[:, n % 2, :], ACT.Gelu).then_inc(S["gelu_ok"], 1)

            def spill(g):
                act.wait_ge(S["gelu_ok"], (g + 1) * GRP)
                act.dma_start(early_dram[g], early[:, g % 2].rearrange("p b t -> p (b t)")).then_inc(early_out[g % 2], 16)

            u_split(0, 0)
            u_split(1, 1)
            for n in range(NTOP):
                u_split(n + 2, n % 2)
                early_gelu(n)
                if n % GRP == GRP - 1:
                    spill(n // GRP)
                if n == NTOP - 3:
                    act.wait_ge(S["soft"], 1)
                    act.activation(gate[:], best[:], ACT.Exp).then_inc(S["soft_exp"], 1)

            def pieces(it):
                for c in range(2):
                    if not (isinstance(it, int) and it * 2 + c == 0):
                        k = 1 - c
                        act.wait_ge(S["u_mm"], it * 2 + (NTOP + c))
                        act.activation(early[:].rearrange("p s b t -> p (s b) t")[:, bass.ds(it * 2 + (c - 1), 1), :],
                                       ps[:, k:k + 1, :], ACT.Gelu).then_inc(S["gelu_ok"], 1)
                        act.wait_ge(u_in[k], it * 16 + (NTOP + 2 * c) * 8 + 16)
                        act.activation(uw["hi"][:, k, :], uraw[:, k, :], ACT.Copy).then_inc(S["u_hi"], 1)
                    for q in range(GT // 4):
                        act.wait_ge(S["g_mm"], it * (2 * GT // 4) + (c * (GT // 4) + q + 1))
                        if q == 0:
                            need(act, g_store[c], it * 16)
                        act.activation(piece[:, c, :, q * 4:q * 4 + 4].rearrange("p i t -> p t i"),
                                       ps[:, 4 + q % 4, :].rearrange("p (t i) -> p t i", t=4), ACT.Copy).then_inc(S["g_out"], 1)

            for k in range(2):
                act.wait_ge(early_out[k], EARLY_TOP // 2 * 16)
            pieces(0)
            with act.Fori(1, NPIECE // 2 - 1, 1) as it:
                pieces(it)
            spill(EARLY_TOP)
            pieces(NPIECE // 2 - 1)
            early_gelu(NLAST - 1)
            u_split(NLAST + 1, 1)

            def early_block(it, s, b):
                n = it * 2 * GRP + (s * GRP + b)
                if b == 0:
                    act.wait_ge(S["v_in"], it * 32 + (s * 16 + 16))
                need(act, S["early_mm"], it * 2 * GRP + (s * GRP + b - GRP + 1))
                act.activation(vw["hi"][:, b, :], vraw[:, b, :], ACT.Copy).then_inc(S["v_hi"], 1)
                act.wait_ge(S["prod_ok"], n + 1)
                act.activation(act_w["hi"][:, s, b, :], prod[:, b % 2, :], ACT.Copy).then_inc(S["aw_hi"], 1)

            for n in range(NLAST, NEARLY):
                if n < NEARLY - 1:
                    act.wait_ge(S["u_lo"], n + 2)
                    act.dma_start(uraw[:, (n + 3) % 2, :], uT[n + 3]).then_inc(u_in[(n + 3) % 2], 16)
                if n == NLAST:
                    spill(SPILLED - 1)
                if n >= NEARLY - GRP:
                    if n == NEARLY - GRP:
                        for k in range(2):
                            act.wait_ge(g_store[k], 16 * NPIECE // 2)
                    early_block(0, 0, n - (NEARLY - GRP))
                u_split(n + 2, n % 2)
                early_gelu(n)

            def v_split(g, b):
                if b == 0:
                    act.wait_ge(S["v_in"], g * 16 + 16)
                    act.wait_ge(S["o2_mm"], g * 8 - 8 * (EARLY - 1))
                act.activation(vw["hi"][:, b, :], vraw[:, b, :], ACT.Copy).then_inc(S["v_hi"], 1)

            def period(g, s, more_u=True, first=False):
                for b in range(GRP):
                    n = g * GRP + b
                    for vb in V_SPLITS[b] if not first else ():
                        v_split(g - 1, vb)
                    if more_u or b < 2:
                        u_split(n + 2, b % 2)
                    act.wait_ge(S["u_mm"], n + 1)
                    need(act, S["prod_ok"], n - 1)
                    act.activation(gelu[:, b % 2, :], ps[:, b % 2, :], ACT.Gelu).then_inc(S["gelu_ok"], 1)
                    act.wait_ge(S["prod_ok"], n + 1)
                    if b == 0:
                        need(act, S["o2_mm"], g * 8 - 8 * EARLY)
                    act.activation(act_w["hi"][:, s, b, :], prod[:, b % 2, :], ACT.Copy).then_inc(S["aw_hi"], 1)

            for b in range(GRP):
                early_block(0, 1, b)
            with act.Fori(1, EARLY // 2, 1) as it:
                for s in range(2):
                    for b in range(GRP):
                        early_block(it, s, b)
            act.wait_ge(S["early_mm"], NEARLY - GRP)
            period(EARLY, 0, first=True)
            period(EARLY + 1, 1)
            with act.Fori(EARLY // 2 + 1, NGRP // 2 - 1, 1) as it:
                period(it * 2, 0)
                period(it * 2 + 1, 1)
            period(NGRP - 2, 0)
            period(NGRP - 1, 1, more_u=False)
            for b in range(GRP):
                v_split(NGRP - 1, b)
            for tt in range(TT):
                act.wait_ge(S["o2_out"], (NGRP - EARLY) * 8 + 2 * tt + 2)
                need(act, S["fss_ok"], tt)
                act.activation(gelu[:].rearrange("p s t -> p (s t)"), acc[:, tt, :], ACT.Square,
                               accum_out=rowstat[:, 0, tt:tt + 1]).then_inc(S["fss_ok"], 1)
            act.wait_ge(S["fss_ok"], TT)
            act.activation(rowstat[:, 1, :], rowstat[:, 0, :], ACT.Sqrt, bias=eps[:], scale=1.0 / D).then_inc(S["fsd_ok"], 1)

        @block.vector
        def _(dve):
            chain = Chain(dve, vec)
            dve.wait_ge(S["par_in"], 32)
            chain.done(dve.tensor_tensor(lbw[:, 0], lb_logits[:, 0], lb_logits[:, 1], ALU.max))
            for r in range(2):
                ins = dve.tensor_tensor(lbw[:, 1 + r], lb_logits[:, r], lbw[:, 0], ALU.subtract)
            ins.then_inc(S["lb_max"], 1)
            dve.wait_ge(S["lb_exp"], 1)
            chain.done(dve.tensor_tensor(lbw[:, 1], lbw[:, 3], lbw[:, 4], ALU.add))
            chain.done(dve.reciprocal(lbw[:, 2], lbw[:, 1]))
            chain.done(dve.tensor_tensor(lbw[:, 0], lbw[:, 3], lbw[:, 2], ALU.mult))
            chain.done(dve.tensor_scalar(lbw[:, 5], lbw[:, 0], -1.0, 1.0, ALU.mult, ALU.add))
            dve.wait_ge(S["sd_ok"], 2)
            chain.done(dve.reciprocal(rstd[:], sd[:]))
            for c in range(DC):
                dve.scalar_tensor_tensor(out=xt[:, c, :], in0=xt[:, c, :], scalar=mix_g[:, c:c + 1], in1=rstd[:],
                                         op0=ALU.mult, op1=ALU.mult).then_inc(S["yf_ok"], 1)
            for c in range(DC):
                dve.wait_ge(S["yhi_ok"], c + 1)
                dve.tensor_tensor(y["lo"][:, c, :], xt[:, c, :], y["hi"][:, c, :].bitcast(F32),
                                  ALU.subtract).then_inc(S["y_ok"], 1)
            dve.wait_ge(S["f_sig"], 1)
            for h in range(HH):
                ins = dve.tensor_scalar(f_z[:, h, :], f_z[:, h, :], lbw[:, 5, h:h + 1], lbw[:, 0, h:h + 1],
                                        ALU.mult, ALU.add)
            chain.done(ins)
            chain.done(dve.tensor_scalar(kk[:], f_z, -1.0, 1.0, ALU.mult, ALU.add))
            halves = lambda ap: ap.rearrange("p h (b i) -> p (h b) i", i=HALF)
            flat = lambda ap: ap.rearrange("p h l -> p (h l)")
            chain.done(dve.memset(starts[:], 0.0))
            chain.done(dve.tensor_copy(halves(starts[:])[:, :, 0:1], halves(f_z)[:, :, 0:1]))
            chain.done(dve.memset(halves(f_z)[:, :, 0:1], 0.0))
            chain.done(dve.tensor_tensor_scan(flat(decay[:]), flat(f_z), flat(starts[:]), 0.0, ALU.mult, ALU.add))
            chain.done(dve.tensor_scalar(decay[:], decay[:], TINY, None, ALU.max))
            chain.done(dve.reciprocal(inv[:], decay[:]))
            chunks = lambda ap: ap.rearrange("p (c i) -> p c i", i=CH)
            at_mid = lambda ap: chunks(ap)[:, :, HALF - 1:HALF].to_broadcast([P, NCH, HALF])
            dve.wait_ge(S["z_out"], 8)
            chain.done(dve.tensor_tensor(q_z, q_z, decay[:, :, META:LEN], ALU.mult))
            for h in range(HH):
                part = chunks(q_z[:, h, :])[:, :, 0:HALF]
                ins = dve.tensor_tensor(part, part, at_mid(inv[:, h, META:LEN]), ALU.mult)
            chain.done(ins)
            chain.done(dve.tensor_tensor(kk[:], kk[:], inv[:], ALU.mult))
            for h in range(HH):
                part = chunks(kk[:, h, META:LEN])[:, :, 0:HALF]
                ins = dve.tensor_tensor(part, part, at_mid(decay[:, h, META:LEN]), ALU.mult)
            chain.done(ins)
            for h in range(HH):
                ends = decay[:, h, :].rearrange("p (b i) -> p b i", i=HALF)[:, :, HALF - 1]
                ins = dve.tensor_tensor(ecol[:, h, :], ends[:, 0:NBLK - 1:2], ends[:, 1:NBLK:2], ALU.mult)
            chain.done(ins)
            for h in range(HH):
                ins = dve.tensor_tensor(chunks(qi[:, h, :]), chunks(q_z[:, h, :]),
                                        ecol[:, h, :].unsqueeze(2).to_broadcast([P, NCH, CH]), ALU.mult)
            ins.then_inc(S["hg_ok"], 1)
            for n in range(0, 10, 2):
                dve.wait_ge(S["tr_mm"], n + 1)
                dve.tensor_copy(transposed_dst(n), transposed_src(n)).then_inc(S["tr_out_v"], 1)
            dve.wait_ge(S["upd_mm"], 1)
            dve.tensor_copy(state[:, 0, :], ps[:, 4, :]).then_inc(S["state_ok"], 1)
            for c in range(NCH):
                if c * CH % P == 0:
                    tt = c * CH // P
                    dve.wait_ge(S["wsc_mm"], tt + 1)
                    need(dve, S["o_mm"], (tt - 1) * P // CH)
                    for r in range(P // CH):
                        own = slice(r * CH, (r + 1) * CH)
                        ins = dve.tensor_tensor(within[own, tt % 2, :, own],
                                                ps[own, 6 + tt % 2, 0:HH * CH].rearrange("p (h t) -> p h t", h=HH),
                                                chunkmask[own].unsqueeze(1).to_broadcast([CH, HH, CH]), ALU.mult)
                    ins.then_inc(S["within_ok"], 1)
                if c < NCH - 1:
                    dve.wait_ge(S["upd_mm"], c + 2)
                    dve.wait_ge(S["state_ok"], c + 1)
                    need(dve, S["o_mm"], c - 2)
                    for h in range(HH):
                        head = slice(h * P, (h + 1) * P)
                        ins = dve.scalar_tensor_tensor(out=state[:, (c + 1) % 4, head], in0=state[:, c % 4, head],
                                                       scalar=ecol[:, h, c:c + 1], in1=ps[:, 4 + (c + 1) % 2, head],
                                                       op0=ALU.mult, op1=ALU.add)
                    ins.then_inc(S["state_ok"], 1)
            dve.wait_ge(S["og_sig"], 1)
            for h in range(HH):
                ins = dve.scalar_tensor_tensor(out=og_z[:, h, :], in0=og_z[:, h, :], scalar=hg_g[:, h:h + 1],
                                               in1=orstd[:, h, :], op0=ALU.mult, op1=ALU.mult)
            ins.then_inc(S["og_used"], 1)
            dve.wait_ge(S["og_used"], 1)
            dve.wait_ge(S["o_out"], TT)
            chain.done(dve.tensor_tensor(og_z, og_z, o_hg[:], ALU.mult))

            def logits(n):
                s, lo = n % 2, P if n < AQ else 0
                dve.wait_ge(S["asc_mm"], n + 1)
                need(dve, S["aexp"], n - 1)
                head = n % 2 * 4 + n % AQ // 2
                dve.tensor_copy(atsc[:, s, KEYS:KEYS + 1], sink[:, head:head + 1])
                chain.done(dve.scalar_tensor_tensor(out=atsc[:, s, lo:KEYS], in0=ps[:, 6 + s, lo:KEYS],
                                                    scalar=HD ** -0.5, in1=bandmask[:, lo:KEYS],
                                                    op0=ALU.mult, op1=ALU.add))
                dve.tensor_reduce(atstat[:, 0, s:s + 1], atsc[:, s, lo:KEYS + 1], AX_X, ALU.max,
                                  negate=True).then_inc(S["amax"], 1)

            def normalise(n):
                s, lo = n % 2, P if n < AQ else 0
                dve.wait_ge(S["aexp"], n + 1)
                chain.done(dve.reciprocal(atstat[:, 2, s:s + 1], atstat[:, 1, s:s + 1]))
                dve.tensor_scalar(atp[:, s, lo:KEYS], atp[:, s, lo:KEYS], atstat[:, 2, s:s + 1], None,
                                  ALU.mult).then_inc(S["anorm"], 1)

            def attention_lo(tt):
                own = slice(tt * P, (tt + 1) * P)
                dve.wait_ge(S["oat_hi"], tt + 1)
                dve.tensor_tensor(oat["lo"][:, :, own], ps[:, tt % 2, :].rearrange("p (c t) -> p c t", c=4),
                                  oat["hi"][:, :, own].bitcast(F32), ALU.subtract).then_inc(S["oat_ok"], 1)

            dve.wait_ge(S["consts"], 1)
            for n in range(TT * AQ + 1):
                if n >= 1:
                    normalise(n - 1)
                if n < TT * AQ:
                    logits(n)
                if n in (4, 8, 12, 16):
                    h = n // 4 - 1
                    dve.wait_ge(S["osd_ok"], h + 1)
                    chain.done(dve.reciprocal(orstd[:, h, :], orstd[:, h, :]))
                    dve.tensor_tensor(o_hg[:, h, :], og_z[:, h, :], orstd[:, h, :], ALU.mult).then_inc(S["ohg_f"], 1)
                if n > AQ and n % AQ == 2:
                    attention_lo(n // AQ - 1)
            attention_lo(TT - 1)
            for h in range(HH):
                dve.wait_ge(S["ohg_hi"], h + 1)
                dve.tensor_tensor(ohg["lo"][:, h, :], o_hg[:, h, :], ohg["hi"][:, h, :].bitcast(F32),
                                  ALU.subtract).then_inc(S["ohg_ok"], 1)

            dve.wait_ge(S["ohg_ok"], HH)
            for c in range(DC):
                s = c % 2
                dve.wait_ge(S["w_used"], T_BRANCH + c + 1)
                need(dve, S["m_ok"], c - 1)
                dve.wait_ge(S["gate_sig"], c + 1)
                dve.tensor_tensor(mtmp[:, s, 0, :], gates[:, c, :], ps[:, 2 * s, :], ALU.mult)
                chain.done(dve.tensor_tensor(mtmp[:, s, 1, :], gates[:, DC + c, :], ps[:, 2 * s + 1, :], ALU.mult))
                dve.tensor_tensor(mtmp[:, s, 0, :], mtmp[:, s, 0, :], mtmp[:, s, 1, :], ALU.add).then_inc(S["br_f"], 1)
                dve.wait_ge(S["m_hi"], c + 1)
                dve.tensor_tensor(m["lo"][:, c, :], mtmp[:, s, 0, :], m["hi"][:, c, :].bitcast(F32),
                                  ALU.subtract).then_inc(S["m_ok"], 1)
            dve.wait_ge(S["acc_in"], 16)
            dve.wait_ge(S["w_used"], T_OUT + DC)
            for n in range(2 * TT):
                own = acc[:, n // 2, n % 2 * 512:(n % 2 + 1) * 512]
                dve.tensor_tensor(own, own, ps[:, n, :], ALU.add).then_inc(S["acc_ok"], 1)
            dve.wait_ge(S["ysd_ok"], 1)
            chain.done(dve.reciprocal(rowstat[:, 2, :], rowstat[:, 1, :]))
            for tt in range(TT):
                dve.tensor_scalar(ynat[:, tt, :], acc[:, tt, :], rowstat[:, 2, tt:tt + 1], None,
                                  ALU.mult).then_inc(S["ynat_ok"], 1)
            for c in range(DC):
                dve.wait_ge(S["ht_hi"], c + 1)
                dve.scalar_tensor_tensor(out=hT["lo"][:, c, :], in0=ps[:, c % 2, :], scalar=ffn_g[:, c:c + 1],
                                         in1=hT["hi"][:, c, :].bitcast(F32), op0=ALU.mult, op1=ALU.subtract
                                         ).then_inc(S["ht_ok"], 1)

            def set_tops(n):
                s = n % 2
                dve.wait_ge(S["s_out"], n + 1)
                for tt in range(TT):
                    ins = dve.max(top_v[:, tt, n, 0:8], score[:, s, tt, :])
                chain.done(ins)
                for tt in range(TT):
                    dve.max_index(top_i[:, tt, n, 0:8], top_v[:, tt, n, 0:8], score[:, s, tt, :])
                for tt in range(TT):
                    ins = dve.match_replace(scut[:, s, tt, :], top_v[:, tt, n, 0:8], score[:, s, tt, :], LOWEST)
                ins.then_inc(S["s_used"], 1)
                dve.wait_ge(S["s_used"], n + 1)
                for tt in range(TT):
                    ins = dve.max(top_v[:, tt, n, 8:16], scut[:, s, tt, :])
                chain.done(ins)
                for tt in range(TT):
                    ins = dve.max_index(top_i[:, tt, n, 8:16], top_v[:, tt, n, 8:16], scut[:, s, tt, :])
                chain.done(ins)

            for n in range(RS + 1):
                if n < RS:
                    dve.wait_ge(S["q_hi"], n + 1)
                    dve.tensor_tensor(q2["lo"][:, n % 2, :], ps[:, n % 2, :], q2["hi"][:, n % 2, :].bitcast(F32),
                                      ALU.subtract).then_inc(S["q_ok"], 1)
                if n >= 1:
                    set_tops(n - 1)
            tv = top_v[:].rearrange("p t (h c) a -> p (t h) c a", c=2)
            a = 0
            while a < TOP:
                same = PAIRS.count(PAIRS[a])
                wide = PAIRS[a]
                dst = cand[:, :, STARTS[a]:STARTS[a] + same * wide].rearrange("p n (a b) -> p n a b", b=wide)
                ins = dve.tensor_tensor(dst, tv[:, :, 0, a:a + same].unsqueeze(3).to_broadcast([P, TT * RH, same, wide]),
                                        tv[:, :, 1, 0:wide].unsqueeze(2).to_broadcast([P, TT * RH, same, wide]), ALU.add)
                a += same
            chain.done(ins)
            bests = best[:].rearrange("p t h k -> p (t h) k")
            for n in range(TT * RH):
                ins = dve.max(bests[:, n, 0:8], cand[:, n, :])
            chain.done(ins)
            for n in range(TT * RH):
                dve.max_index(pos_u[:, n, 0:8], bests[:, n, 0:8], cand[:, n, :])
            for n in range(TT * RH):
                ins = dve.match_replace(ccut[:, n, :], bests[:, n, 0:8], cand[:, n, :], LOWEST)
            chain.done(ins)
            for n in range(TT * RH):
                ins = dve.max(bests[:, n, 8:16], ccut[:, n, :])
            chain.done(ins)
            for n in range(TT * RH):
                ins = dve.max_index(pos_u[:, n, 8:16], bests[:, n, 8:16], ccut[:, n, :])
            chain.done(ins)
            dve.tensor_copy(top_f[:], top_i[:])
            chain.done(dve.tensor_copy(pos[:].rearrange("p t h k -> p (t h) k"), pos_u[:]))
            dve.tensor_copy(step_f[:, :, :, 0:1], top_f[:, :, :, 0:1])
            dve.tensor_tensor(step_f[:, :, :, 1:TOP], top_f[:, :, :, 1:TOP], top_f[:, :, :, 0:TOP - 1],
                              ALU.subtract).then_inc(S["pos_ok"], 1)
            chain.done(dve.tensor_copy(tot[:, 0, :], bests[:, :, 0]))
            dve.tensor_tensor(bests, bests, tot[:, 0, :].unsqueeze(2).to_broadcast([P, TT * RH, TOP]),
                              ALU.subtract).then_inc(S["soft"], 1)
            dve.wait_ge(S["pos_ok"], 1)
            chain.done(dve.tensor_copy(posb[:], pos[:]))
            for a in range(1, TOP):
                chain.done(dve.tensor_scalar(tmp_j[:], pos[:], float(STARTS[a]), float(PAIRS[a - 1]), ALU.is_ge, ALU.mult))
                chain.done(dve.tensor_tensor(posb[:], posb[:], tmp_j[:], ALU.subtract))
            chain.done(dve.tensor_copy(ej[:], key_step(1, 0)))
            for b in range(1, TOP):
                chain.done(dve.scalar_tensor_tensor(out=tmp_j[:], in0=posb[:], scalar=float(b), in1=key_step(1, b),
                                                    op0=ALU.is_ge, op1=ALU.mult))
                chain.done(dve.tensor_tensor(ej[:], ej[:], tmp_j[:], ALU.add))
            chain.done(dve.scalar_tensor_tensor(out=ei_high[:], in0=pos[:], scalar=float(STARTS[EI_POOL]),
                                                in1=key_step(0, EI_POOL), op0=ALU.is_ge, op1=ALU.mult))
            for a in range(EI_POOL + 1, TOP):
                chain.done(dve.scalar_tensor_tensor(out=tmp_j[:], in0=pos[:], scalar=float(STARTS[a]), in1=key_step(0, a),
                                                    op0=ALU.is_ge, op1=ALU.mult))
                chain.done(dve.tensor_tensor(ei_high[:], ei_high[:], tmp_j[:], ALU.add))
            dve.wait_ge(S["ei_ok"], 1)
            dve.tensor_tensor(ei[:], ei[:], ei_high[:], ALU.add).then_inc(S["ei_ok"], 1)
            dve.wait_ge(S["soft_exp"], 1)
            gs = gate[:].rearrange("p t h k -> p (t h) k")
            chain.done(dve.tensor_reduce(tot[:, 0, :], gs, AX_X, ALU.add))
            chain.done(dve.reciprocal(tot[:, 1, :], tot[:, 0, :]))
            dve.tensor_tensor(gs, gs, tot[:, 1, :].unsqueeze(2).to_broadcast([P, TT * RH, TOP]),
                              ALU.mult).then_inc(S["gate_ok"], 1)
            for q in range(3):
                dve.wait_ge(S["col_mm"], q + 1)
                dve.tensor_copy(cols[:, q, :], ps[:, 4 + q, :]).then_inc(S["col_ok"], 1)

            def one_hot(it):
                for s in range(4):
                    n = it * 4 + s
                    own = bass.ds(n * BATCH, BATCH)
                    spread = lambda q: cols[:, q, own].unsqueeze(2).to_broadcast([P, BATCH, NK])
                    every = iota[:].unsqueeze(1).to_broadcast([P, BATCH, NK])
                    need(dve, S["hotg_ok"], it * 4 + (s - 1))
                    dve.tensor_tensor(hot_j[:, s % 2], every, spread(1), ALU.is_equal).then_inc(S["hotj_ok"], 1)
                    need(dve, S["g_mm"], it * 8 + (2 * s - 2))
                    dve.tensor_tensor(hot_i[:, s % 2], every, spread(0), ALU.is_equal).then_inc(S["hoti_ok"], 1)

            dve.wait_ge(S["col_ok"], 3)
            one_hot(0)
            with dve.Fori(1, TOK // BATCH // 4, 1) as it:
                one_hot(it)

            def u_split(n, k):
                dve.wait_ge(S["u_hi"], n + 1)
                dve.tensor_tensor(uw["lo"][:, k, :], uraw[:, k, :], uw["hi"][:, k, :].bitcast(F32),
                                  ALU.subtract).then_inc(S["u_lo"], 1)

            def v_split(g, b):
                dve.wait_ge(S["v_hi"], g * GRP + (b + 1))
                dve.tensor_tensor(vw["lo"][:, b, :], vraw[:, b, :], vw["hi"][:, b, :].bitcast(F32),
                                  ALU.subtract).then_inc(S["v_lo"], 1)

            def group(g, s, more_u=True, first=False):
                for b in range(GRP):
                    n = g * GRP + b
                    for vb in V_SPLITS[b] if not first else ():
                        v_split(g - 1, vb)
                    if more_u or b < 2:
                        u_split(n + 2, b % 2)
                    if b == 0:
                        dve.wait_ge(gm_in[s], g * 8 + (16 - 8 * s))
                    dve.wait_ge(S["gelu_ok"], n + 1)
                    need(dve, S["aw_ok"], n - 1)
                    dve.tensor_tensor(prod[:, b % 2, :].rearrange("p (c t) -> p c t", c=NPIECE),
                                      gelu[:, b % 2, :].rearrange("p (c t) -> p c t", c=NPIECE),
                                      gmat[:, s, :, b, :], ALU.mult).then_inc(S["prod_ok"], 1)
                    dve.wait_ge(S["aw_hi"], n + 1)
                    dve.tensor_tensor(act_w["lo"][:, s, b, :], prod[:, b % 2, :], act_w["hi"][:, s, b, :].bitcast(F32),
                                      ALU.subtract).then_inc(S["aw_ok"], 1)

            def add_up(g):
                for j in range(8):
                    own = acc[:, j // 2, j % 2 * 512:(j % 2 + 1) * 512]
                    dve.wait_ge(S["o2_mm"], g * 8 + (j + 1 - 8 * (EARLY - 1)))
                    dve.tensor_tensor(own, own, ps[:, 2 + j % 4, :], ALU.add).then_inc(S["o2_out"], 1)

            def early_groups(it):
                for s in range(2):
                    for b in range(GRP):
                        n = it * 2 * GRP + (s * GRP + b)
                        dve.wait_ge(S["v_hi"], n + 1)
                        dve.tensor_tensor(vw["lo"][:, b, :], vraw[:, b, :], vw["hi"][:, b, :].bitcast(F32),
                                          ALU.subtract).then_inc(S["v_lo"], 1)
                        if b == 0:
                            dve.wait_ge(gm_in[s], it * 16 + 16)
                            if isinstance(it, int):
                                dve.wait_ge(S["gelu_ok"], NLAST + (s + 1) * GRP)
                            else:
                                dve.wait_ge(S["early_in"], it * 32 + (s - 1) * 16)
                        need(dve, S["aw_ok"], it * 2 * GRP + (s * GRP + b - 1))
                        dve.tensor_tensor(prod[:, b % 2, :].rearrange("p (c t) -> p c t", c=NPIECE),
                                          early[:, s, b, :].rearrange("p (c t) -> p c t", c=NPIECE),
                                          gmat[:, s, :, b, :], ALU.mult).then_inc(S["prod_ok"], 1)
                        dve.wait_ge(S["aw_hi"], n + 1)
                        dve.tensor_tensor(act_w["lo"][:, s, b, :], prod[:, b % 2, :],
                                          act_w["hi"][:, s, b, :].bitcast(F32), ALU.subtract).then_inc(S["aw_ok"], 1)

            early_groups(0)
            with dve.Fori(1, EARLY // 2, 1) as it:
                early_groups(it)
            dve.wait_ge(S["u_lo"], NEARLY + 2)
            for j in range(8):
                own = acc[:, j // 2, j % 2 * 512:(j % 2 + 1) * 512]
                dve.wait_ge(S["o2_mm"], j + 1)
                dve.tensor_tensor(own, own, ps[:, j, :], ALU.add).then_inc(S["o2_out"], 1)
            group(EARLY, 0, first=True)
            with dve.Fori(EARLY // 2, NGRP // 2 - 1, 1) as it:
                group(it * 2 + 1, 1)
                add_up(it * 2)
                group(it * 2 + 2, 0)
                add_up(it * 2 + 1)
            group(NGRP - 1, 1, more_u=False)
            for b in range(GRP):
                if b == 0:
                    add_up(NGRP - 2)
                v_split(NGRP - 1, b)
            add_up(NGRP - 1)
            dve.wait_ge(S["fsd_ok"], 1)
            dve.wait_ge(S["fin_in"], 16)
            chain.done(dve.reciprocal(rowstat[:, 2, :], rowstat[:, 1, :]))
            for tt in range(TT):
                dve.scalar_tensor_tensor(out=fin_o[:, tt, :], in0=acc[:, tt, :], scalar=rowstat[:, 2, tt:tt + 1],
                                         in1=fin_g[:], op0=ALU.mult, op1=ALU.mult).then_inc(S["fin_ok"], 1)

        @block.tensor
        def _(pe):
            def three(dst, lhs, rhs, first, last):
                for i, (a, b) in enumerate(SPLIT):
                    ins = pe.matmul(dst, lhs[a], rhs[b], start=first and i == 0, stop=last and i == 2)
                return ins

            def parts(t, *index):
                return {k: t[k].__getitem__((slice(None),) + index) for k in t}

            def project(k, rhs, dst):
                for c in range(DC):
                    own = parts(rhs, c, slice(META, LEN)) if rhs is y else parts(rhs, c)
                    ins = three(dst, parts(w, k, slice(c * P, (c + 1) * P)), own, c == 0, c == DC - 1)
                return ins

            pe.wait_ge(S["consts"], 1)
            pe.wait_ge(S["xsq_ok"], 1)
            for c in range(DC):
                pe.matmul(ps[:, 4, :], ones[:], xsq[:, c, META:LEN], start=c == 0, stop=c == DC - 1)
            for c in range(DC):
                ins = pe.matmul(ps[:, 5, 0:META], ones[:], xsq[:, c, 0:META], start=c == 0, stop=c == DC - 1)
            ins.then_inc(S["xsum_ok"], 1)
            pe.wait_ge(S["y_ok"], DC)

            def z_pair(it, meta):
                for k in range(2):
                    pe.wait_ge(S["w_lo"], it * 2 + (k + 1))
                    need(pe, S["z_out"], it * 2 + (k - 1))
                    ins = project(k, y, ps[:, k, :])
                    if meta:
                        for c in range(DC):
                            ins = three(ps[0:META, 2 + k, 0:P], parts(y, c, slice(0, META)),
                                        parts(w, k, slice(c * P, (c + 1) * P)), c == 0, c == DC - 1)
                    ins.then_inc(S["w_used"], 1)

            def turn_meta(blocks, bank):
                for q, n in enumerate(blocks):
                    ins = pe.transpose(ps[:, bank, q * META:(q + 1) * META], znat[:, n, :], ident[0:META, 0:META])
                ins.then_inc(S["mt_mm"], 1)

            z_pair(0, True)
            z_pair(1, True)
            pe.wait_ge(S["z_out"], 4)
            turn_meta(range(4), 4)
            with pe.Fori(2, 4, 1) as it:
                z_pair(it, False)
            with pe.Fori(4, 7, 1) as it:
                z_pair(it, True)
            pe.wait_ge(S["z_out"], 14)
            turn_meta([8], 5)
            with pe.Fori(7, N_Z // 2, 1) as it:
                z_pair(it, False)

            def gate_products(first, last):
                for i in range(first, last):
                    t, c, (a, b) = i // (3 * DC), i // 3 % DC, SPLIT[i % 3]
                    if i % (3 * DC) == 0:
                        pe.wait_ge(S["w_lo"], T_GATE + t + 1)
                        need(pe, S["gate_out"], t - 1)
                    ins = pe.matmul(ps[:, 2 + t % 2, :], w[a][:, t % 2, c * P:(c + 1) * P], y[b][:, c, META:LEN],
                                    start=i % (3 * DC) == 0, stop=(i + 1) % (3 * DC) == 0)
                    if (i + 1) % (3 * DC) == 0:
                        ins.then_inc(S["w_used"], 1)

            pe.wait_ge(S["z_out"], N_Z)
            for n in range(10):
                need(pe, S["tr_out_s" if n % 2 else "tr_out_v"], n // 2)
                if n == 5:
                    pe.wait_ge(S["hg_ok"], 1)
                tile = lambda tt: slice(META + tt * P, META + (tt + 1) * P)
                if n < 4:
                    srcs = [v_z[:, h, tile(n)] for h in range(HH)]
                elif n == 4:
                    srcs = [av_z[:, tile(tt)] for tt in range(TT)]
                else:
                    srcs = [kk[:, h, tile(n - 5) if n < 9 else slice(0, META)] for h in range(HH)]
                rows = P if n < 9 else META
                for q, src in enumerate(srcs):
                    ins = pe.transpose(ps[0:rows, 2 + n % 2, q * P:(q + 1) * P], src, ident[:])
                ins.then_inc(S["tr_mm"], 1)
            for k in ("tr_out_v", "tr_out_s"):
                pe.wait_ge(S[k], 5)

            def chunk(c):
                return slice(c * CH, (c + 1) * CH)

            def rows(c):
                return slice(c * CH % P, c * CH % P + CH)

            def update(j):
                need(pe, S["state_ok"], j - 1)
                for h in range(HH):
                    head = slice(h * P, (h + 1) * P)
                    if j == 0:
                        k_, v_ = kmeta[:, head], vmeta[:, head]
                    else:
                        k_, v_ = (t[rows(j - 1), (j - 1) * CH // P, head] for t in (knat, vnat))
                    ins = pe.matmul(ps[:, 4 + j % 2, head], k_, v_, start=True, stop=True)
                ins.then_inc(S["upd_mm"], 1)

            update(0)
            for c in range(NCH):
                tt = c * CH // P
                if c * CH % P == 0:
                    need(pe, S["within_ok"], tt - 1)
                    for cc in range(c, c + P // CH):
                        for h in range(HH):
                            ins = pe.matmul(ps[rows(cc), 6 + tt % 2, h * CH:(h + 1) * CH],
                                            kk[:, h, META + cc * CH:META + (cc + 1) * CH], q_z[:, h, chunk(cc)],
                                            start=True, stop=True)
                    ins.then_inc(S["wsc_mm"], 1)
                if c < NCH - 1:
                    update(c + 1)
                if c * CH % P == 0:
                    pe.wait_ge(S["within_ok"], tt + 1)
                    need(pe, S["o_out"], tt - 1)
                    for h in range(HH):
                        pe.matmul(ps[:, tt % 2, h * P:(h + 1) * P], vnat[:, tt, h * P:(h + 1) * P],
                                  within[:, tt % 2, h, :], start=h == 0, stop=False)
                pe.wait_ge(S["state_ok"], c + 1)
                for h in range(HH):
                    head = slice(h * P, (h + 1) * P)
                    dst = ps[:, tt % 2, h * P + c * CH % P:h * P + c * CH % P + CH]
                    ins = pe.matmul(dst, state[:, c % 4, head], qi[:, h, chunk(c)], start=False,
                                    stop=h == HH - 1 and (c + 1) * CH % P == 0)
                ins.then_inc(S["o_mm"], 1)
                gate_products(c * GATES_HG, (c + 1) * GATES_HG)
            pe.wait_ge(S["osq_ok"], 1)
            for h in range(HH):
                need(pe, S["osd_ok"], h - 1)
                pe.matmul(ps[:, 4 + h % 2, :], ones[:], osq[:, h, :], start=True, stop=True).then_inc(S["osum_mm"], 1)

            pe.wait_ge(S["state_ok"], NCH)
            pe.wait_ge(S["o_out"], TT)
            pe.wait_ge(S["osd_ok"], HH)
            pe.wait_ge(S["mt_out"], 2)

            def scores(n):
                tt, c, kv, s = n // AQ, n % AQ // 2, slice(n % 2 * HD, (n % 2 + 1) * HD), n % 2
                need(pe, S["amax"], n - 1)
                lo = P if tt == 0 else 0
                q_ = aq_z[kv, c, tt * P:(tt + 1) * P]
                pe.matmul(ps[:, 6 + s, lo:BAND], q_, ak_z[kv, META + (tt - 1) * P + lo:META + (tt + 1) * P],
                          start=True, stop=True)
                pe.matmul(ps[:, 6 + s, BAND:KEYS], q_, ak_z[kv, 0:META], start=True, stop=True).then_inc(S["asc_mm"], 1)

            def turn(n):
                tt, s = n // AQ, n % 2
                pe.wait_ge(S["anorm"], n + 1)
                need(pe, S["atr_out"], 2 * (n - 1))
                for q in range(0 if tt else 1, 2):
                    pe.transpose(ps[:, 4 + s, q * P:(q + 1) * P], atp[:, s, q * P:(q + 1) * P], ident[:])
                pe.transpose(ps[0:META, 4 + s, BAND:BAND + P], atp[:, s, BAND:KEYS], ident[:]).then_inc(S["atr_mm"], 1)

            def values(n):
                tt, c, kv, s = n // AQ, n % AQ // 2, slice(n % 2 * HD, (n % 2 + 1) * HD), n % 2
                pe.wait_ge(S["atr_out"], 2 * (n + 1))
                if n % AQ == 0:
                    need(pe, S["oat_ok"], tt - 1)
                dst = ps[kv, tt % 2, c * P:(c + 1) * P]
                if tt:
                    pe.matmul(dst, avnat[:, tt - 1, kv], atpT[:, s, 0:P], start=True, stop=False)
                pe.matmul(dst, avnat[:, tt, kv], atpT[:, s, P:BAND], start=tt == 0, stop=False)
                pe.matmul(dst, avmeta[:, kv], atpTm[:, s, :], start=False, stop=True).then_inc(S["apv_mm"], 1)

            for n in range(TT * AQ + 2):
                if n < TT * AQ:
                    scores(n)
                if 1 <= n <= TT * AQ:
                    turn(n - 1)
                if n >= 2:
                    values(n - 2)
                if n < TT * AQ:
                    gate_products(GATES_AT0 + n * GATES_AT, GATES_AT0 + (n + 1) * GATES_AT)

            pe.wait_ge(S["ohg_ok"], HH)
            pe.wait_ge(S["oat_ok"], TT)
            for c in range(DC):
                pe.wait_ge(S["w_lo"], T_BRANCH + c + 1)
                need(pe, S["br_f"], c - 1)
                if c == 0:
                    pe.wait_ge(S["gate_out"], N_GATE)
                s = c % 2
                for side, src in enumerate((ohg, oat)):
                    for q in range(4):
                        ins = three(ps[:, 2 * s + side, :], parts(w, s, slice((side * 4 + q) * P, (side * 4 + q + 1) * P)),
                                    parts(src, q), q == 0, q == 3)
                    if side == 0:
                        continue
                    ins.then_inc(S["w_used"], 1)
            pe.wait_ge(S["m_ok"], DC)
            for c in range(DC):
                pe.wait_ge(S["w_lo"], T_OUT + c + 1)
                for n in range(2 * TT):
                    ins = three(ps[:, n, :], parts(m, c, slice(n // 2 * P, (n // 2 + 1) * P)),
                                parts(w, c % 2, slice(n % 2 * 512, (n % 2 + 1) * 512)), c == 0, c == DC - 1)
                ins.then_inc(S["w_used"], 1)
            pe.wait_ge(S["ynat_ok"], TT)
            for c in range(DC):
                need(pe, S["ht_ok"], c - 1)
                for tt in range(TT):
                    ins = pe.transpose(ps[:, c % 2, tt * P:(tt + 1) * P], ynat[:, tt, c * P:(c + 1) * P], ident[:])
                ins.then_inc(S["ht_mm"], 1)
            pe.wait_ge(S["ht_ok"], DC)
            for n in range(RS + 1):
                if n < RS:
                    pe.wait_ge(S["w_lo"], T_WQ + n + 1)
                    need(pe, S["q_ok"], n - 1)
                    project(n % 2, hT, ps[:, n % 2, :]).then_inc(S["w_used"], 1)
                if n >= 1:
                    r = n - 1
                    pe.wait_ge(S["q_ok"], n)
                    need(pe, S["s_out"], r - 1)
                    for tt in range(TT):
                        ins = three(ps[:, 2 + r % 2, tt * P:(tt + 1) * P], parts(q2, r % 2, slice(tt * P, (tt + 1) * P)),
                                    parts(keys, r), True, True)
                    ins.then_inc(S["s_mm"], 1)
            def u_group(g):
                for b in range(GRP):
                    n = g * GRP + b
                    pe.wait_ge(S["u_lo"], n + 1)
                    need(pe, S["gelu_ok"], n - 1)
                    for c in range(DC):
                        ins = three(ps[:, b % 2, :], parts(uw, b % 2, slice(c * P, (c + 1) * P)), parts(hT, c),
                                    c == 0, c == DC - 1)
                    ins.then_inc(S["u_mm"], 1)

            for g in range(EARLY_TOP):
                u_group(g)
            for q, (t, ok) in enumerate(((ei, "ei_ok"), (ej, None), (gate, "gate_ok"))):
                if q == 0:
                    pe.wait_ge(S["gate_ok"], 1)
                if ok:
                    pe.wait_ge(S[ok], 2 if q == 0 else 1)
                for tt in range(TT):
                    ins = pe.transpose(ps[:, 4 + q, tt * P:(tt + 1) * P],
                                       t[:, tt].rearrange("p h k -> p (h k)"), ident[:])
                ins.then_inc(S["col_mm"], 1)

            def gate_matrices(it):
                for c in range(2):
                    for s in range(GT // BATCH):
                        batch = it * (2 * GT // BATCH) + (c * GT // BATCH + s)
                        pe.wait_ge(S["hotg_ok"], batch + 1)
                        pe.wait_ge(S["hoti_ok"], batch + 1)
                        for q in range(2):
                            bank = 4 + s % 2 * 2 + q
                            need(pe, S["g_out"], it * (2 * GT // 4) + (c * GT // 4 + 2 * s + q - 3))
                            for t in range(4):
                                ins = pe.matmul(ps[:, bank, t * P:(t + 1) * P], hot_g[:, s % 2, q * 4 + t, :],
                                                hot_i[:, s % 2, q * 4 + t, :], start=True, stop=True)
                            ins.then_inc(S["g_mm"], 1)
                        if s == 0:
                            pe.wait_ge(S["u_lo"], it * 2 + (NTOP + c + 1))
                            pe.wait_ge(S["gelu_ok"], it * 2 + (NTOP + c - 1))
                        ins = three(ps[:, c, :], parts(uw, c, slice(s * P, (s + 1) * P)), parts(hT, s), s == 0, s == DC - 1)
                        if s == DC - 1:
                            ins.then_inc(S["u_mm"], 1)

            pe.wait_ge(S["col_ok"], 3)
            gate_matrices(0)
            with pe.Fori(1, NPIECE // 2, 1) as it:
                gate_matrices(it)
            for g in range(NLAST // GRP, EARLY):
                u_group(g)
            pe.wait_ge(S["g_out"], TOK // 4)
            pe.wait_ge(S["gelu_ok"], NEARLY)

            def v_group(g, s):
                pe.wait_ge(S["aw_ok"], g * GRP + GRP)
                pe.wait_ge(S["v_lo"], g * GRP + GRP)
                for j in range(2 * TT):
                    pe.wait_ge(S["o2_out"], g * 8 + (j - 3 - 8 * (EARLY - 1)))
                    for b in range(GRP):
                        ins = three(ps[:, 2 + j % 4, :], parts(act_w, s, b, slice(j // 2 * P, (j // 2 + 1) * P)),
                                    parts(vw, b, slice(j % 2 * 512, (j % 2 + 1) * 512)), b == 0, b == GRP - 1)
                    ins.then_inc(S["o2_mm"], 1)

            def early_groups(it, first=False, last=False):
                for s in range(2):
                    for b in range(GRP):
                        n = it * 2 * GRP + (s * GRP + b)
                        start, end = first and s == 0 and b == 0, last and s == 1 and b == GRP - 1
                        pe.wait_ge(S["aw_ok"], n + 1)
                        pe.wait_ge(S["v_lo"], n + 1)
                        for j in range(2 * TT):
                            ins = three(ps[:, j, :], parts(act_w, s, b, slice(j // 2 * P, (j // 2 + 1) * P)),
                                        parts(vw, b, slice(j % 2 * 512, (j % 2 + 1) * 512)), start, end)
                            if end:
                                ins.then_inc(S["o2_mm"], 1)
                        if not end:
                            ins.then_inc(S["early_mm"], 1)

            early_groups(0, first=True)
            with pe.Fori(1, EARLY // 2 - 1, 1) as it:
                early_groups(it)
            early_groups(EARLY // 2 - 1, last=True)
            pe.wait_ge(S["o2_out"], 2)
            u_group(EARLY)
            u_group(EARLY + 1)
            v_group(EARLY, 0)
            with pe.Fori(EARLY // 2, NGRP // 2 - 1, 1) as it:
                u_group(it * 2 + 2)
                v_group(it * 2 + 1, 1)
                u_group(it * 2 + 3)
                v_group(it * 2 + 2, 0)
            v_group(NGRP - 1, 1)


def kernel(x, meta_tokens, mix_norm_g, w_in, b_gate, hg_lb_logits, hg_norm_g, attn_sinks, w_branch_hg,
           w_branch_attn, w_out, ffn_norm_g, peer_w_q, peer_subkeys, peer_u, peer_v, final_norm_g):
    import numpy as np
    from concourse import bacc
    from concourse.bass_utils import run_bass_kernel_spmd

    a = np.asarray

    def columns(t):
        return a(t).reshape(-1, P).T

    def blocks(t):
        t = a(t)
        return t.reshape(DC, P, t.shape[1] // P, P).transpose(2, 1, 0, 3).reshape(-1, P, D)

    tokens = a(x)[0]
    both = np.concatenate([a(meta_tokens), tokens], axis=0)
    w = a(w_in)[0]
    width = HH * P
    f, q, v_, og = w[:, width:2 * width], w[:, 0:width], w[:, 2 * width:3 * width], w[:, 3 * width:4 * width]
    at0 = 4 * width
    aq, ak, av = w[:, at0:at0 + AQ * HD], w[:, at0 + 512:at0 + 640], w[:, at0 + 640:at0 + 768]
    aq = aq.reshape(D, 2, 4, HD).transpose(0, 2, 1, 3).reshape(D, AQ * HD)
    wb_at = a(w_branch_attn)[0].reshape(2, 4, HD, D).transpose(1, 0, 2, 3).reshape(AQ * HD, D)
    gates = w[:, at0 + 768:]
    branch = np.concatenate([a(w_branch_hg)[0], wb_at], axis=0)
    keys = a(peer_subkeys)[0].reshape(RS, NK, P).transpose(2, 0, 1).reshape(P, 2, RH * NK).transpose(1, 0, 2)
    wstream = np.concatenate([blocks(f), blocks(q), blocks(v_), blocks(ak), blocks(av), blocks(og), blocks(aq),
                              blocks(gates), blocks(branch), a(w_out)[0].reshape(DC, P, D), keys,
                              blocks(a(peer_w_q)[0])], axis=0)
    assert wstream.shape == (N_TILES, P, D)
    params = np.concatenate([columns(mix_norm_g), columns(ffn_norm_g), columns(hg_norm_g),
                             columns(hg_lb_logits), columns(b_gate)], axis=1)
    arrays = {
        "xT": both.T.reshape(DC, P, LEN).transpose(1, 0, 2),
        "x": tokens,
        "params": params,
        "sinks": a(attn_sinks),
        "final_g": a(final_norm_g)[None],
        "wstream": wstream,
        "uT": a(peer_u)[0].reshape(NK, NK, DC, P).transpose(0, 3, 2, 1).reshape(NK, P, D),
        "v": a(peer_v)[0].reshape(NK, NK, D),
    }
    nc = bacc.Bacc("TRN2", target_bir_lowering=False, num_devices=1)
    arrays = {f"in_{k}": np.ascontiguousarray(t) for k, t in arrays.items()}
    ins = [nc.dram_tensor(k, t.shape, F32, kind="ExternalInput").ap() for k, t in arrays.items()]
    gates_dram = nc.dram_tensor("gates_dram", [NGRP, NPIECE, P, GRP * GT], F32, kind="Internal").ap()
    out = nc.dram_tensor("out", (TOK, D), F32, kind="ExternalOutput").ap()
    early_dram = nc.dram_tensor("early_dram", [SPILLED, P, GRP * TOK], F32, kind="Internal").ap()
    build(nc, *ins, gates_dram, early_dram, out)
    r = run_bass_kernel_spmd(nc, [arrays], core_ids=[0])
    return r.results[0]["out"].reshape(1, TOK, D)
```

```python
from contextlib import ExitStack

import concourse.bass as bass
from concourse import mybir

F32 = mybir.dt.float32
F32R = mybir.dt.float32r
U32 = mybir.dt.uint32
ALU = mybir.AluOpType
ACT = mybir.ActivationFunctionType
AX_X = mybir.AxisListType.X

P = 128
D = 1024
DC = D // P
TOK = 512
TT = TOK // P
META = 16
LEN = META + TOK
EPS = 1e-6
HH = 4
CH = 32
HALF = CH // 2
NCH = TOK // CH
NBLK = LEN // HALF
TINY = 1e-37
AQ = 8
HD = 64
BAND = 2 * P
KEYS = BAND + META
HIDDEN = -1e30
RH = 8
RS = 2 * RH
NK = 128
TOP = 16
PAIRS = [TOP // (a + 1) for a in range(TOP)]
STARTS = [sum(PAIRS[:a]) for a in range(TOP)]
CAND = sum(PAIRS)
LOWEST = -3.0e38

Z_META = 10
Z_REST = 12
N_Z = Z_META + Z_REST
N_GATE = 16
T_GATE = N_Z
T_BRANCH = T_GATE + N_GATE
T_OUT = T_BRANCH + DC
T_KEYS = T_OUT + DC
T_WQ = T_KEYS + 2
N_TILES = T_WQ + RS

GRP = 4
NGRP = NK // GRP
GT = 64
NPIECE = TOK // GT
BATCH = 8
EARLY_TOP, EARLY_GATES, EARLY_LAST = 4, 2, 2
EARLY = EARLY_TOP + EARLY_GATES + EARLY_LAST
SPILLED = EARLY - 2
NEARLY = EARLY * GRP
NTOP = EARLY_TOP * GRP
NLAST = NEARLY - EARLY_LAST * GRP
assert EARLY_GATES * GRP == NPIECE and EARLY_LAST == 2
EI_POOL = 6
GATES_HG = 6
GATES_MID = 16
GATES_AT = 8
assert NCH * GATES_HG + 2 * GATES_MID + TT * AQ * GATES_AT == N_GATE * 3 * DC
V_SPLITS = ((0, 1), (2,), (3,), ())

SPLIT = (("hi", "hi"), ("hi", "lo"), ("lo", "hi"))


def need(eng, semaphore, value):
    if not (isinstance(value, int) and value <= 0):
        eng.wait_ge(semaphore, value)


def gates_before(n):
    return NCH * GATES_HG + GATES_MID + min(n, TT * AQ) * GATES_AT + (GATES_MID if n > TT * AQ else 0)


def gate_blocks_done(first, last):
    return range(first // (3 * DC), last // (3 * DC))


class Chain:

    def __init__(self, eng, sem):
        self.eng, self.sem, self.count = eng, sem, 0

    def done(self, ins):
        ins.then_inc(self.sem, 1)
        self.count += 1
        self.eng.wait_ge(self.sem, self.count)


def build(nc, xT, x, params, sinks, ffn_g, final_g, wstream, uT, v, gates_dram, early_dram, out):
    ctx = ExitStack()
    with ctx:
        BASE = 16512

        def at(name, shape, dt, offset):
            return nc.alloc_sbuf_tensor_at(name, shape, dt, offset=BASE + offset)

        def sem(name):
            return ctx.enter_context(nc.semaphore(name))

        C, A, B, Z, G0, RING, E, X = 0, 8192, 41984, 58880, 105344, 138112, 162688, 179584
        ident = at("ident", [P, P], F32, C)
        ones = at("ones", [P, P], F32, C + 512)
        iota = at("iota", [P, P], F32, C + 1024)
        bandmask = at("bandmask", [P, KEYS], F32, C + 1536)
        chunkmask = at("chunkmask", [P, CH], F32, C + 2624)
        par = at("par", [P, 36], F32, C + 2752)
        sink = at("sink", [P, AQ], F32, C + 2944)
        eps = at("eps", [P, 1], F32, C + 2976)
        lbw = at("lbw", [P, 6, HH], F32, C + 3008)
        rowstat = at("rowstat", [P, 3, TT], F32, C + 3104)
        atstat = at("atstat", [P, 3, 2], F32, C + 3168)
        ecol = at("ecol", [P, HH, NCH], F32, C + 3200)
        sd = at("sd", [P, TOK], F32, C + 3456)
        rstd = at("rstd", [P, TOK], F32, C + 5504)
        meta_sd = at("meta_sd", [META, 2], F32, C + 7552)
        mix_g, hg_g = par[:, 0:8], par[:, 8:12]
        lb_logits = par[:, 12:20].rearrange("p (r h) -> p r h", r=2)
        b_gate = par[:, 20:36]

        y = {k: at("y" + k, [P, DC, LEN], F32R, A + i * DC * LEN * 4) for i, k in enumerate(("hi", "lo"))}
        xt = at("xt", [P, DC, LEN], F32, B)
        xsq = at("xsq", [P, DC, LEN], F32, Z)
        zm = at("zm", [P, Z_META, LEN], F32, Z)
        zr = at("zr", [P, Z_REST, TOK], F32, Z + Z_META * LEN * 4)
        f_z, v_z, ak_z, av_z = zm[:, 0:4], zm[:, 4:8], zm[:, 8], zm[:, 9]
        q_z, og_z, aq_z = zr[:, 0:4], zr[:, 4:8], zr[:, 8:12]
        gates = at("gates", [P, N_GATE, TOK], F32, G0)
        raw = at("raw", [P, 2, D], F32, RING)
        w = {k: at("w" + k, [P, 2, D], F32R, RING + 8192 + i * 8192) for i, k in enumerate(("hi", "lo"))}
        decay = at("decay", [P, HH, LEN], F32, B)
        inv = at("inv", [P, HH, LEN], F32, B + 8448)
        starts = at("starts", [P, HH, LEN], F32, B + 8448)
        kk = at("kk", [P, HH, LEN], F32, E)
        qi = at("qi", [P, HH, TOK], F32, E + 8448)
        knat = at("knat", [P, TT, 512], F32, Z)
        vnat = at("vnat", [P, TT, 512], F32, X + 12288)
        znat = at("znat", [META, Z_META, P], F32, X + 20480)
        vmeta = znat[:, 4:8, :].rearrange("p h d -> p (h d)")
        avmeta = znat[:, 9, :]
        kmeta = at("kmeta", [META, 512], F32, X + 25600)
        avnat = at("avnat", [P, TT, P], F32, X + 27648)
        atsc = at("atsc", [P, 2, KEYS + 8], F32, X)
        atp = at("atp", [P, 2, KEYS + 8], F32, X + 2240)
        atpT = at("atpT", [P, 2, BAND], F32, X + 4480)
        atpTm = at("atpTm", [META, 2, P], F32, X + 6528)
        state = at("state", [P, 4, 512], F32, X)
        within = at("within", [P, 2, HH, P], F32, X + 8192)
        osq = at("osq", [P, HH, TOK], F32, Z)
        o_hg = at("o_hg", [P, HH, TOK], F32, B)
        orstd = at("orstd", [P, HH, TOK], F32, B + 8192)
        ohg = {k: at("ohg" + k, [P, HH, TOK], F32R, Z + i * 8192) for i, k in enumerate(("hi", "lo"))}
        oat = {k: at("oat" + k, [P, 4, TOK], F32R, E + i * 8192) for i, k in enumerate(("hi", "lo"))}
        m = {k: at("m" + k, [P, DC, TOK], F32R, A + i * 16384) for i, k in enumerate(("hi", "lo"))}
        mtmp = at("mtmp", [P, 2, 2, TOK], F32, B)
        acc = at("acc", [P, TT, D], F32, Z + Z_META * LEN * 4 + 8192)
        ynat = at("ynat", [P, TT, D], F32, E)
        ffn_row = at("ffn_row", [P, D], F32, E + 32768)
        ysq = at("ysq", [P, 2, D], F32, A)
        hT = {k: at("hT" + k, [P, DC, TOK], F32R, G0 + i * 16384) for i, k in enumerate(("hi", "lo"))}
        keys = {k: at("keys" + k, [P, RS, NK], F32R, E + 16384 + i * 8192) for i, k in enumerate(("hi", "lo"))}
        q2 = {k: at("q2" + k, [P, 2, TOK], F32R, A + i * 4096) for i, k in enumerate(("hi", "lo"))}
        score = at("score", [P, 2, TT, NK], F32, A + 8192)
        scut = at("scut", [P, 2, TT, NK], F32, A + 12288)
        top_v = at("top_v", [P, TT, RS, TOP], F32, A + 16384)
        top_i = at("top_i", [P, TT, RS, TOP], U32, A + 20480)
        top_f = at("top_f", [P, TT, RS, TOP], F32, A + 24576)
        step_f = at("step_f", [P, TT, RS, TOP], F32, A + 28672)
        cand = at("cand", [P, TT * RH, CAND], F32, A + 32768)
        ccut = at("ccut", [P, TT * RH, CAND], F32, A + 39168)
        best = at("best", [P, TT, RH, TOP], F32, E)
        pos_u = at("pos_u", [P, TT * RH, TOP], U32, E + 2048)
        pos = at("pos", [P, TT, RH, TOP], F32, E + 4096)
        gate = at("gate", [P, TT, RH, TOP], F32, E + 6144)
        tot = at("tot", [P, 2, TT * RH], F32, E + 8192)
        ei = at("ei", [P, TT, RH, TOP], F32, E + 8448)
        ej = at("ej", [P, TT, RH, TOP], F32, E + 10496)
        posb = at("posb", [P, TT, RH, TOP], F32, E + 12544)
        tmp_i = at("tmp_i", [P, TT, RH, TOP], F32, A + 47616)
        tmp_j = at("tmp_j", [P, TT, RH, TOP], F32, A + 45568)
        ei_high = at("ei_high", [P, TT, RH, TOP], F32, A + 49664)
        cols = at("cols", [P, 3, TOK], F32, E + 24576)
        hot_i = at("hot_i", [P, 2, BATCH, NK], F32, E + 0)
        hot_g = at("hot_g", [P, 2, BATCH, NK], F32, E + 8192)
        hot_j = at("hot_j", [P, 2, BATCH, NK], F32, E + 16384)
        early = at("early", [P, 2, GRP, TOK], F32, E + 32768)
        piece = at("piece", [P, 2, NK, GT], F32, A)
        vw = {k: at("vw" + k, [P, GRP, D], F32R, A + i * 16384) for i, k in enumerate(("hi", "lo"))}
        act_w = {k: at("aw" + k, [P, 2, GRP, TOK], F32R, A + 32768 + i * 16384) for i, k in enumerate(("hi", "lo"))}
        gelu = at("gelu", [P, 2, TOK], F32, A + 65536)
        prod = at("prod", [P, 2, TOK], F32, A + 69632)
        uraw = at("uraw", [P, 2, D], F32, RING)
        uw = {k: at("uw" + k, [P, 2, D], F32R, RING + 8192 + i * 8192) for i, k in enumerate(("hi", "lo"))}
        vraw = at("vraw", [P, GRP, D], F32, E)
        gmat = at("gmat", [P, 2, NPIECE, GRP, GT], F32, E + 16384)
        fin_g = at("fin_g", [P, D], F32, E)
        fin_o = at("fin_o", [P, TT, D], F32, A)

        ps = ctx.enter_context(nc.psum_tensor("ps", [P, 8, 512], F32))

        vec, poo = sem("vec"), sem("poo")
        names = """par_in acc_in fin_in consts xsq_ok xsum_ok sd_ok rstd_ok z_copied gate_copied zn_out yhi_ok y_ok w_hi w_lo w_used z_out
            gate_out lb_exp lb_max f_sig og_sig og_used hg_ok tr_mm tr_out_v tr_out_s upd_mm state_ok wsc_mm within_ok
            o_mm o_out osq_ok osum_mm osd_ok mt_mm mt_out gate_sig ohg_f ohg_hi ohg_ok asc_mm amax aexp anorm atr_mm atr_out apv_mm
            oat_hi oat_ok br_f m_hi m_ok acc_mm ffn_in acc_ok ss_ok ysd_ok ynat_ok ht_mm ht_hi ht_ok early_mm early_in q_hi q_ok s_mm s_out
            s_used tops_ok topf_ok step_ok pos_ok soft soft_exp gate_ok ei_ok col_mm col_ok hoti_ok hotj_ok hotg_ok g_mm g_out
            v_in u_hi u_lo v_hi v_lo u_mm gelu_ok prod_ok aw_hi aw_ok o2_mm o2_out final_mm fss_ok fsd_ok fin_ok stored"""
        S = {n: sem(n) for n in names.split()}
        w_in, g_store, u_in, gm_in, early_out = ([sem(f"{n}{k}") for k in range(2)] for n in
                                                 ("w_in", "g_store", "u_in", "gm_in", "early_out"))

        xt_in = [sem(f"xt_in{c}") for c in range(DC)]

        block = ctx.enter_context(nc.Block())


        def key_step(c, a):
            return step_f[:].rearrange("p t (h c) a -> p t h c a", c=2)[:, :, :, c, a:a + 1].to_broadcast([P, TT, RH, TOP])

        @block.sync
        def _(sp):
            sp.dma_start(par[:], params).then_inc(S["par_in"], 16)
            sp.dma_start(sink[:], sinks.to_broadcast([P, AQ])).then_inc(S["par_in"], 16)
            sp.dma_start(raw[:, 0, :], wstream[0]).then_inc(w_in[0], 16)
            for c in range(DC):
                sp.dma_start(xt[:, c, :], xT[:, c, :]).then_inc(xt_in[c], 16)
                if c == 1:
                    sp.dma_start(raw[:, c, :], wstream[c]).then_inc(w_in[c], 16)
            with sp.Fori(1, N_TILES // 2, 1) as it:
                for k in range(2):
                    sp.wait_ge(S["w_lo"], it * 2 + (k - 1))
                    sp.dma_start(raw[:, k, :], wstream[bass.ds(it * 2 + k, 1)].rearrange("o p d -> p (o d)")
                                 ).then_inc(w_in[k], 16)
            for k in range(2):
                sp.wait_ge(S["w_lo"], N_TILES - 1 + k)
                sp.dma_start(uraw[:, k, :], uT[k]).then_inc(u_in[k], 16)
            with sp.Fori(1, NTOP // 2 + 2, 1) as it:
                for k in range(2):
                    sp.wait_ge(S["u_lo"], it * 2 + (k - 1))
                    sp.dma_start(uraw[:, k, :], uT[bass.ds(it * 2 + k, 1)].rearrange("o p d -> p (o d)")
                                 ).then_inc(u_in[k], 16)
            for c in range(NPIECE):
                if c:
                    n = NTOP + 3 + c
                    sp.wait_ge(S["u_lo"], n - 1)
                    sp.dma_start(uraw[:, n % 2, :], uT[n]).then_inc(u_in[n % 2], 16)
                sp.wait_ge(S["g_out"], (c + 1) * GT // 4)
                sp.dma_start(gates_dram[:, c].rearrange("g j r -> j g r"),
                             piece[:, c % 2].rearrange("p (g i) t -> p g (i t)", i=GRP)).then_inc(g_store[c % 2], 16)
            for k in range(2):
                sp.wait_ge(g_store[k], 16 * NPIECE // 2)
            sp.wait_ge(S["g_mm"], TOK // 4)
            def early_groups(it):
                for s in range(2):
                    g = NLAST // GRP + s if isinstance(it, int) else it * 2 + (s - 2)
                    need(sp, S["prod_ok"], it * 2 * GRP + (s - 1) * GRP)
                    gates_of = gates_dram[bass.ds(g, 1)].rearrange("o c j r -> j (o c) r")
                    sp.dma_start(gmat[:, s], gates_of).then_inc(gm_in[s], 16)
                    if not isinstance(it, int):
                        sp.dma_start(early[:, s].rearrange("p b t -> p (b t)"), early_dram[bass.ds(g, 1)]
                                     .rearrange("o p d -> p (o d)")).then_inc(S["early_in"], 16)
                    need(sp, S["v_lo"], it * 2 * GRP + s * GRP)
                    sp.dma_start(vraw[:], v[bass.ds(g * GRP, GRP)].rearrange("i j d -> j i d")).then_inc(S["v_in"], 16)

            sp.wait_ge(u_in[0], (NLAST + 4) * 8 + 16)
            early_groups(0)
            for k in range(2):
                sp.wait_ge(early_out[k], 16 * SPILLED // 2)
            with sp.Fori(1, EARLY // 2, 1) as it:
                early_groups(it)
            sp.wait_ge(S["prod_ok"], (EARLY - 1) * GRP)
            sp.dma_start(gmat[:, 0], gates_dram[EARLY].rearrange("c j r -> j c r")).then_inc(gm_in[0], 16)
            for n in (2, 3):
                sp.wait_ge(S["u_lo"], NEARLY + n - 1)
                sp.dma_start(uraw[:, n % 2, :], uT[NEARLY + n]).then_inc(u_in[n % 2], 16)

            def load_v(g):
                sp.wait_ge(S["v_lo"], g * GRP)
                sp.dma_start(vraw[:], v[bass.ds(g * GRP, GRP)].rearrange("i j d -> j i d")).then_inc(S["v_in"], 16)

            def period(g, s, more=True):
                if isinstance(g, int) and g == EARLY:
                    load_v(g)
                if more:
                    for b in range(GRP):
                        sp.wait_ge(S["u_lo"], g * GRP + (GRP + b - 1))
                        sp.dma_start(uraw[:, b % 2, :], uT[bass.ds(g * GRP + (GRP + b), 1)]
                                     .rearrange("o p d -> p (o d)")).then_inc(u_in[b % 2], 16)
                        if b == 1:
                            need(sp, S["prod_ok"], g * GRP)
                            sp.dma_start(gmat[:, 1 - s], gates_dram[bass.ds(g + 1, 1)]
                                         .rearrange("o c j r -> j (o c) r")).then_inc(gm_in[1 - s], 16)
                if not (isinstance(g, int) and g == EARLY):
                    load_v(g)

            period(EARLY, 0)
            with sp.Fori(EARLY // 2, NGRP // 2 - 1, 1) as it:
                period(it * 2 + 1, 1)
                period(it * 2 + 2, 0)
            period(NGRP - 1, 1, more=False)
            sp.wait_ge(S["v_lo"], NGRP * GRP)
            sp.dma_start(fin_g[:], final_g.to_broadcast([P, D])).then_inc(S["fin_in"], 16)
            for tt in range(TT):
                sp.wait_ge(S["fin_ok"], tt + 1)
                sp.dma_start(out[tt * P:(tt + 1) * P, :], fin_o[:, tt, :]).then_inc(S["stored"], 16)
            sp.wait_ge(S["stored"], 16 * TT)

        @block.gpsimd
        def _(pool):
            chain = Chain(pool, poo)
            pool.memset(ones[:], 1.0)
            pool.memset(eps[:], EPS)
            pool.iota(iota[:], [[1, P]], base=0, channel_multiplier=0, allow_small_or_imprecise_dtypes=True)
            pool.memset(ident[:], 0.0)
            pool.memset(bandmask[:], 0.0)
            pool.memset(within[:], 0.0)
            chain.done(pool.memset(chunkmask[:], 1.0))
            chain.done(pool.affine_select(out=ident[:], in_=ident[:], compare_op=ALU.not_equal, fill=1.0,
                                          base=0, pattern=[[-1, P]], channel_multiplier=1))
            chain.done(pool.affine_select(out=bandmask[:, 0:P], in_=bandmask[:, 0:P], compare_op=ALU.is_gt,
                                          fill=HIDDEN, base=0, pattern=[[1, P]], channel_multiplier=-1))
            chain.done(pool.affine_select(out=bandmask[:, P:BAND], in_=bandmask[:, P:BAND], compare_op=ALU.is_ge,
                                          fill=HIDDEN, base=0, pattern=[[-1, P]], channel_multiplier=1))
            for r in range(P // CH):
                band = chunkmask[r * CH:(r + 1) * CH, :]
                chain.done(pool.affine_select(out=band, in_=band, compare_op=ALU.is_ge, fill=0.0,
                                              base=0, pattern=[[1, CH]], channel_multiplier=-1))
            pool.sem_inc(S["consts"], 1)

            def split_lo(n, k, dst):
                pool.wait_ge(S["w_hi"], n + 1)
                pool.tensor_tensor(dst["lo"], raw[:, k, :], dst["hi"].bitcast(F32), ALU.subtract).then_inc(S["w_lo"], 1)

            def slot(k):
                return {part: w[part][:, k, :] for part in w}

            pool.wait_ge(S["w_lo"], 1)
            split_lo(1, 1, slot(1))

            def scale_blocks(first, last, dst, shift, copied, ok):
                with pool.Fori(first // 2, last // 2, 1) as it:
                    for k in range(2):
                        own = dst[:, bass.ds(it * 2 + (k - shift), 1)]
                        split_lo(it * 2 + (k + 2), k, slot(k))
                        pool.wait_ge(S[copied], it * 2 + (k + 1 - (T_GATE if dst is gates else 0)))
                        pool.tensor_tensor(own, own, rstd[:].unsqueeze(1), ALU.mult).then_inc(S[ok], 1)

            pool.wait_ge(S["rstd_ok"], 1)
            scale_blocks(0, 4, zm[:, :, META:LEN], 0, "z_copied", "z_out")
            scale_blocks(4, 8, zr, 4, "z_copied", "z_out")
            scale_blocks(8, 14, zm[:, :, META:LEN], 4, "z_copied", "z_out")
            scale_blocks(14, N_Z, zr, 10, "z_copied", "z_out")
            scale_blocks(T_GATE, T_BRANCH, gates, T_GATE, "gate_copied", "gate_out")
            with pool.Fori(T_BRANCH // 2 + 1, T_KEYS // 2, 1) as it:
                for k in range(2):
                    split_lo(it * 2 + k, k, slot(k))
            for k in range(2):
                split_lo(T_KEYS + k, k, {p: keys[p][:, k * RH:(k + 1) * RH, :].rearrange("p r n -> p (r n)") for p in keys})
            with pool.Fori(T_WQ // 2, N_TILES // 2, 1) as it:
                for k in range(2):
                    split_lo(it * 2 + k, k, slot(k))

            def u_split(n):
                pool.wait_ge(S["u_hi"], n + 1)
                pool.tensor_tensor(uw["lo"][:, n % 2, :], uraw[:, n % 2, :], uw["hi"][:, n % 2, :].bitcast(F32),
                                   ALU.subtract).then_inc(S["u_lo"], 1)

            for n in range(NTOP // 2):
                if n == 4:
                    pool.wait_ge(S["topf_ok"], 1)
                    pool.tensor_copy(step_f[:, :, :, 0:1], top_f[:, :, :, 0:1])
                    pool.tensor_tensor(step_f[:, :, :, 1:TOP], top_f[:, :, :, 1:TOP], top_f[:, :, :, 0:TOP - 1],
                                       ALU.subtract).then_inc(S["step_ok"], 1)
                u_split(n)
            pool.wait_ge(S["pos_ok"], 1)
            pool.wait_ge(S["step_ok"], 1)
            chain.done(pool.tensor_copy(ei[:], key_step(0, 0)))
            for a in range(1, EI_POOL):
                u_split(NTOP // 2 + a - 1)
                chain.done(pool.tensor_scalar(tmp_i[:], pos[:], float(STARTS[a]), None, ALU.is_ge))
                chain.done(pool.tensor_tensor(tmp_i[:], tmp_i[:], key_step(0, a), ALU.mult))
                ins = pool.tensor_tensor(ei[:], ei[:], tmp_i[:], ALU.add)
                if a < EI_POOL - 1:
                    chain.done(ins)
            ins.then_inc(S["ei_ok"], 1)
            for n in range(NTOP // 2 + EI_POOL - 1, NTOP + 1):
                u_split(n)

            def weigh(it):
                for c in range(2):
                    for s in range(GT // BATCH):
                        batch = it * (2 * GT // BATCH) + (c * GT // BATCH + s)
                        pool.wait_ge(S["hotj_ok"], batch + 1)
                        need(pool, S["g_mm"], it * (2 * GT // 4) + (c * GT // 4 + 2 * s - 2))
                        pool.tensor_tensor(hot_g[:, s % 2], hot_j[:, s % 2], cols[:, 2, bass.ds(batch * BATCH, BATCH)]
                                           .unsqueeze(2).to_broadcast([P, BATCH, NK]), ALU.mult).then_inc(S["hotg_ok"], 1)
                        if 2 <= s < 6:
                            quarter = slice((s - 2) * D // 4, (s - 1) * D // 4)
                            pool.wait_ge(S["u_hi"], it * 2 + (NTOP + 2 + c))
                            ins = pool.tensor_tensor(uw["lo"][:, 1 - c, quarter], uraw[:, 1 - c, quarter],
                                                     uw["hi"][:, 1 - c, quarter].bitcast(F32), ALU.subtract)
                            if s == 5:
                                ins.then_inc(S["u_lo"], 1)

            pool.wait_ge(S["col_ok"], 3)
            weigh(0)
            with pool.Fori(1, NPIECE // 2, 1) as it:
                weigh(it)
            for n in range(NLAST + 1, NEARLY + 2):
                u_split(n)

        def transposed_dst(n):
            if n < 4:
                return vnat[:, n, :]
            if n == 4:
                return avnat[:].rearrange("p t c -> p (t c)")
            return knat[:, n - 5, :] if n < 9 else kmeta[:]

        def transposed_src(n):
            dst = transposed_dst(n)
            return ps[0:dst.shape[0], 2 + n % 2, 0:dst.shape[1]]

        def turned_hT(part, n):
            return hT[part][:, n % 2 * 4:(n % 2 + 1) * 4, n // 2 * P:(n // 2 + 1) * P]

        @block.scalar
        def _(act):
            def split_hi(n, k, dst=None):
                act.wait_ge(w_in[k], (n - k) * 8 + 16)
                if not isinstance(n, int) or n < T_KEYS:
                    need(act, S["w_used"], n - 1)
                elif n >= T_WQ:
                    act.wait_ge(S["w_used"], n - 3)
                act.activation(w["hi"][:, k, :] if dst is None else dst, raw[:, k, :], ACT.Copy).then_inc(S["w_hi"], 1)

            act.wait_ge(S["par_in"], 32)
            split_hi(0, 0)
            for c in range(DC):
                act.wait_ge(xt_in[c], 16)
                act.activation(y["hi"][:, c, :], xt[:, c, :], ACT.Copy, scale=mix_g[:, c:c + 1]).then_inc(S["yhi_ok"], 1)
                act.activation(xsq[:, c, :], xt[:, c, :], ACT.Square).then_inc(S["xsq_ok"], 1)
                if c == 1:
                    split_hi(c, c)
            act.wait_ge(S["xsum_ok"], 1)
            act.activation(sd[:], ps[:, 4, :], ACT.Sqrt, bias=eps[:], scale=1.0 / D).then_inc(S["sd_ok"], 1)
            act.activation(meta_sd[:, 0:1], ps[0:META, 5, 0:1], ACT.Sqrt, bias=eps[0:META], scale=1.0 / D
                           ).then_inc(S["sd_ok"], 1)
            act.wait_ge(S["lb_max"], 1)
            act.activation(lbw[:, 3:5], lbw[:, 1:3], ACT.Exp).then_inc(S["lb_exp"], 1)
            def z_tiles(first, last, dst, shift, meta):
                with act.Fori(first // 2, last // 2, 1) as it:
                    for k in range(2):
                        own = bass.ds(it * 2 + (k - shift), 1)
                        act.wait_ge(S["w_used"], it * 2 + (k + 1))
                        if meta:
                            act.activation(znat[:, own, :], ps[0:META, 2 + k:3 + k, 0:P],
                                           ACT.Copy, scale=meta_sd[:, 1:2]).then_inc(S["zn_out"], 1)
                        act.activation(dst[:, own, META:LEN] if meta else dst[:, own, :], ps[:, k:k + 1, :], ACT.Copy
                                       ).then_inc(S["z_copied"], 1)
                        split_hi(it * 2 + (k + 2), k)

            def gate_out(t):
                act.wait_ge(S["w_used"], T_GATE + t + 1)
                act.activation(gates[:, t, :], ps[:, 2 + t % 2, :], ACT.Copy).then_inc(S["gate_copied"], 1)
                split_hi(T_GATE + t + 2, t % 2)

            act.wait_ge(S["rstd_ok"], 2)
            z_tiles(0, 4, zm, 0, True)
            act.wait_ge(S["mt_mm"], 1)
            act.activation(f_z[:, :, 0:META], ps[:, 4, 0:HH * META].rearrange("p (h t) -> p h t", h=HH),
                           ACT.Copy).then_inc(S["mt_out"], 1)
            act.wait_ge(S["mt_out"], 1)
            act.wait_ge(S["z_out"], 4)
            act.activation(f_z, f_z, ACT.Sigmoid).then_inc(S["f_sig"], 1)
            z_tiles(4, 8, zr, 4, False)
            z_tiles(8, 14, zm, 4, True)
            act.wait_ge(S["mt_mm"], 2)
            act.activation(ak_z[:, 0:META], ps[:, 5, 0:META], ACT.Copy).then_inc(S["mt_out"], 1)
            z_tiles(14, N_Z, zr, 10, False)

            for n in range(1, 10, 2):
                act.wait_ge(S["tr_mm"], n + 1)
                act.activation(transposed_dst(n), transposed_src(n), ACT.Copy).then_inc(S["tr_out_s"], 1)
            act.wait_ge(S["hg_ok"], 1)
            act.wait_ge(S["z_out"], N_Z)
            act.activation(orstd[:], og_z, ACT.Sigmoid).then_inc(S["og_sig"], 1)
            for tt in range(TT):
                act.wait_ge(S["o_mm"], (tt + 1) * P // CH)
                act.activation(o_hg[:, :, tt * P:(tt + 1) * P], ps[:, tt % 2, :].rearrange("p (h t) -> p h t", h=HH),
                               ACT.Copy).then_inc(S["o_out"], 1)
                for t in gate_blocks_done(tt * P // CH * GATES_HG, (tt + 1) * P // CH * GATES_HG):
                    gate_out(t)
            act.wait_ge(S["o_out"], TT)
            act.activation(osq[:], o_hg[:], ACT.Square).then_inc(S["osq_ok"], 1)
            act.wait_ge(S["og_used"], 1)
            for h in range(HH):
                act.wait_ge(S["osum_mm"], h + 1)
                act.activation(orstd[:, h, :], ps[:, 4 + h % 2, :], ACT.Sqrt, bias=eps[:],
                               scale=1.0 / P).then_inc(S["osd_ok"], 1)

            def exponentials(n):
                s, lo = n % 2, P if n < AQ else 0
                act.wait_ge(S["amax"], n + 1)
                need(act, S["atr_mm"], n - 1)
                act.activation(atp[:, s, lo:KEYS + 1], atsc[:, s, lo:KEYS + 1], ACT.Exp, bias=atstat[:, 0, s:s + 1],
                               accum_out=atstat[:, 1, s:s + 1]).then_inc(S["aexp"], 1)

            def turned(n):
                s, lo = n % 2, P if n < AQ else 0
                act.wait_ge(S["atr_mm"], n + 1)
                need(act, S["apv_mm"], n - 1)
                act.activation(atpT[:, s, lo:BAND], ps[:, 4 + s, lo:BAND], ACT.Copy).then_inc(S["atr_out"], 1)
                act.activation(atpTm[:, s, :], ps[0:META, 4 + s, BAND:BAND + P], ACT.Copy).then_inc(S["atr_out"], 1)

            for n in range(TT * AQ + 1):
                if n >= 1:
                    for t in gate_blocks_done(gates_before(n - 1), gates_before(n)):
                        gate_out(t)
                if n < TT * AQ:
                    exponentials(n)
                if n >= 1:
                    turned(n - 1)
                if n == TT * AQ:
                    for t in gate_blocks_done(gates_before(n), gates_before(n + 1)):
                        gate_out(t)
                if HH * TT + 2 <= n < HH * TT + 2 + HH:
                    h = n - (HH * TT + 2)
                    act.wait_ge(S["ohg_f"], (h + 1) * TT)
                    act.activation(ohg["hi"][:, h, :], o_hg[:, h, :], ACT.Copy).then_inc(S["ohg_hi"], 1)
                if n >= 1 and n % AQ == 0:
                    tt = n // AQ - 1
                    act.wait_ge(S["apv_mm"], n)
                    act.activation(oat["hi"][:, :, tt * P:(tt + 1) * P],
                                   ps[:, tt % 2, :].rearrange("p (c t) -> p c t", c=4), ACT.Copy).then_inc(S["oat_hi"], 1)

            def gate_sigmoids(c):
                for t in (c, DC + c):
                    act.wait_ge(S["gate_out"], t + 1)
                    act.activation(gates[:, t, :], gates[:, t, :], ACT.Sigmoid, bias=b_gate[:, t:t + 1]
                                   ).then_inc(S["gate_sig"], 1)

            for c in range(2):
                gate_sigmoids(c)
            act.wait_ge(S["asc_mm"], TT * AQ)
            act.dma_start(ffn_row[:], ffn_g.to_broadcast([P, D])).then_inc(S["ffn_in"], 16)
            act.dma_start(acc[:], x.rearrange("(t p) d -> p t d", p=P)).then_inc(S["acc_in"], 16)
            for c in range(DC):
                split_hi(T_BRANCH + c + 2, c % 2)
                if c + 2 < DC:
                    gate_sigmoids(c + 2)
                act.wait_ge(S["br_f"], c + 1)
                act.activation(m["hi"][:, c, :], mtmp[:, c % 2, 0, :], ACT.Copy).then_inc(S["m_hi"], 1)
            for c in range(DC):
                n = T_OUT + c + 2
                half = slice((n - T_KEYS) * RH, (n - T_KEYS + 1) * RH)
                split_hi(n, c % 2, None if n < T_KEYS else keys["hi"][:, half, :].rearrange("p r n -> p (r n)"))
            for tt in range(TT + 1):
                if tt < TT:
                    act.wait_ge(S["acc_ok"], 2 * tt + 2)
                    need(act, S["ss_ok"], tt - 1)
                    act.activation(ysq[:, tt % 2, :], acc[:, tt, :], ACT.Square,
                                   accum_out=rowstat[:, 0, tt:tt + 1]).then_inc(S["ss_ok"], 1)
                    act.wait_ge(S["ss_ok"], tt + 1)
                    act.activation(rowstat[:, 1, tt:tt + 1], rowstat[:, 0, tt:tt + 1], ACT.Sqrt, bias=eps[:],
                                   scale=1.0 / D).then_inc(S["ysd_ok"], 1)
                for n in (2 * tt - 2, 2 * tt - 1) if tt else ():
                    act.wait_ge(S["ht_mm"], n + 1)
                    act.activation(turned_hT("hi", n), ps[:, n, :].rearrange("p (c t) -> p c t", c=4), ACT.Copy
                                   ).then_inc(S["ht_hi"], 1)
            split_hi(T_WQ, 0)
            split_hi(T_WQ + 1, 1)
            def u_split(n, k):
                act.wait_ge(u_in[k], (n - k) * 8 + 16)
                need(act, S["u_mm"], n - 1)
                act.activation(uw["hi"][:, k, :], uraw[:, k, :], ACT.Copy).then_inc(S["u_hi"], 1)

            for n in range(RS + 1):
                if n == RS:
                    act.wait_ge(S["w_used"], T_KEYS + RS)
                    u_split(0, 0)
                    u_split(1, 1)
                if n < RS:
                    act.wait_ge(S["w_used"], T_KEYS + n + 1)
                    need(act, S["s_mm"], n - 1)
                    act.activation(q2["hi"][:, n % 2, :], ps[:, n % 2, :], ACT.Copy).then_inc(S["q_hi"], 1)
                    if T_WQ + n + 2 < N_TILES:
                        split_hi(T_WQ + n + 2, n % 2)
                if n >= 1:
                    act.wait_ge(S["s_mm"], n)
                    need(act, S["s_used"], n - 2)
                    act.activation(score[:, (n - 1) % 2], ps[:, 2 + (n - 1) % 2, :].rearrange("p (t n) -> p t n", t=TT),
                                   ACT.Copy).then_inc(S["s_out"], 1)
            def early_gelu(n):
                g, b = n // GRP, n % GRP
                act.wait_ge(S["u_mm"], n + 1)
                if g >= 2 and b == 0:
                    act.wait_ge(early_out[g % 2], g // 2 * 16)
                act.activation(early[:, g % 2, b, :], ps[:, n % 2, :], ACT.Gelu).then_inc(S["gelu_ok"], 1)

            def spill(g):
                act.wait_ge(S["gelu_ok"], (g + 1) * GRP)
                act.dma_start(early_dram[g], early[:, g % 2].rearrange("p b t -> p (b t)")).then_inc(early_out[g % 2], 16)

            for n in range(NTOP):
                if n == 2:
                    act.wait_ge(S["tops_ok"], RS)
                    act.activation(top_f[:], top_i[:], ACT.Copy).then_inc(S["topf_ok"], 1)
                if n == NTOP - 1:
                    for q in (0, 2):
                        act.wait_ge(S["col_mm"], q + 1)
                        act.activation(cols[:, q, :], ps[:, 4 + q, :], ACT.Copy).then_inc(S["col_ok"], 1)
                u_split(n + 2, n % 2)
                early_gelu(n)
                if n % GRP == GRP - 1:
                    spill(n // GRP)
                if n == NTOP - 3:
                    act.wait_ge(S["soft"], 1)
                    act.activation(gate[:], best[:], ACT.Exp).then_inc(S["soft_exp"], 1)

            def pieces(it):
                for c in range(2):
                    if not (isinstance(it, int) and it * 2 + c == 0):
                        k = 1 - c
                        act.wait_ge(S["u_mm"], it * 2 + (NTOP + c))
                        act.activation(early[:].rearrange("p s b t -> p (s b) t")[:, bass.ds(it * 2 + (c - 1), 1), :],
                                       ps[:, k:k + 1, :], ACT.Gelu).then_inc(S["gelu_ok"], 1)
                        act.wait_ge(u_in[k], it * 16 + (NTOP + 2 * c) * 8 + 16)
                        act.activation(uw["hi"][:, k, :], uraw[:, k, :], ACT.Copy).then_inc(S["u_hi"], 1)
                    for q in range(GT // 4):
                        act.wait_ge(S["g_mm"], it * (2 * GT // 4) + (c * (GT // 4) + q + 1))
                        if q == 0:
                            need(act, g_store[c], it * 16)
                        act.activation(piece[:, c, :, q * 4:q * 4 + 4].rearrange("p i t -> p t i"),
                                       ps[:, 4 + q % 4, :].rearrange("p (t i) -> p t i", t=4), ACT.Copy).then_inc(S["g_out"], 1)

            for k in range(2):
                act.wait_ge(early_out[k], EARLY_TOP // 2 * 16)
            pieces(0)
            with act.Fori(1, NPIECE // 2 - 1, 1) as it:
                pieces(it)
            spill(EARLY_TOP)
            pieces(NPIECE // 2 - 1)
            early_gelu(NLAST - 1)
            u_split(NLAST + 1, 1)

            def early_block(it, s, b):
                n = it * 2 * GRP + (s * GRP + b)
                if b == 0:
                    act.wait_ge(S["v_in"], it * 32 + (s * 16 + 16))
                need(act, S["early_mm"], it * 2 * GRP + (s * GRP + b - GRP + 1))
                act.activation(vw["hi"][:, b, :], vraw[:, b, :], ACT.Copy).then_inc(S["v_hi"], 1)
                act.wait_ge(S["prod_ok"], n + 1)
                act.activation(act_w["hi"][:, s, b, :], prod[:, b % 2, :], ACT.Copy).then_inc(S["aw_hi"], 1)

            for n in range(NLAST, NEARLY):
                if n >= NEARLY - GRP:
                    if n == NEARLY - GRP:
                        for k in range(2):
                            act.wait_ge(g_store[k], 16 * NPIECE // 2)
                    early_block(0, 0, n - (NEARLY - GRP))
                if n < NEARLY - 1:
                    act.wait_ge(S["u_lo"], n + 2)
                    act.dma_start(uraw[:, (n + 3) % 2, :], uT[n + 3]).then_inc(u_in[(n + 3) % 2], 16)
                if n == NLAST:
                    spill(SPILLED - 1)
                u_split(n + 2, n % 2)
                early_gelu(n)

            def v_split(g, b):
                if b == 0:
                    act.wait_ge(S["v_in"], g * 16 + 16)
                    act.wait_ge(S["o2_mm"], g * 8 - 8 * (EARLY - 1))
                act.activation(vw["hi"][:, b, :], vraw[:, b, :], ACT.Copy).then_inc(S["v_hi"], 1)

            def period(g, s, more_u=True, first=False):
                for b in range(GRP):
                    n = g * GRP + b
                    for vb in V_SPLITS[b] if not first else ():
                        v_split(g - 1, vb)
                    if more_u or b < 2:
                        u_split(n + 2, b % 2)
                    act.wait_ge(S["u_mm"], n + 1)
                    need(act, S["prod_ok"], n - 1)
                    act.activation(gelu[:, b % 2, :], ps[:, b % 2, :], ACT.Gelu).then_inc(S["gelu_ok"], 1)
                    act.wait_ge(S["prod_ok"], n + 1)
                    if b == 0:
                        need(act, S["o2_mm"], g * 8 - 8 * EARLY)
                    act.activation(act_w["hi"][:, s, b, :], prod[:, b % 2, :], ACT.Copy).then_inc(S["aw_hi"], 1)

            for b in range(GRP):
                early_block(0, 1, b)
            with act.Fori(1, EARLY // 2, 1) as it:
                for s in range(2):
                    for b in range(GRP):
                        early_block(it, s, b)
            act.wait_ge(S["early_mm"], NEARLY - GRP)
            period(EARLY, 0, first=True)
            period(EARLY + 1, 1)
            with act.Fori(EARLY // 2 + 1, NGRP // 2 - 1, 1) as it:
                period(it * 2, 0)
                period(it * 2 + 1, 1)
            period(NGRP - 2, 0)
            period(NGRP - 1, 1, more_u=False)
            act.wait_ge(S["v_in"], NGRP * 16)
            for b in range(GRP):
                act.wait_ge(S["final_mm"], b + 1)
                act.activation(vw["hi"][:, b, :], vraw[:, b, :], ACT.Copy).then_inc(S["v_hi"], 1)
            for tt in range(TT):
                act.wait_ge(S["o2_out"], (NGRP - 2 - (EARLY - 1)) * 8 + 2 * tt + 2)
                need(act, S["fss_ok"], tt)
                act.activation(gelu[:].rearrange("p s t -> p (s t)"), acc[:, tt, :], ACT.Square,
                               accum_out=rowstat[:, 0, tt:tt + 1]).then_inc(S["fss_ok"], 1)
                act.wait_ge(S["fss_ok"], tt + 1)
                act.activation(rowstat[:, 1, tt:tt + 1], rowstat[:, 0, tt:tt + 1], ACT.Sqrt, bias=eps[:],
                               scale=1.0 / D).then_inc(S["fsd_ok"], 1)

        @block.vector
        def _(dve):
            chain = Chain(dve, vec)
            dve.wait_ge(S["w_hi"], 1)
            dve.tensor_tensor(w["lo"][:, 0, :], raw[:, 0, :], w["hi"][:, 0, :].bitcast(F32),
                              ALU.subtract).then_inc(S["w_lo"], 1)
            dve.wait_ge(S["par_in"], 32)
            for c in range(DC):
                dve.wait_ge(S["yhi_ok"], c + 1)
                dve.scalar_tensor_tensor(out=y["lo"][:, c, :], in0=xt[:, c, :], scalar=mix_g[:, c:c + 1],
                                         in1=y["hi"][:, c, :].bitcast(F32), op0=ALU.mult, op1=ALU.subtract
                                         ).then_inc(S["y_ok"], 1)
            chain.done(dve.tensor_tensor(lbw[:, 0], lb_logits[:, 0], lb_logits[:, 1], ALU.max))
            for r in range(2):
                ins = dve.tensor_tensor(lbw[:, 1 + r], lb_logits[:, r], lbw[:, 0], ALU.subtract)
            ins.then_inc(S["lb_max"], 1)
            dve.wait_ge(S["sd_ok"], 2)
            dve.reciprocal(rstd[:], sd[:]).then_inc(S["rstd_ok"], 1)
            dve.reciprocal(meta_sd[:, 1:2], meta_sd[:, 0:1]).then_inc(S["rstd_ok"], 1)
            dve.wait_ge(S["lb_exp"], 1)
            chain.done(dve.tensor_tensor(lbw[:, 1], lbw[:, 3], lbw[:, 4], ALU.add))
            chain.done(dve.reciprocal(lbw[:, 2], lbw[:, 1]))
            chain.done(dve.tensor_tensor(lbw[:, 0], lbw[:, 3], lbw[:, 2], ALU.mult))
            chain.done(dve.tensor_scalar(lbw[:, 5], lbw[:, 0], -1.0, 1.0, ALU.mult, ALU.add))
            dve.wait_ge(S["f_sig"], 1)
            for h in range(HH):
                ins = dve.tensor_scalar(f_z[:, h, :], f_z[:, h, :], lbw[:, 5, h:h + 1], lbw[:, 0, h:h + 1],
                                        ALU.mult, ALU.add)
            chain.done(ins)
            chain.done(dve.tensor_scalar(kk[:], f_z, -1.0, 1.0, ALU.mult, ALU.add))
            halves = lambda ap: ap.rearrange("p h (b i) -> p (h b) i", i=HALF)
            flat = lambda ap: ap.rearrange("p h l -> p (h l)")
            chain.done(dve.memset(starts[:], 0.0))
            chain.done(dve.tensor_copy(halves(starts[:])[:, :, 0:1], halves(f_z)[:, :, 0:1]))
            chain.done(dve.memset(halves(f_z)[:, :, 0:1], 0.0))
            chain.done(dve.tensor_tensor_scan(flat(decay[:]), flat(f_z), flat(starts[:]), 0.0, ALU.mult, ALU.add))
            chain.done(dve.tensor_scalar(decay[:], decay[:], TINY, None, ALU.max))
            chain.done(dve.reciprocal(inv[:], decay[:]))
            chunks = lambda ap: ap.rearrange("p (c i) -> p c i", i=CH)
            at_mid = lambda ap: chunks(ap)[:, :, HALF - 1:HALF].to_broadcast([P, NCH, HALF])
            dve.wait_ge(S["z_out"], 8)
            chain.done(dve.tensor_tensor(q_z, q_z, decay[:, :, META:LEN], ALU.mult))
            for h in range(HH):
                part = chunks(q_z[:, h, :])[:, :, 0:HALF]
                ins = dve.tensor_tensor(part, part, at_mid(inv[:, h, META:LEN]), ALU.mult)
            chain.done(ins)
            chain.done(dve.tensor_tensor(kk[:], kk[:], inv[:], ALU.mult))
            for h in range(HH):
                part = chunks(kk[:, h, META:LEN])[:, :, 0:HALF]
                ins = dve.tensor_tensor(part, part, at_mid(decay[:, h, META:LEN]), ALU.mult)
            chain.done(ins)
            for h in range(HH):
                ends = decay[:, h, :].rearrange("p (b i) -> p b i", i=HALF)[:, :, HALF - 1]
                ins = dve.tensor_tensor(ecol[:, h, :], ends[:, 0:NBLK - 1:2], ends[:, 1:NBLK:2], ALU.mult)
            chain.done(ins)
            for h in range(HH):
                ins = dve.tensor_tensor(chunks(qi[:, h, :]), chunks(q_z[:, h, :]),
                                        ecol[:, h, :].unsqueeze(2).to_broadcast([P, NCH, CH]), ALU.mult)
            ins.then_inc(S["hg_ok"], 1)
            for n in range(0, 10, 2):
                dve.wait_ge(S["tr_mm"], n + 1)
                dve.tensor_copy(transposed_dst(n), transposed_src(n)).then_inc(S["tr_out_v"], 1)
            dve.wait_ge(S["upd_mm"], 1)
            dve.tensor_copy(state[:, 0, :], ps[:, 4, :]).then_inc(S["state_ok"], 1)
            for c in range(NCH):
                if c * CH % P == 0:
                    tt = c * CH // P
                    dve.wait_ge(S["wsc_mm"], tt + 1)
                    need(dve, S["o_mm"], (tt - 1) * P // CH)
                    for r in range(P // CH):
                        own = slice(r * CH, (r + 1) * CH)
                        ins = dve.tensor_tensor(within[own, tt % 2, :, own],
                                                ps[own, 6 + tt % 2, 0:HH * CH].rearrange("p (h t) -> p h t", h=HH),
                                                chunkmask[own].unsqueeze(1).to_broadcast([CH, HH, CH]), ALU.mult)
                    ins.then_inc(S["within_ok"], 1)
                if c < NCH - 1:
                    dve.wait_ge(S["upd_mm"], c + 2)
                    dve.wait_ge(S["state_ok"], c + 1)
                    need(dve, S["o_mm"], c - 2)
                    for h in range(HH):
                        head = slice(h * P, (h + 1) * P)
                        ins = dve.scalar_tensor_tensor(out=state[:, (c + 1) % 4, head], in0=state[:, c % 4, head],
                                                       scalar=ecol[:, h, c:c + 1], in1=ps[:, 4 + (c + 1) % 2, head],
                                                       op0=ALU.mult, op1=ALU.add)
                    ins.then_inc(S["state_ok"], 1)
            dve.wait_ge(S["og_sig"], 1)
            for h in range(HH):
                ins = dve.scalar_tensor_tensor(out=og_z[:, h, :], in0=og_z[:, h, :], scalar=hg_g[:, h:h + 1],
                                               in1=orstd[:, h, :], op0=ALU.mult, op1=ALU.mult)
            ins.then_inc(S["og_used"], 1)
            dve.wait_ge(S["og_used"], 1)
            dve.wait_ge(S["o_out"], TT)
            chain.done(dve.tensor_tensor(og_z, og_z, o_hg[:], ALU.mult))

            def logits(n):
                s, lo = n % 2, P if n < AQ else 0
                dve.wait_ge(S["asc_mm"], n + 1)
                need(dve, S["aexp"], n - 1)
                head = n % 2 * 4 + n % AQ // 2
                dve.tensor_copy(atsc[:, s, KEYS:KEYS + 1], sink[:, head:head + 1])
                chain.done(dve.scalar_tensor_tensor(out=atsc[:, s, lo:KEYS], in0=ps[:, 6 + s, lo:KEYS],
                                                    scalar=HD ** -0.5, in1=bandmask[:, lo:KEYS],
                                                    op0=ALU.mult, op1=ALU.add))
                dve.tensor_reduce(atstat[:, 0, s:s + 1], atsc[:, s, lo:KEYS + 1], AX_X, ALU.max,
                                  negate=True).then_inc(S["amax"], 1)

            def normalise(n):
                s, lo = n % 2, P if n < AQ else 0
                dve.wait_ge(S["aexp"], n + 1)
                chain.done(dve.reciprocal(atstat[:, 2, s:s + 1], atstat[:, 1, s:s + 1]))
                dve.tensor_scalar(atp[:, s, lo:KEYS], atp[:, s, lo:KEYS], atstat[:, 2, s:s + 1], None,
                                  ALU.mult).then_inc(S["anorm"], 1)

            def attention_lo(tt):
                own = slice(tt * P, (tt + 1) * P)
                dve.wait_ge(S["oat_hi"], tt + 1)
                dve.tensor_tensor(oat["lo"][:, :, own], ps[:, tt % 2, :].rearrange("p (c t) -> p c t", c=4),
                                  oat["hi"][:, :, own].bitcast(F32), ALU.subtract).then_inc(S["oat_ok"], 1)

            dve.wait_ge(S["consts"], 1)
            for n in range(TT * AQ + 1):
                if n >= 1:
                    normalise(n - 1)
                if n < TT * AQ:
                    logits(n)
                if 1 <= n <= HH * TT:
                    h, own = (n - 1) // TT, slice((n - 1) % TT * P, ((n - 1) % TT + 1) * P)
                    dve.wait_ge(S["osd_ok"], h + 1)
                    chain.done(dve.reciprocal(orstd[:, h, own], orstd[:, h, own]))
                    dve.tensor_tensor(o_hg[:, h, own], og_z[:, h, own], orstd[:, h, own], ALU.mult).then_inc(S["ohg_f"], 1)
                if HH * TT + 4 <= n < HH * TT + 4 + HH:
                    h = n - (HH * TT + 4)
                    dve.wait_ge(S["ohg_hi"], h + 1)
                    dve.tensor_tensor(ohg["lo"][:, h, :], o_hg[:, h, :], ohg["hi"][:, h, :].bitcast(F32),
                                      ALU.subtract).then_inc(S["ohg_ok"], 1)
                if n > AQ and n % AQ == 2:
                    attention_lo(n // AQ - 1)
            attention_lo(TT - 1)

            dve.wait_ge(S["ohg_ok"], HH)
            for c in range(DC):
                s = c % 2
                dve.wait_ge(S["w_used"], T_BRANCH + c + 1)
                need(dve, S["m_ok"], c - 1)
                dve.wait_ge(S["gate_sig"], 2 * (c + 1))
                dve.tensor_tensor(mtmp[:, s, 0, :], gates[:, c, :], ps[:, 2 * s, :], ALU.mult)
                chain.done(dve.tensor_tensor(mtmp[:, s, 1, :], gates[:, DC + c, :], ps[:, 2 * s + 1, :], ALU.mult))
                dve.tensor_tensor(mtmp[:, s, 0, :], mtmp[:, s, 0, :], mtmp[:, s, 1, :], ALU.add).then_inc(S["br_f"], 1)
                dve.wait_ge(S["m_hi"], c + 1)
                dve.tensor_tensor(m["lo"][:, c, :], mtmp[:, s, 0, :], m["hi"][:, c, :].bitcast(F32),
                                  ALU.subtract).then_inc(S["m_ok"], 1)
            dve.wait_ge(S["acc_in"], 16)
            dve.wait_ge(S["ffn_in"], 16)
            for tt in range(TT + 2):
                for n in (2 * tt, 2 * tt + 1) if tt < TT else ():
                    if n < 2 * TT - 1:
                        dve.wait_ge(S["acc_mm"], n + 1)
                    else:
                        dve.wait_ge(S["w_used"], T_OUT + DC)
                    own = acc[:, n // 2, n % 2 * 512:(n % 2 + 1) * 512]
                    dve.tensor_tensor(own, own, ps[:, n, :], ALU.add).then_inc(S["acc_ok"], 1)
                if 1 <= tt <= TT:
                    dve.wait_ge(S["ysd_ok"], tt)
                    chain.done(dve.reciprocal(rowstat[:, 2, tt - 1:tt], rowstat[:, 1, tt - 1:tt]))
                    dve.scalar_tensor_tensor(out=ynat[:, tt - 1, :], in0=acc[:, tt - 1, :], scalar=rowstat[:, 2, tt - 1:tt],
                                             in1=ffn_row[:], op0=ALU.mult, op1=ALU.mult).then_inc(S["ynat_ok"], 1)
                for n in (2 * tt - 4, 2 * tt - 3) if tt >= 2 else ():
                    dve.wait_ge(S["ht_hi"], n + 1)
                    dve.tensor_tensor(turned_hT("lo", n), ps[:, n, :].rearrange("p (c t) -> p c t", c=4),
                                      turned_hT("hi", n).bitcast(F32), ALU.subtract).then_inc(S["ht_ok"], 1)

            def set_tops(n):
                s = n % 2
                dve.wait_ge(S["s_out"], n + 1)
                for tt in range(TT):
                    ins = dve.max(top_v[:, tt, n, 0:8], score[:, s, tt, :])
                chain.done(ins)
                for tt in range(TT):
                    dve.max_index(top_i[:, tt, n, 0:8], top_v[:, tt, n, 0:8], score[:, s, tt, :])
                for tt in range(TT):
                    ins = dve.match_replace(scut[:, s, tt, :], top_v[:, tt, n, 0:8], score[:, s, tt, :], LOWEST)
                ins.then_inc(S["s_used"], 1)
                dve.wait_ge(S["s_used"], n + 1)
                for tt in range(TT):
                    ins = dve.max(top_v[:, tt, n, 8:16], scut[:, s, tt, :])
                chain.done(ins)
                for tt in range(TT):
                    ins = dve.max_index(top_i[:, tt, n, 8:16], top_v[:, tt, n, 8:16], scut[:, s, tt, :])
                ins.then_inc(S["tops_ok"], 1)

            for n in range(RS + 1):
                if n < RS:
                    dve.wait_ge(S["q_hi"], n + 1)
                    dve.tensor_tensor(q2["lo"][:, n % 2, :], ps[:, n % 2, :], q2["hi"][:, n % 2, :].bitcast(F32),
                                      ALU.subtract).then_inc(S["q_ok"], 1)
                if n >= 1:
                    set_tops(n - 1)
            tv = top_v[:].rearrange("p t (h c) a -> p (t h) c a", c=2)
            a = 0
            while a < TOP:
                same = PAIRS.count(PAIRS[a])
                wide = PAIRS[a]
                dst = cand[:, :, STARTS[a]:STARTS[a] + same * wide].rearrange("p n (a b) -> p n a b", b=wide)
                ins = dve.tensor_tensor(dst, tv[:, :, 0, a:a + same].unsqueeze(3).to_broadcast([P, TT * RH, same, wide]),
                                        tv[:, :, 1, 0:wide].unsqueeze(2).to_broadcast([P, TT * RH, same, wide]), ALU.add)
                a += same
            chain.done(ins)
            bests = best[:].rearrange("p t h k -> p (t h) k")
            for n in range(TT * RH):
                ins = dve.max(bests[:, n, 0:8], cand[:, n, :])
            chain.done(ins)
            for n in range(TT * RH):
                dve.max_index(pos_u[:, n, 0:8], bests[:, n, 0:8], cand[:, n, :])
            for n in range(TT * RH):
                ins = dve.match_replace(ccut[:, n, :], bests[:, n, 0:8], cand[:, n, :], LOWEST)
            chain.done(ins)
            for n in range(TT * RH):
                ins = dve.max(bests[:, n, 8:16], ccut[:, n, :])
            chain.done(ins)
            for n in range(TT * RH):
                ins = dve.max_index(pos_u[:, n, 8:16], bests[:, n, 8:16], ccut[:, n, :])
            chain.done(ins)
            dve.tensor_copy(pos[:].rearrange("p t h k -> p (t h) k"), pos_u[:]).then_inc(S["pos_ok"], 1)
            chain.done(dve.tensor_copy(tot[:, 0, :], bests[:, :, 0]))
            dve.tensor_tensor(bests, bests, tot[:, 0, :].unsqueeze(2).to_broadcast([P, TT * RH, TOP]),
                              ALU.subtract).then_inc(S["soft"], 1)
            dve.wait_ge(S["pos_ok"], 1)
            chain.done(dve.tensor_copy(posb[:], pos[:]))
            for a in range(1, TOP):
                chain.done(dve.tensor_scalar(tmp_j[:], pos[:], float(STARTS[a]), float(PAIRS[a - 1]), ALU.is_ge, ALU.mult))
                chain.done(dve.tensor_tensor(posb[:], posb[:], tmp_j[:], ALU.subtract))
            dve.wait_ge(S["step_ok"], 1)
            chain.done(dve.tensor_copy(ej[:], key_step(1, 0)))
            for b in range(1, TOP):
                chain.done(dve.scalar_tensor_tensor(out=tmp_j[:], in0=posb[:], scalar=float(b), in1=key_step(1, b),
                                                    op0=ALU.is_ge, op1=ALU.mult))
                chain.done(dve.tensor_tensor(ej[:], ej[:], tmp_j[:], ALU.add))
            chain.done(dve.scalar_tensor_tensor(out=ei_high[:], in0=pos[:], scalar=float(STARTS[EI_POOL]),
                                                in1=key_step(0, EI_POOL), op0=ALU.is_ge, op1=ALU.mult))
            for a in range(EI_POOL + 1, TOP):
                chain.done(dve.scalar_tensor_tensor(out=tmp_j[:], in0=pos[:], scalar=float(STARTS[a]), in1=key_step(0, a),
                                                    op0=ALU.is_ge, op1=ALU.mult))
                chain.done(dve.tensor_tensor(ei_high[:], ei_high[:], tmp_j[:], ALU.add))
            dve.wait_ge(S["ei_ok"], 1)
            dve.tensor_tensor(ei[:], ei[:], ei_high[:], ALU.add).then_inc(S["ei_ok"], 1)
            dve.wait_ge(S["soft_exp"], 1)
            gs = gate[:].rearrange("p t h k -> p (t h) k")
            chain.done(dve.tensor_reduce(tot[:, 0, :], gs, AX_X, ALU.add))
            chain.done(dve.reciprocal(tot[:, 1, :], tot[:, 0, :]))
            dve.tensor_tensor(gs, gs, tot[:, 1, :].unsqueeze(2).to_broadcast([P, TT * RH, TOP]),
                              ALU.mult).then_inc(S["gate_ok"], 1)
            dve.wait_ge(S["col_mm"], 2)
            dve.tensor_copy(cols[:, 1, :], ps[:, 5, :]).then_inc(S["col_ok"], 1)

            def one_hot(it):
                for s in range(4):
                    n = it * 4 + s
                    own = bass.ds(n * BATCH, BATCH)
                    spread = lambda q: cols[:, q, own].unsqueeze(2).to_broadcast([P, BATCH, NK])
                    every = iota[:].unsqueeze(1).to_broadcast([P, BATCH, NK])
                    need(dve, S["hotg_ok"], it * 4 + (s - 1))
                    dve.tensor_tensor(hot_j[:, s % 2], every, spread(1), ALU.is_equal).then_inc(S["hotj_ok"], 1)
                    need(dve, S["g_mm"], it * 8 + (2 * s - 2))
                    dve.tensor_tensor(hot_i[:, s % 2], every, spread(0), ALU.is_equal).then_inc(S["hoti_ok"], 1)

            dve.wait_ge(S["col_ok"], 3)
            one_hot(0)
            with dve.Fori(1, TOK // BATCH // 4, 1) as it:
                one_hot(it)

            def u_split(n, k):
                dve.wait_ge(S["u_hi"], n + 1)
                dve.tensor_tensor(uw["lo"][:, k, :], uraw[:, k, :], uw["hi"][:, k, :].bitcast(F32),
                                  ALU.subtract).then_inc(S["u_lo"], 1)

            def v_split(g, b):
                dve.wait_ge(S["v_hi"], g * GRP + (b + 1))
                dve.tensor_tensor(vw["lo"][:, b, :], vraw[:, b, :], vw["hi"][:, b, :].bitcast(F32),
                                  ALU.subtract).then_inc(S["v_lo"], 1)

            def group(g, s, more_u=True, first=False):
                for b in range(GRP):
                    n = g * GRP + b
                    for vb in V_SPLITS[b] if not first else ():
                        v_split(g - 1, vb)
                    if more_u or b < 2:
                        u_split(n + 2, b % 2)
                    if b == 0:
                        dve.wait_ge(gm_in[s], g * 8 + (16 - 8 * s))
                    dve.wait_ge(S["gelu_ok"], n + 1)
                    need(dve, S["aw_ok"], n - 1)
                    dve.tensor_tensor(prod[:, b % 2, :].rearrange("p (c t) -> p c t", c=NPIECE),
                                      gelu[:, b % 2, :].rearrange("p (c t) -> p c t", c=NPIECE),
                                      gmat[:, s, :, b, :], ALU.mult).then_inc(S["prod_ok"], 1)
                    dve.wait_ge(S["aw_hi"], n + 1)
                    dve.tensor_tensor(act_w["lo"][:, s, b, :], prod[:, b % 2, :], act_w["hi"][:, s, b, :].bitcast(F32),
                                      ALU.subtract).then_inc(S["aw_ok"], 1)

            def add_up(g):
                for j in range(8):
                    own = acc[:, j // 2, j % 2 * 512:(j % 2 + 1) * 512]
                    dve.wait_ge(S["o2_mm"], g * 8 + (j + 1 - 8 * (EARLY - 1)))
                    dve.tensor_tensor(own, own, ps[:, 2 + j % 4, :], ALU.add).then_inc(S["o2_out"], 1)

            def early_groups(it):
                for s in range(2):
                    for b in range(GRP):
                        n = it * 2 * GRP + (s * GRP + b)
                        dve.wait_ge(S["v_hi"], n + 1)
                        dve.tensor_tensor(vw["lo"][:, b, :], vraw[:, b, :], vw["hi"][:, b, :].bitcast(F32),
                                          ALU.subtract).then_inc(S["v_lo"], 1)
                        if b == 0:
                            dve.wait_ge(gm_in[s], it * 16 + 16)
                            if isinstance(it, int):
                                dve.wait_ge(S["gelu_ok"], NLAST + (s + 1) * GRP)
                            else:
                                dve.wait_ge(S["early_in"], it * 32 + (s - 1) * 16)
                        need(dve, S["aw_ok"], it * 2 * GRP + (s * GRP + b - 1))
                        dve.tensor_tensor(prod[:, b % 2, :].rearrange("p (c t) -> p c t", c=NPIECE),
                                          early[:, s, b, :].rearrange("p (c t) -> p c t", c=NPIECE),
                                          gmat[:, s, :, b, :], ALU.mult).then_inc(S["prod_ok"], 1)
                        dve.wait_ge(S["aw_hi"], n + 1)
                        dve.tensor_tensor(act_w["lo"][:, s, b, :], prod[:, b % 2, :],
                                          act_w["hi"][:, s, b, :].bitcast(F32), ALU.subtract).then_inc(S["aw_ok"], 1)

            early_groups(0)
            with dve.Fori(1, EARLY // 2, 1) as it:
                early_groups(it)
            dve.wait_ge(S["u_lo"], NEARLY + 2)
            for j in range(8):
                own = acc[:, j // 2, j % 2 * 512:(j % 2 + 1) * 512]
                dve.wait_ge(S["o2_mm"], j + 1)
                dve.tensor_tensor(own, own, ps[:, j, :], ALU.add).then_inc(S["o2_out"], 1)
            group(EARLY, 0, first=True)
            with dve.Fori(EARLY // 2, NGRP // 2 - 1, 1) as it:
                group(it * 2 + 1, 1)
                add_up(it * 2)
                group(it * 2 + 2, 0)
                add_up(it * 2 + 1)
            group(NGRP - 1, 1, more_u=False)
            for b in range(GRP):
                v_split(NGRP - 1, b)
            dve.wait_ge(S["fin_in"], 16)
            for tt in range(TT + 1):
                for j in (2 * tt, 2 * tt + 1) if tt < TT else ():
                    own = acc[:, tt, j % 2 * 512:(j % 2 + 1) * 512]
                    dve.wait_ge(S["o2_mm"], (NGRP - 2 - (EARLY - 1)) * 8 + j + 1)
                    dve.tensor_tensor(own, own, ps[:, j, :], ALU.add).then_inc(S["o2_out"], 1)
                if tt >= 1:
                    dve.wait_ge(S["fsd_ok"], tt)
                    chain.done(dve.reciprocal(rowstat[:, 2, tt - 1:tt], rowstat[:, 1, tt - 1:tt]))
                    dve.scalar_tensor_tensor(out=fin_o[:, tt - 1, :], in0=acc[:, tt - 1, :], scalar=rowstat[:, 2, tt - 1:tt],
                                             in1=fin_g[:], op0=ALU.mult, op1=ALU.mult).then_inc(S["fin_ok"], 1)

        @block.tensor
        def _(pe):
            def three(dst, lhs, rhs, first, last):
                for i, (a, b) in enumerate(SPLIT):
                    ins = pe.matmul(dst, lhs[a], rhs[b], start=first and i == 0, stop=last and i == 2)
                return ins

            def parts(t, *index):
                return {k: t[k].__getitem__((slice(None),) + index) for k in t}

            def project(k, rhs, dst):
                for c in range(DC):
                    own = parts(rhs, c, slice(META, LEN)) if rhs is y else parts(rhs, c)
                    ins = three(dst, parts(w, k, slice(c * P, (c + 1) * P)), own, c == 0, c == DC - 1)
                return ins

            def z_pair(it, meta=None):
                for k in range(2):
                    pe.wait_ge(S["w_lo"], it * 2 + (k + 1))
                    need(pe, S["z_copied"], it * 2 + (k - 1))
                    if isinstance(it, int) and it == k == 0:
                        pe.wait_ge(S["consts"], 1)
                        for c in range(DC):
                            pe.wait_ge(S["y_ok"], c + 1)
                            ins = three(ps[:, 0, :], parts(w, 0, slice(c * P, (c + 1) * P)), parts(y, c, slice(META, LEN)),
                                        c == 0, c == DC - 1)
                            pe.wait_ge(S["xsq_ok"], c + 1)
                            pe.matmul(ps[:, 4, :], ones[:], xsq[:, c, META:LEN], start=c == 0, stop=c == DC - 1)
                            ins = pe.matmul(ps[0:META, 5, 0:1], xsq[:, c, 0:META], ones[:, 0:1],
                                            start=c == 0, stop=c == DC - 1)
                        ins.then_inc(S["xsum_ok"], 1)
                    else:
                        ins = project(k, y, ps[:, k, :])
                    if meta is not None:
                        need(pe, S["zn_out"], it * 2 + (k - 1 - meta))
                        for c in range(DC):
                            ins = three(ps[0:META, 2 + k, 0:P], parts(y, c, slice(0, META)),
                                        parts(w, k, slice(c * P, (c + 1) * P)), c == 0, c == DC - 1)
                    ins.then_inc(S["w_used"], 1)

            def turn_meta(blocks, bank):
                for q, n in enumerate(blocks):
                    ins = pe.transpose(ps[:, bank, q * META:(q + 1) * META], znat[:, n, :], ident[0:META, 0:META])
                ins.then_inc(S["mt_mm"], 1)

            z_pair(0, meta=0)
            z_pair(1, meta=0)
            pe.wait_ge(S["zn_out"], 4)
            turn_meta(range(4), 4)
            with pe.Fori(2, 4, 1) as it:
                z_pair(it)
            with pe.Fori(4, 7, 1) as it:
                z_pair(it, meta=4)
            pe.wait_ge(S["zn_out"], Z_META)
            turn_meta([8], 5)
            with pe.Fori(7, N_Z // 2, 1) as it:
                z_pair(it)

            def gate_products(first, last):
                for i in range(first, last):
                    t, c, (a, b) = i // (3 * DC), i // 3 % DC, SPLIT[i % 3]
                    if i % (3 * DC) == 0:
                        pe.wait_ge(S["w_lo"], T_GATE + t + 1)
                        need(pe, S["gate_copied"], t - 1)
                    ins = pe.matmul(ps[:, 2 + t % 2, :], w[a][:, t % 2, c * P:(c + 1) * P], y[b][:, c, META:LEN],
                                    start=i % (3 * DC) == 0, stop=(i + 1) % (3 * DC) == 0)
                    if (i + 1) % (3 * DC) == 0:
                        ins.then_inc(S["w_used"], 1)

            pe.wait_ge(S["z_out"], 14)
            for n in range(10):
                need(pe, S["tr_out_s" if n % 2 else "tr_out_v"], n // 2)
                if n == 5:
                    pe.wait_ge(S["hg_ok"], 1)
                tile = lambda tt: slice(META + tt * P, META + (tt + 1) * P)
                if n < 4:
                    srcs = [v_z[:, h, tile(n)] for h in range(HH)]
                elif n == 4:
                    srcs = [av_z[:, tile(tt)] for tt in range(TT)]
                else:
                    srcs = [kk[:, h, tile(n - 5) if n < 9 else slice(0, META)] for h in range(HH)]
                rows = P if n < 9 else META
                for q, src in enumerate(srcs):
                    ins = pe.transpose(ps[0:rows, 2 + n % 2, q * P:(q + 1) * P], src, ident[:])
                ins.then_inc(S["tr_mm"], 1)
            for k in ("tr_out_v", "tr_out_s"):
                pe.wait_ge(S[k], 5)

            def chunk(c):
                return slice(c * CH, (c + 1) * CH)

            def rows(c):
                return slice(c * CH % P, c * CH % P + CH)

            def update(j):
                need(pe, S["state_ok"], j - 1)
                for h in range(HH):
                    head = slice(h * P, (h + 1) * P)
                    if j == 0:
                        k_, v_ = kmeta[:, head], vmeta[:, head]
                    else:
                        k_, v_ = (t[rows(j - 1), (j - 1) * CH // P, head] for t in (knat, vnat))
                    ins = pe.matmul(ps[:, 4 + j % 2, head], k_, v_, start=True, stop=True)
                ins.then_inc(S["upd_mm"], 1)

            update(0)
            for c in range(NCH):
                tt = c * CH // P
                if c * CH % P == 0:
                    need(pe, S["within_ok"], tt - 1)
                    for cc in range(c, c + P // CH):
                        for h in range(HH):
                            ins = pe.matmul(ps[rows(cc), 6 + tt % 2, h * CH:(h + 1) * CH],
                                            kk[:, h, META + cc * CH:META + (cc + 1) * CH], q_z[:, h, chunk(cc)],
                                            start=True, stop=True)
                    ins.then_inc(S["wsc_mm"], 1)
                if c < NCH - 1:
                    update(c + 1)
                if c * CH % P == 0:
                    pe.wait_ge(S["within_ok"], tt + 1)
                    need(pe, S["o_out"], tt - 1)
                    for h in range(HH):
                        pe.matmul(ps[:, tt % 2, h * P:(h + 1) * P], vnat[:, tt, h * P:(h + 1) * P],
                                  within[:, tt % 2, h, :], start=h == 0, stop=False)
                pe.wait_ge(S["state_ok"], c + 1)
                for h in range(HH):
                    head = slice(h * P, (h + 1) * P)
                    dst = ps[:, tt % 2, h * P + c * CH % P:h * P + c * CH % P + CH]
                    ins = pe.matmul(dst, state[:, c % 4, head], qi[:, h, chunk(c)], start=False,
                                    stop=h == HH - 1 and (c + 1) * CH % P == 0)
                ins.then_inc(S["o_mm"], 1)
                gate_products(c * GATES_HG, (c + 1) * GATES_HG)
            gate_products(NCH * GATES_HG, NCH * GATES_HG + GATES_MID)
            pe.wait_ge(S["osq_ok"], 1)
            for h in range(HH):
                need(pe, S["osd_ok"], h - 1)
                pe.matmul(ps[:, 4 + h % 2, :], ones[:], osq[:, h, :], start=True, stop=True).then_inc(S["osum_mm"], 1)

            pe.wait_ge(S["state_ok"], NCH)
            pe.wait_ge(S["o_out"], TT)
            pe.wait_ge(S["osd_ok"], HH)
            pe.wait_ge(S["mt_out"], 2)
            pe.wait_ge(S["z_out"], N_Z)

            def scores(n):
                tt, c, kv, s = n // AQ, n % AQ // 2, slice(n % 2 * HD, (n % 2 + 1) * HD), n % 2
                need(pe, S["amax"], n - 1)
                lo = P if tt == 0 else 0
                q_ = aq_z[kv, c, tt * P:(tt + 1) * P]
                pe.matmul(ps[:, 6 + s, lo:BAND], q_, ak_z[kv, META + (tt - 1) * P + lo:META + (tt + 1) * P],
                          start=True, stop=True)
                pe.matmul(ps[:, 6 + s, BAND:KEYS], q_, ak_z[kv, 0:META], start=True, stop=True).then_inc(S["asc_mm"], 1)

            def turn(n):
                tt, s = n // AQ, n % 2
                pe.wait_ge(S["anorm"], n + 1)
                need(pe, S["atr_out"], 2 * (n - 1))
                for q in range(0 if tt else 1, 2):
                    pe.transpose(ps[:, 4 + s, q * P:(q + 1) * P], atp[:, s, q * P:(q + 1) * P], ident[:])
                pe.transpose(ps[0:META, 4 + s, BAND:BAND + P], atp[:, s, BAND:KEYS], ident[:]).then_inc(S["atr_mm"], 1)

            def values(n):
                tt, c, kv, s = n // AQ, n % AQ // 2, slice(n % 2 * HD, (n % 2 + 1) * HD), n % 2
                pe.wait_ge(S["atr_out"], 2 * (n + 1))
                if n % AQ == 0:
                    need(pe, S["oat_ok"], tt - 1)
                dst = ps[kv, tt % 2, c * P:(c + 1) * P]
                if tt:
                    pe.matmul(dst, avnat[:, tt - 1, kv], atpT[:, s, 0:P], start=True, stop=False)
                pe.matmul(dst, avnat[:, tt, kv], atpT[:, s, P:BAND], start=tt == 0, stop=False)
                pe.matmul(dst, avmeta[:, kv], atpTm[:, s, :], start=False, stop=True).then_inc(S["apv_mm"], 1)

            for n in range(TT * AQ + 2):
                if n < TT * AQ:
                    scores(n)
                if 1 <= n <= TT * AQ:
                    turn(n - 1)
                if n >= 2:
                    values(n - 2)
                if n <= TT * AQ:
                    gate_products(gates_before(n), gates_before(n + 1))

            pe.wait_ge(S["ohg_ok"], HH)
            pe.wait_ge(S["oat_ok"], TT - 1)
            for c in range(DC):
                pe.wait_ge(S["w_lo"], T_BRANCH + c + 1)
                need(pe, S["br_f"], c - 1)
                if c == 1:
                    pe.wait_ge(S["gate_copied"], N_GATE)
                s = c % 2
                for side, src in enumerate((ohg, oat)):
                    if c == 0 and side == 1:
                        pe.wait_ge(S["oat_ok"], TT)
                    for q in range(4):
                        ins = three(ps[:, 2 * s + side, :], parts(w, s, slice((side * 4 + q) * P, (side * 4 + q + 1) * P)),
                                    parts(src, q), q == 0, q == 3)
                    if side == 0:
                        continue
                    ins.then_inc(S["w_used"], 1)
            for c in range(DC):
                pe.wait_ge(S["w_lo"], T_OUT + c + 1)
                pe.wait_ge(S["m_ok"], c + 1)
                for n in (4, 5, 6, 7, 0, 1, 2, 3) if c == 0 else range(2 * TT):
                    if c == n == 0:
                        pe.wait_ge(S["br_f"], DC)
                    ins = three(ps[:, n, :], parts(m, c, slice(n // 2 * P, (n // 2 + 1) * P)),
                                parts(w, c % 2, slice(n % 2 * 512, (n % 2 + 1) * 512)), c == 0, c == DC - 1)
                    if c == DC - 1 and n < 2 * TT - 1:
                        ins.then_inc(S["acc_mm"], 1)
                ins.then_inc(S["w_used"], 1)
            for tt in range(TT):
                pe.wait_ge(S["ynat_ok"], tt + 1)
                for c in range(DC):
                    ins = pe.transpose(ps[:, 2 * tt + c // 4, c % 4 * P:(c % 4 + 1) * P],
                                       ynat[:, tt, c * P:(c + 1) * P], ident[:])
                    if c % 4 == 3:
                        ins.then_inc(S["ht_mm"], 1)
            pe.wait_ge(S["ht_ok"], 2 * TT)
            for n in range(RS + 1):
                if n < RS:
                    pe.wait_ge(S["w_lo"], T_WQ + n + 1)
                    need(pe, S["q_ok"], n - 1)
                    project(n % 2, hT, ps[:, n % 2, :]).then_inc(S["w_used"], 1)
                if n >= 1:
                    r = n - 1
                    pe.wait_ge(S["q_ok"], n)
                    need(pe, S["s_out"], r - 1)
                    for tt in range(TT):
                        ins = three(ps[:, 2 + r % 2, tt * P:(tt + 1) * P], parts(q2, r % 2, slice(tt * P, (tt + 1) * P)),
                                    parts(keys, r), True, True)
                    ins.then_inc(S["s_mm"], 1)
            def u_block(n, k):
                pe.wait_ge(S["u_lo"], n + 1)
                need(pe, S["gelu_ok"], n - 1)
                for c in range(DC):
                    ins = three(ps[:, k, :], parts(uw, k, slice(c * P, (c + 1) * P)), parts(hT, c),
                                c == 0, c == DC - 1)
                ins.then_inc(S["u_mm"], 1)

            def u_group(g):
                for b in range(GRP):
                    u_block(g * GRP + b, b % 2)

            for n in range(NTOP - 1):
                u_block(n, n % 2)
            for q, (t, ok) in enumerate(((ei, "ei_ok"), (ej, None), (gate, "gate_ok"))):
                if q == 0:
                    pe.wait_ge(S["gate_ok"], 1)
                if ok:
                    pe.wait_ge(S[ok], 2 if q == 0 else 1)
                for tt in range(TT):
                    ins = pe.transpose(ps[:, 4 + q, tt * P:(tt + 1) * P],
                                       t[:, tt].rearrange("p h k -> p (h k)"), ident[:])
                ins.then_inc(S["col_mm"], 1)

            u_block(NTOP - 1, (NTOP - 1) % 2)

            def gate_matrices(it):
                for c in range(2):
                    for s in range(GT // BATCH):
                        batch = it * (2 * GT // BATCH) + (c * GT // BATCH + s)
                        pe.wait_ge(S["hotg_ok"], batch + 1)
                        pe.wait_ge(S["hoti_ok"], batch + 1)
                        for q in range(2):
                            bank = 4 + s % 2 * 2 + q
                            need(pe, S["g_out"], it * (2 * GT // 4) + (c * GT // 4 + 2 * s + q - 3))
                            for t in range(4):
                                ins = pe.matmul(ps[:, bank, t * P:(t + 1) * P], hot_g[:, s % 2, q * 4 + t, :],
                                                hot_i[:, s % 2, q * 4 + t, :], start=True, stop=True)
                            ins.then_inc(S["g_mm"], 1)
                        if s == 0:
                            pe.wait_ge(S["u_lo"], it * 2 + (NTOP + c + 1))
                            pe.wait_ge(S["gelu_ok"], it * 2 + (NTOP + c - 1))
                        ins = three(ps[:, c, :], parts(uw, c, slice(s * P, (s + 1) * P)), parts(hT, s), s == 0, s == DC - 1)
                        if s == DC - 1:
                            ins.then_inc(S["u_mm"], 1)

            pe.wait_ge(S["col_ok"], 3)
            gate_matrices(0)
            with pe.Fori(1, NPIECE // 2, 1) as it:
                gate_matrices(it)
            for g in range(NLAST // GRP, EARLY):
                u_group(g)
            pe.wait_ge(S["g_out"], TOK // 4)
            pe.wait_ge(S["gelu_ok"], NEARLY)

            def v_group(g, s):
                pe.wait_ge(S["aw_ok"], g * GRP + GRP)
                pe.wait_ge(S["v_lo"], g * GRP + GRP)
                for j in range(2 * TT):
                    pe.wait_ge(S["o2_out"], g * 8 + (j - 3 - 8 * (EARLY - 1)))
                    for b in range(GRP):
                        ins = three(ps[:, 2 + j % 4, :], parts(act_w, s, b, slice(j // 2 * P, (j // 2 + 1) * P)),
                                    parts(vw, b, slice(j % 2 * 512, (j % 2 + 1) * 512)), b == 0, b == GRP - 1)
                    ins.then_inc(S["o2_mm"], 1)

            def early_groups(it, first=False, last=False):
                for s in range(2):
                    for b in range(GRP):
                        n = it * 2 * GRP + (s * GRP + b)
                        start, end = first and s == 0 and b == 0, last and s == 1 and b == GRP - 1
                        pe.wait_ge(S["aw_ok"], n + 1)
                        pe.wait_ge(S["v_lo"], n + 1)
                        for j in range(2 * TT):
                            ins = three(ps[:, j, :], parts(act_w, s, b, slice(j // 2 * P, (j // 2 + 1) * P)),
                                        parts(vw, b, slice(j % 2 * 512, (j % 2 + 1) * 512)), start, end)
                            if end:
                                ins.then_inc(S["o2_mm"], 1)
                        if not end:
                            ins.then_inc(S["early_mm"], 1)

            early_groups(0, first=True)
            with pe.Fori(1, EARLY // 2 - 1, 1) as it:
                early_groups(it)
            early_groups(EARLY // 2 - 1, last=True)
            pe.wait_ge(S["o2_out"], 2)
            u_group(EARLY)
            u_group(EARLY + 1)
            v_group(EARLY, 0)
            with pe.Fori(EARLY // 2, NGRP // 2 - 2, 1) as it:
                u_group(it * 2 + 2)
                v_group(it * 2 + 1, 1)
                u_group(it * 2 + 3)
                v_group(it * 2 + 2, 0)
            u_group(NGRP - 2)
            v_group(NGRP - 3, 1)
            u_group(NGRP - 1)
            for n in range(2 * GRP):
                pe.wait_ge(S["aw_ok"], (NGRP - 2) * GRP + n + 1)
                pe.wait_ge(S["v_lo"], (NGRP - 2) * GRP + n + 1)
                if n == 0:
                    pe.wait_ge(S["gelu_ok"], NGRP * GRP)
                    pe.wait_ge(S["o2_out"], (NGRP - 2 - (EARLY - 1)) * 8)
                for j in range(2 * TT):
                    ins = three(ps[:, j, :], parts(act_w, n // GRP, n % GRP, slice(j // 2 * P, (j // 2 + 1) * P)),
                                parts(vw, n % GRP, slice(j % 2 * 512, (j % 2 + 1) * 512)), n == 0, n == 2 * GRP - 1)
                    if n == 2 * GRP - 1:
                        ins.then_inc(S["o2_mm"], 1)
                if n < 2 * GRP - 1:
                    ins.then_inc(S["final_mm"], 1)


def kernel(x, meta_tokens, mix_norm_g, w_in, b_gate, hg_lb_logits, hg_norm_g, attn_sinks, w_branch_hg,
           w_branch_attn, w_out, ffn_norm_g, peer_w_q, peer_subkeys, peer_u, peer_v, final_norm_g):
    import numpy as np
    from concourse import bacc
    from concourse.bass_utils import run_bass_kernel_spmd

    a = np.asarray

    def columns(t):
        return a(t).reshape(-1, P).T

    def blocks(t):
        t = a(t)
        return t.reshape(DC, P, t.shape[1] // P, P).transpose(2, 1, 0, 3).reshape(-1, P, D)

    tokens = a(x)[0]
    both = np.concatenate([a(meta_tokens), tokens], axis=0)
    w = a(w_in)[0]
    width = HH * P
    f, q, v_, og = w[:, width:2 * width], w[:, 0:width], w[:, 2 * width:3 * width], w[:, 3 * width:4 * width]
    at0 = 4 * width
    aq, ak, av = w[:, at0:at0 + AQ * HD], w[:, at0 + 512:at0 + 640], w[:, at0 + 640:at0 + 768]
    aq = aq.reshape(D, 2, 4, HD).transpose(0, 2, 1, 3).reshape(D, AQ * HD)
    wb_at = a(w_branch_attn)[0].reshape(2, 4, HD, D).transpose(1, 0, 2, 3).reshape(AQ * HD, D)
    gates = w[:, at0 + 768:]
    branch = np.concatenate([a(w_branch_hg)[0], wb_at], axis=0)
    keys = a(peer_subkeys)[0].reshape(RS, NK, P).transpose(2, 0, 1).reshape(P, 2, RH * NK).transpose(1, 0, 2)
    wstream = np.concatenate([blocks(f), blocks(q), blocks(v_), blocks(ak), blocks(av), blocks(og), blocks(aq),
                              blocks(gates), blocks(branch), a(w_out)[0].reshape(DC, P, D), keys,
                              blocks(a(peer_w_q)[0])], axis=0)
    assert wstream.shape == (N_TILES, P, D)
    params = np.concatenate([columns(mix_norm_g), columns(hg_norm_g),
                             columns(hg_lb_logits), columns(b_gate)], axis=1)
    arrays = {
        "xT": both.T.reshape(DC, P, LEN).transpose(1, 0, 2),
        "x": tokens,
        "params": params,
        "sinks": a(attn_sinks),
        "ffn_g": a(ffn_norm_g),
        "final_g": a(final_norm_g)[None],
        "wstream": wstream,
        "uT": a(peer_u)[0].reshape(NK, NK, DC, P).transpose(0, 3, 2, 1).reshape(NK, P, D),
        "v": a(peer_v)[0].reshape(NK, NK, D),
    }
    nc = bacc.Bacc("TRN2", target_bir_lowering=False, num_devices=1)
    arrays = {f"in_{k}": np.ascontiguousarray(t) for k, t in arrays.items()}
    ins = [nc.dram_tensor(k, t.shape, F32, kind="ExternalInput").ap() for k, t in arrays.items()]
    gates_dram = nc.dram_tensor("gates_dram", [NGRP, NPIECE, P, GRP * GT], F32, kind="Internal").ap()
    out = nc.dram_tensor("out", (TOK, D), F32, kind="ExternalOutput").ap()
    early_dram = nc.dram_tensor("early_dram", [SPILLED, P, GRP * TOK], F32, kind="Internal").ap()
    build(nc, *ins, gates_dram, early_dram, out)
    r = run_bass_kernel_spmd(nc, [arrays], core_ids=[0])
    return r.results[0]["out"].reshape(1, TOK, D)
```
